# Optimizing a Trainium2 kernel written in Bass

```python
import math
import jax, jax.numpy as jnp
from jax import lax
import numpy as np

D_MODEL = 1024
BATCH = 1
SEQ = 1024
DEPTH = 1
DEC_BATCH = 1
DEC_SEQ = 1024
PAST_LEN = 128

GRID_W = 64
D_ATTN = D_MODEL // 2
HEAD_DIM = 64
N_Q_HEADS = D_ATTN // HEAD_DIM
N_KV_HEADS = 2
Q_PER_KV = N_Q_HEADS // N_KV_HEADS
KV_WIDTH = N_KV_HEADS * HEAD_DIM
Q_BLOCK = 128
ROPE_THETA = 10000.0
ROPE_SECTION = HEAD_DIM // 2
QK_EPS = 1e-6
D_LRU = D_MODEL - D_ATTN
N_LRU_HEADS = 8
LRU_HEAD_DIM = D_LRU // N_LRU_HEADS
CONV_WIDTH = 4
CONV_LEFT = CONV_WIDTH // 2
LRU_C = 8.0
D_MIX = D_ATTN + D_LRU
D_IN_PROJ = D_ATTN + 2 * KV_WIDTH + 2 * D_LRU
N_GROUPS = 4
EXPERTS_PER_GROUP = 4
N_EXPERTS = N_GROUPS * EXPERTS_PER_GROUP
TOP_K = 2
D_EXPERT = 256
LN_EPS = 1e-5
DEEPNORM_ALPHA = (2.0 * DEPTH) ** 0.25
DEEPNORM_BETA = (8.0 * DEPTH) ** -0.25

kernel_name = 'hymba_rglru_axial_gqa_hmoe_encoder'

def layer_norm(x, g, b):
    xf = x.astype(jnp.float32)
    mu = jnp.mean(xf, axis=-1, keepdims=True)
    xc = xf - mu
    var = jnp.mean(jnp.square(xc), axis=-1, keepdims=True)
    return (xc * lax.rsqrt(var + LN_EPS) * g + b).astype(x.dtype)

def rms_norm(x, g, eps):
    xf = x.astype(jnp.float32)
    return xf * lax.rsqrt(jnp.mean(jnp.square(xf), axis=-1, keepdims=True) + eps) * g

def axial_rope_tables(S):
    rows = S // GRID_W
    row = jnp.repeat(jnp.arange(rows, dtype=jnp.float32), GRID_W)
    col = jnp.tile(jnp.arange(GRID_W, dtype=jnp.float32), rows)
    half = ROPE_SECTION // 2
    inv_freq = ROPE_THETA ** (-jnp.arange(half, dtype=jnp.float32) / half)
    ang_r = row[:, None] * inv_freq
    ang_c = col[:, None] * inv_freq
    return jnp.cos(ang_r), jnp.sin(ang_r), jnp.cos(ang_c), jnp.sin(ang_c)

def rotate_section(x, cos, sin):
    x1, x2 = jnp.split(x, 2, axis=-1)
    c = cos[None, :, None, :]
    s = sin[None, :, None, :]
    return jnp.concatenate([x1 * c - x2 * s, x1 * s + x2 * c], axis=-1)

def apply_axial_rope(x, cos_r, sin_r, cos_c, sin_c):
    x_row, x_col = jnp.split(x, 2, axis=-1)
    return jnp.concatenate([rotate_section(x_row, cos_r, sin_r),
                            rotate_section(x_col, cos_c, sin_c)], axis=-1)

def bidir_block_attention(q, k, v):
    B, S = q.shape[0], q.shape[1]
    n_blk = S // Q_BLOCK
    qb = q.reshape(B, n_blk, Q_BLOCK, N_KV_HEADS, Q_PER_KV, HEAD_DIM).transpose(1, 0, 3, 4, 2, 5)
    kt = k.transpose(0, 2, 1, 3)
    vt = v.transpose(0, 2, 1, 3)
    scale = HEAD_DIM ** -0.5

    def one_block(q_blk):
        s = jnp.einsum('bkgqd,bksd->bkgqs', q_blk, kt, preferred_element_type=jnp.float32) * scale
        p = jax.nn.softmax(s, axis=-1)
        return jnp.einsum('bkgqs,bksd->bkgqd', p.astype(vt.dtype), vt)

    o = lax.map(one_block, qb)
    return o.transpose(1, 0, 4, 2, 3, 5).reshape(B, S, N_Q_HEADS * HEAD_DIM)

def centred_depthwise_conv(x, w, b):
    S = x.shape[1]
    xp = jnp.pad(x, ((0, 0), (CONV_LEFT, CONV_WIDTH - 1 - CONV_LEFT), (0, 0)))
    out = b
    for tap in range(CONV_WIDTH):
        out = out + xp[:, tap:tap + S, :] * w[tap]
    return out

def rg_lru_scan(xc, wa, ba, wx, bx, lam, reverse):
    B, S, _ = xc.shape
    xf = xc.astype(jnp.float32)
    xh = xf.reshape(B, S, N_LRU_HEADS, LRU_HEAD_DIM)
    r = jax.nn.sigmoid(jnp.einsum('bshi,hij->bshj', xh, wa) + ba).reshape(B, S, D_LRU)
    i = jax.nn.sigmoid(jnp.einsum('bshi,hij->bshj', xh, wx) + bx).reshape(B, S, D_LRU)
    log_a = -LRU_C * r * jax.nn.softplus(-lam.astype(jnp.float32))
    a = jnp.exp(log_a)
    u = jnp.sqrt(-jnp.expm1(2.0 * log_a)) * (i * xf)
    if reverse:
        a = jnp.flip(a, axis=1)
        u = jnp.flip(u, axis=1)

    def combine(left, right):
        a_l, u_l = left
        a_r, u_r = right
        return a_l * a_r, a_r * u_l + u_r

    _, h = lax.associative_scan(combine, (a, u), axis=1)
    if reverse:
        h = jnp.flip(h, axis=1)
    return h

def mixer(h, w_in, conv_w, conv_b, lru_wa, lru_ba, lru_wx, lru_bx, lru_lambda,
          q_norm_g, k_norm_g, attn_out_g, lru_out_g, w_out):
    B, S, _ = h.shape
    proj = h @ w_in
    cuts = [D_ATTN, D_ATTN + KV_WIDTH, D_ATTN + 2 * KV_WIDTH, D_ATTN + 2 * KV_WIDTH + D_LRU]
    q, k, v, x_lru, y_lru = jnp.split(proj, cuts, axis=-1)
    cos_r, sin_r, cos_c, sin_c = axial_rope_tables(S)
    q = rms_norm(q.reshape(B, S, N_Q_HEADS, HEAD_DIM), q_norm_g, QK_EPS)
    k = rms_norm(k.reshape(B, S, N_KV_HEADS, HEAD_DIM), k_norm_g, QK_EPS)
    q = apply_axial_rope(q, cos_r, sin_r, cos_c, sin_c).astype(h.dtype)
    k = apply_axial_rope(k, cos_r, sin_r, cos_c, sin_c).astype(h.dtype)
    v = v.reshape(B, S, N_KV_HEADS, HEAD_DIM)
    attn = bidir_block_attention(q, k, v)
    xc = centred_depthwise_conv(x_lru, conv_w, conv_b)
    h_fwd = rg_lru_scan(xc, lru_wa[0], lru_ba[0], lru_wx[0], lru_bx[0], lru_lambda[0], False)
    h_bwd = rg_lru_scan(xc, lru_wa[1], lru_ba[1], lru_wx[1], lru_bx[1], lru_lambda[1], True)
    lru = (h_fwd + h_bwd) * jax.nn.gelu(y_lru.astype(jnp.float32))
    merged = jnp.concatenate([rms_norm(attn, attn_out_g, LN_EPS),
                              rms_norm(lru, lru_out_g, LN_EPS)], axis=-1).astype(h.dtype)
    return merged @ w_out

def hier_moe(h, router_wg, router_bg, router_we, router_be, exp_w1, exp_w3, exp_w2):
    B, S, D = h.shape
    xt = h.reshape(B * S, D)
    g_logits = (xt @ router_wg).astype(jnp.float32) + router_bg
    g_prob = jax.nn.softmax(g_logits, axis=-1)
    g_onehot = jax.nn.one_hot(jnp.argmax(g_logits, axis=-1), N_GROUPS, dtype=jnp.float32)
    g_sel_prob = jnp.sum(g_prob * g_onehot, axis=-1)
    e_logits = jnp.einsum('td,dge->tge', xt, router_we).astype(jnp.float32) + router_be
    e_logits_sel = jnp.einsum('tge,tg->te', e_logits, g_onehot)
    top_v, top_i = lax.top_k(e_logits_sel, TOP_K)
    top_w = jax.nn.softmax(top_v, axis=-1) * g_sel_prob[:, None]
    g_idx = jnp.argmax(g_onehot, axis=-1)
    expert_id = g_idx[:, None] * EXPERTS_PER_GROUP + top_i
    gate = jnp.sum(jax.nn.one_hot(expert_id, N_EXPERTS, dtype=jnp.float32) * top_w[..., None], axis=1)
    y = jnp.zeros((B * S, D), jnp.float32)
    for e in range(N_EXPERTS):
        hid = jax.nn.silu(xt @ exp_w1[e]) * (xt @ exp_w3[e])
        y = y + gate[:, e:e + 1] * (hid @ exp_w2[e]).astype(jnp.float32)
    return y.reshape(B, S, D).astype(h.dtype)

def trunk(x, ln_in_g, ln_in_b, w_in, conv_w, conv_b, lru_wa, lru_ba, lru_wx, lru_bx,
          lru_lambda, q_norm_g, k_norm_g, attn_out_g, lru_out_g, w_out, ln1_g, ln1_b,
          router_wg, router_bg, router_we, router_be, exp_w1, exp_w3, exp_w2, ln2_g, ln2_b):
    h = layer_norm(x, ln_in_g, ln_in_b)
    for l in range(DEPTH):
        mix = mixer(h, w_in[l], conv_w[l], conv_b[l], lru_wa[l], lru_ba[l], lru_wx[l], lru_bx[l],
                    lru_lambda[l], q_norm_g[l], k_norm_g[l], attn_out_g[l], lru_out_g[l], w_out[l])
        h = layer_norm(DEEPNORM_ALPHA * h + mix, ln1_g[l], ln1_b[l])
        ffn = hier_moe(h, router_wg[l], router_bg[l], router_we[l], router_be[l],
                       exp_w1[l], exp_w3[l], exp_w2[l])
        h = layer_norm(DEEPNORM_ALPHA * h + ffn, ln2_g[l], ln2_b[l])
    return h

def setup_inputs(seed: int = 0) -> dict:
    key = jax.random.key(seed)
    ks = jax.random.split(key, 32)
    f32 = jnp.float32
    nrm = lambda k, shape: jax.random.normal(k, shape, f32)
    u = jax.random.uniform(ks[11], (DEPTH, 2, D_LRU), f32, minval=0.9, maxval=0.999)
    a0 = u ** (1.0 / LRU_C)
    lam = jnp.log(a0) - jnp.log1p(-a0)
    return {
        'x_prompt': nrm(ks[0], (BATCH, SEQ, D_MODEL)),
        'x_sample': nrm(ks[1], (DEC_BATCH, DEC_SEQ, D_MODEL)),
        'ln_in_g': 1.0 + 0.05 * nrm(ks[2], (D_MODEL,)),
        'ln_in_b': 0.02 * nrm(ks[3], (D_MODEL,)),
        'w_in': nrm(ks[4], (DEPTH, D_MODEL, D_IN_PROJ)) * D_MODEL ** -0.5,
        'conv_w': nrm(ks[5], (DEPTH, CONV_WIDTH, D_LRU)) * CONV_WIDTH ** -0.5,
        'conv_b': 0.02 * nrm(ks[6], (DEPTH, D_LRU)),
        'lru_wa': nrm(ks[7], (DEPTH, 2, N_LRU_HEADS, LRU_HEAD_DIM, LRU_HEAD_DIM)) * LRU_HEAD_DIM ** -0.5,
        'lru_ba': 0.02 * nrm(ks[8], (DEPTH, 2, N_LRU_HEADS, LRU_HEAD_DIM)),
        'lru_wx': nrm(ks[9], (DEPTH, 2, N_LRU_HEADS, LRU_HEAD_DIM, LRU_HEAD_DIM)) * LRU_HEAD_DIM ** -0.5,
        'lru_bx': 0.02 * nrm(ks[10], (DEPTH, 2, N_LRU_HEADS, LRU_HEAD_DIM)),
        'lru_lambda': lam,
        'q_norm_g': 1.0 + 0.05 * nrm(ks[12], (DEPTH, HEAD_DIM)),
        'k_norm_g': 1.0 + 0.05 * nrm(ks[13], (DEPTH, HEAD_DIM)),
        'attn_out_g': 1.0 + 0.05 * nrm(ks[14], (DEPTH, D_ATTN)),
        'lru_out_g': 1.0 + 0.05 * nrm(ks[15], (DEPTH, D_LRU)),
        'w_out': nrm(ks[16], (DEPTH, D_MIX, D_MODEL)) * D_MIX ** -0.5 * DEEPNORM_BETA,
        'ln1_g': 1.0 + 0.05 * nrm(ks[17], (DEPTH, D_MODEL)),
        'ln1_b': 0.02 * nrm(ks[18], (DEPTH, D_MODEL)),
        'router_wg': nrm(ks[19], (DEPTH, D_MODEL, N_GROUPS)) * D_MODEL ** -0.5,
        'router_bg': 0.01 * nrm(ks[20], (DEPTH, N_GROUPS)),
        'router_we': nrm(ks[21], (DEPTH, D_MODEL, N_GROUPS, EXPERTS_PER_GROUP)) * D_MODEL ** -0.5,
        'router_be': 0.01 * nrm(ks[22], (DEPTH, N_GROUPS, EXPERTS_PER_GROUP)),
        'exp_w1': nrm(ks[23], (DEPTH, N_EXPERTS, D_MODEL, D_EXPERT)) * D_MODEL ** -0.5,
        'exp_w3': nrm(ks[24], (DEPTH, N_EXPERTS, D_MODEL, D_EXPERT)) * D_MODEL ** -0.5,
        'exp_w2': nrm(ks[25], (DEPTH, N_EXPERTS, D_EXPERT, D_MODEL)) * D_EXPERT ** -0.5 * DEEPNORM_BETA,
        'ln2_g': 1.0 + 0.05 * nrm(ks[26], (DEPTH, D_MODEL)),
        'ln2_b': 0.02 * nrm(ks[27], (DEPTH, D_MODEL)),
    }

def reference(x_prompt, x_sample, ln_in_g, ln_in_b, w_in, conv_w, conv_b, lru_wa, lru_ba,
              lru_wx, lru_bx, lru_lambda, q_norm_g, k_norm_g, attn_out_g, lru_out_g, w_out,
              ln1_g, ln1_b, router_wg, router_bg, router_we, router_be, exp_w1, exp_w3,
              exp_w2, ln2_g, ln2_b):
    weights = (ln_in_g, ln_in_b, w_in, conv_w, conv_b, lru_wa, lru_ba, lru_wx, lru_bx,
               lru_lambda, q_norm_g, k_norm_g, attn_out_g, lru_out_g, w_out, ln1_g, ln1_b,
               router_wg, router_bg, router_we, router_be, exp_w1, exp_w3, exp_w2, ln2_g, ln2_b)
    y_prompt = trunk(x_prompt, *weights)
    y_sample = trunk(x_sample, *weights)
    return (y_prompt, y_sample)


_drawn_inputs = setup_inputs


def setup_inputs(seed=0):
    import zlib

    import numpy as np

    out = dict(_drawn_inputs(seed))
    spreads = {}
    factors = {'lru_ba': 8.0,
     'lru_bx': 8.0,
     'q_norm_g': 3.096,
     'k_norm_g': 2.745,
     'attn_out_g': 2.719,
     'lru_out_g': 2.737,
     'router_bg': 23.148,
     'router_be': 19.052,
     'ln2_b': 3.121}
    for name, (base, spread) in spreads.items():
        noise = np.random.default_rng([zlib.crc32(name.encode()), seed]).standard_normal(out[name].shape)
        drawn = base * np.exp(spread * noise) if base else spread * noise
        out[name] = __import__('jax').numpy.asarray(drawn.astype(out[name].dtype))
    for name, factor in factors.items():
        out[name] = (out[name] * factor).astype(out[name].dtype)
    return out
```

```python
from contextlib import ExitStack, contextmanager

import concourse.bass as bass
from concourse import mybir

F32 = mybir.dt.float32
F32R = mybir.dt.float32r
I32 = mybir.dt.int32
U32 = mybir.dt.uint32
ALU = mybir.AluOpType
ACT = mybir.ActivationFunctionType
AX = mybir.AxisListType.X

P = 128
D = 1024
KD = D // P
SEQS = 2
SEQ = 1024
T = SEQS * SEQ
NT = T // P
TPS = SEQ // P
CH = 256
NC = T // CH
CPS = SEQ // CH
HD = 64
NQ = 8
NKV = 2
NH = NQ + NKV
QW = NQ * HD
KVW = NKV * HD
QKVW = QW + 2 * KVW
QKW = QW + KVW
LW = 512
FT = LW // P
LHD = 64
TAPS = 4
G = 4
E_IN_G = 4
NE = G * E_IN_G
DE = 256
KE = DE // P
RW = G + NE
MT = 2 * NT + NE
SLOTS = MT * P
LN_EPS = 1e-5
QK_EPS = 1e-6
LRU_C = 8.0
ALPHA = 2.0 ** 0.25
SCALE = HD ** -0.5
NEWTON = 3


class Chain:

    def __init__(self, eng, sem, done=0):
        self.eng, self.sem, self.done, self.n = eng, sem, done, 0

    def __call__(self, ins):
        self.n += 1
        ins.then_inc(self.sem, 1)
        self.eng.wait_ge(self.sem, self.done + self.n)


def rsqrt(dve, link, x, y, t):
    link(dve.tensor_scalar(t.bitcast(I32), x.bitcast(I32), 1, None, ALU.logical_shift_right))
    link(dve.tensor_scalar(y.bitcast(I32), t.bitcast(I32), -1.0, float(0x5F3759DF), ALU.mult, ALU.add))
    for _ in range(NEWTON):
        link(dve.tensor_tensor(t, y, x, ALU.mult))
        link(dve.tensor_tensor(t, t, y, ALU.mult))
        link(dve.tensor_scalar(t, t, -0.5, 1.5, ALU.mult, ALU.add))
        link(dve.tensor_tensor(y, y, t, ALU.mult))


RSQRT_LINKS = 2 + 4 * NEWTON


def three_pass(pe, out, lhs, rhs, first, last):
    pe.matmul(out, lhs[0], rhs[0], start=first, stop=False)
    pe.matmul(out, lhs[0], rhs[1], start=False, stop=False)
    return pe.matmul(out, lhs[1], rhs[0], start=False, stop=last)


def build(nc, x, ln_in_g, ln_in_b, w_in, conv_w, conv_b, lru_wa, lru_ba, lru_wx, lru_bx, lru_lambda,
          q_norm_g, k_norm_g, attn_out_g, lru_out_g, w_out, ln1_g, ln1_b, router_wg, router_bg,
          router_we, router_be, exp_w1, exp_w3, exp_w2, ln2_g, ln2_b, rope, out):
    h_dram = nc.dram_tensor("h_dram", (T, D), F32, kind="Internal").ap()
    ht_hi_dram = nc.dram_tensor("ht_hi_dram", (NC, P, KD * CH), F32, kind="Internal").ap()
    ht_lo_dram = nc.dram_tensor("ht_lo_dram", (NC, P, KD * CH), F32, kind="Internal").ap()
    q_dram = nc.dram_tensor("q_dram", (NT, P, NQ * P), F32, kind="Internal").ap()
    h1_dram = nc.dram_tensor("h1_dram", (T, D), F32, kind="Internal").ap()
    list_dram = nc.dram_tensor("list_dram", (SLOTS, 1), F32, kind="Internal").ap()
    y_dram = nc.dram_tensor("y_dram", (SLOTS, D), F32, kind="Internal").ap()

    with ExitStack() as whole:
        sb = lambda n, s, d=F32: whole.enter_context(nc.sbuf_tensor(n, s, d))
        ident = sb("ident", [P, P])
        identr = sb("identr", [P, P], F32R)
        logits = sb("logits", [P, NT, RW])
        with ExitStack() as kept:
            sb = lambda n, s, d=F32: kept.enter_context(nc.sbuf_tensor(n, s, d))
            k_hi = sb("k_hi", [P, NKV, T], F32R)
            k_lo = sb("k_lo", [P, NKV, T], F32R)
            v_all = sb("v_all", [P, NT, KVW])
            y_all = sb("y_all", [P, FT, T])
            with nc.sbuf_tensor("x_all", [P, FT, T], F32) as x_all:
                project_lru(nc, x, ln_in_g, ln_in_b, w_in, ident, identr, x_all, y_all, k_hi, k_lo, h_dram,
                            ht_hi_dram, ht_lo_dram)
                project_qkv(nc, w_in, q_norm_g, k_norm_g, rope, identr, ht_hi_dram, ht_lo_dram,
                            k_hi, k_lo, v_all, q_dram)
                lru(nc, conv_w, conv_b, lru_wa, lru_ba, lru_wx, lru_bx, lru_lambda, x_all, y_all)
            attend(nc, w_out, attn_out_g, lru_out_g, ln1_g, ln1_b, router_wg, router_bg, router_we,
                   router_be, ident, k_hi, k_lo, v_all, y_all, h_dram, q_dram, h1_dram, logits)
        sb = lambda n, s, d=F32: whole.enter_context(nc.sbuf_tensor(n, s, d))
        slots = sb("slots", [P, 2, NT], U32)
        weights = sb("weights", [P, 2, NT])
        lists = sb("lists", [P, MT], U32)
        tile_expert = sb("tile_expert", [P, MT], I32)
        tiles_to = sb("tiles_to", [P, NE], I32)
        route(nc, ident, logits, list_dram, slots, weights, lists, tile_expert, tiles_to)
        experts(nc, exp_w1, exp_w3, exp_w2, ident, lists, tile_expert, tiles_to, h1_dram, y_dram)
        combine(nc, ln2_g[0], ln2_b[0], slots, weights, h1_dram, y_dram, out)


@contextmanager
def semaphores(nc, prefix):
    held = []

    def sem(name):
        held.append(nc.alloc_semaphore(prefix + name))
        return held[-1]

    yield sem
    nc.clear_and_free_semaphores(held)
    nc.all_engine_barrier()


def row(ap, n):
    return ap.rearrange("(o n) -> o n", o=1).broadcast_to([P, n])


def run_chunks(eng, ln, transpose, project):
    ln(0, 0)
    transpose(0, 0)
    ln(1, 1)
    with eng.Fori(0, (NC - 2) // 2) as n:
        for u in range(2):
            c = 2 * n + u
            transpose(c + 1, 1 - u)
            project(c, u, 0)
            ln(c + 2, u)
            project(c, u, 1)
    transpose(NC - 1, 1)
    for u in range(2):
        project(NC - 2 + u, u, 0)
        project(NC - 2 + u, u, 1)


def project_lru(nc, x, ln_g, ln_b, w_in, ident, identr, x_all, y_all, k_hi, k_lo, h_dram,
                ht_hi_dram, ht_lo_dram):
    with ExitStack() as ctx:
        sb = lambda n, s, d=F32: ctx.enter_context(nc.sbuf_tensor(n, s, d))
        ps = lambda n, s, d=F32: ctx.enter_context(nc.psum_tensor(n, s, d))
        sem = ctx.enter_context(semaphores(nc, "a_"))
        NF = 2 * FT
        w_hi = sb("wl_hi", [P, KD, NF * P], F32R)
        w_lo = sb("wl_lo", [P, KD, NF * P], F32R)
        raw = x_all[:].rearrange("p f t -> p (f t)").rearrange("p (k n) -> p k n", k=KD)
        g_b = sb("ln_in_g_b", [P, D])
        b_b = sb("ln_in_b_b", [P, D])
        xt = [sb(f"xt{j}", [P, D]) for j in range(2)]
        ht = [sb(f"ht{j}", [P, D]) for j in range(2)]
        t_hi = [k_hi[:, u, :].rearrange("p (k n) -> p k n", k=KD) for u in range(2)]
        t_lo = [k_lo[:, u, :].rearrange("p (k n) -> p k n", k=KD) for u in range(2)]
        stats = sb("stats", [P, 12])
        mv = sb("mv", [P, 2])
        var = sb("var", [P, 1])
        tmp = sb("tmp", [P, 1])
        rstd = [sb(f"rstd{j}", [P, 1]) for j in range(2)]
        shift = [sb(f"shift{j}", [P, 1]) for j in range(2)]
        tps = [ps(f"tps{j}", [P, KD, P]) for j in range(2)]
        acc = [ps(f"acc{j}", [P, 512]) for j in range(4)]

        go = sem("go_a")
        w_in_sem = sem("w_raw_loaded")
        ln_sem = sem("ln_rows_loaded")
        id_sem = sem("ident_made")
        hi_made = sem("w_hi_made")
        lo_made = sem("w_lo_made")
        x_in = [sem(f"x_tile_loaded{j}") for j in range(2)]
        dve_link = sem("dve_link_a")
        stats_done = sem("stats_done")
        xn_done = sem("normalised")
        hg_done = sem("gain_applied")
        h_done = sem("h_done")
        h_stored = [sem(f"h_stored{j}") for j in range(2)]
        tr_done = sem("h_transposed")
        hi_done = sem("t_hi_done")
        lo_done = sem("t_lo_done")
        t_stored = [sem(f"t_stored{c}") for c in range(2)]
        acc_done = sem("acc_done")
        acc_free = sem("acc_free")
        block = ctx.enter_context(nc.Block())

        @block.sync
        def _(sp):
            sp.sem_inc(go, 1)
            w_rows = w_in[0].rearrange("(k p) n -> p k n", p=P)[:, :, QKVW:QKVW + NF * P]
            for j in range(2):
                sp.dma_start(xt[j][:], x[j * P:(j + 1) * P, :]).then_inc(x_in[j], 16)
            sp.dma_start(g_b[:], row(ln_g, D)).then_inc(ln_sem, 16)
            sp.dma_start(b_b[:], row(ln_b, D)).then_inc(ln_sem, 16)
            for k in range(KD):
                sp.dma_start(raw[:, k, :], w_rows[:, k, :]).then_inc(w_in_sem, 16)
            with sp.Fori(0, NC - 1) as c:
                for j in range(2):
                    sp.wait_ge(hg_done, 2 * c + j + 1)
                    sp.dma_start(xt[j][:], x[bass.ds((2 * c + j + 2) * P, P), :]).then_inc(x_in[j], 16)

        @block.gpsimd
        def _(pool):
            pool.memset(ident[:], 0.0).then_inc(id_sem, 1)
            pool.wait_ge(id_sem, 1)
            pool.affine_select(out=ident[:], in_=ident[:], compare_op=ALU.not_equal, fill=1.0, base=0,
                               pattern=[[-1, P]], channel_multiplier=1).then_inc(id_sem, 1)
            pool.wait_ge(ln_sem, 32)
            with pool.Fori(0, NC) as c:
                for j in range(2):
                    pool.wait_ge(hg_done, 2 * c + j + 1)
                    pool.tensor_tensor(ht[j][:], ht[j][:], b_b[:], ALU.add).then_inc(h_done, 1)

        @block.vector
        def _(dve):
            dve.wait_ge(id_sem, 2)
            dve.tensor_copy(identr[:], ident[:]).then_inc(id_sem, 1)
            dve.wait_ge(ln_sem, 32)
            links = 2 * (4 + RSQRT_LINKS)

            def ln(c, u):
                link = Chain(dve, dve_link, c * links)
                for j in range(2):
                    dve.wait_ge(x_in[j], 16 * c + 16)
                    for half in range(2):
                        link(dve.bn_stats(stats[:, 6 * half:6 * half + 6], xt[j][:, 512 * half:512 * half + 512]))
                    dve.nop(nofuse=True)
                    link(dve.bn_aggr(mv[:], stats[:]))
                    link(dve.tensor_scalar(var[:], mv[:, 1:2], LN_EPS, None, ALU.add))
                    rsqrt(dve, link, var[:], rstd[j][:], tmp[:])
                    dve.tensor_scalar(shift[j][:], mv[:, 0:1], rstd[j][:], -1.0, ALU.mult, ALU.mult)\
                       .then_inc(stats_done, 1)
                assert link.n == links
                for j in range(2):
                    dve.wait_ge(xn_done, 2 * c + j + 1)
                    dve.wait_ge(h_stored[j], 16 * c + 16)
                    dve.wait_ge(tr_done, 2 * c + j + 1)
                    dve.tensor_tensor(ht[j][:], xt[j][:], g_b[:], ALU.mult).then_inc(hg_done, 1)

            def transpose(c, u):
                for j in range(2):
                    dve.wait_ge(hi_done, 2 * c + j + 1)
                    part = slice(j * P, (j + 1) * P)
                    dve.tensor_tensor(t_lo[u][:, :, part], tps[j][:], t_hi[u][:, :, part].bitcast(F32),
                                      ALU.subtract).then_inc(lo_done, 1)

            def project(c, u, half):
                pass

            for k in range(KD):
                dve.wait_ge(hi_made, k + 1)
                dve.tensor_tensor(w_lo[:, k, :], raw[:, k, :], w_hi[:, k, :].bitcast(F32), ALU.subtract)\
                   .then_inc(lo_made, 1)
            run_chunks(dve, ln, transpose, project)

        @block.scalar
        def _(act):
            for j in range(2):
                act.sem_inc(h_stored[j], 16)
                act.sem_inc(t_stored[j], 32)
            for k in range(KD):
                act.wait_ge(w_in_sem, 16 * KD)
                act.activation(w_hi[:, k, :], raw[:, k, :], ACT.Copy).then_inc(hi_made, 1)

            def ln(c, u):
                for j in range(2):
                    act.wait_ge(stats_done, 2 * c + j + 1)
                    act.activation(xt[j][:], xt[j][:], ACT.Identity, bias=shift[j][:], scale=rstd[j][:])\
                       .then_inc(xn_done, 1)

            def transpose(c, u):
                for j in range(2):
                    act.wait_ge(tr_done, 2 * c + j + 3)
                    if j == 0:
                        act.wait_ge(acc_done, NF * c + NF)
                        act.wait_ge(t_stored[u], 32 + 16 * (c - u))
                    act.activation(t_hi[u][:, :, j * P:(j + 1) * P], tps[j][:], ACT.Copy).then_inc(hi_done, 1)
                    act.wait_ge(h_done, 2 * c + j + 1)
                    act.dma_start(h_dram[bass.ds((2 * c + j) * P, P), :], ht[j][:]).then_inc(h_stored[j], 16)
                act.wait_ge(hi_done, 2 * c + 2)
                act.dma_start(ht_hi_dram[bass.ds(c, 1)].rearrange("o p n -> (o p) n"),
                              k_hi[:, u, :].bitcast(F32)).then_inc(t_stored[u], 16)
                act.wait_ge(lo_done, 2 * c + 4)
                act.dma_start(ht_lo_dram[bass.ds(c, 1)].rearrange("o p n -> (o p) n"),
                              k_lo[:, u, :].bitcast(F32)).then_inc(t_stored[u], 16)

            def project(c, u, half):
                for f in range(half * FT, (half + 1) * FT):
                    act.wait_ge(acc_done, 2 * NF + NF * c + f + 1)
                    act.wait_ge(go, 1)
                    dst = x_all if f < FT else y_all
                    act.activation(dst[:, f % FT, bass.ds(c * CH, CH)], acc[f % 4][:, 0:CH], ACT.Copy)\
                       .then_inc(acc_free, 1)

            act.wait_ge(lo_made, KD)
            run_chunks(act, ln, transpose, project)
            for c in range(2):
                act.wait_ge(t_stored[c], 32 + 32 * (NC // 2))
            for j in range(2):
                act.wait_ge(h_stored[j], 16 + 16 * NC)

        @block.tensor
        def _(pe):
            pe.sem_inc(tr_done, 2)
            pe.sem_inc(lo_done, 2)
            pe.sem_inc(acc_done, 2 * NF)
            pe.sem_inc(acc_free, 4)
            pe.wait_ge(id_sem, 3)

            def ln(c, u):
                pass

            def transpose(c, u):
                for j in range(2):
                    pe.wait_ge(h_done, 2 * c + j + 1)
                    pe.wait_ge(lo_done, 2 * c + j + 1)
                    for k in range(KD):
                        last = pe.transpose(tps[j][:, k, :], ht[j][:, k * P:(k + 1) * P], ident[:])
                    last.then_inc(tr_done, 1)

            def project(c, u, half):
                if half == 0:
                    pe.wait_ge(lo_done, 2 * c + 4)
                for f in range(half * FT, (half + 1) * FT):
                    pe.wait_ge(acc_free, NF * c + f + 1)
                    cols = slice(f * P, (f + 1) * P)
                    for k in range(KD):
                        last = three_pass(pe, acc[f % 4][:, 0:CH], (w_hi[:, k, cols], w_lo[:, k, cols]),
                                          (t_hi[u][:, k, :], t_lo[u][:, k, :]), k == 0, k == KD - 1)
                    last.then_inc(acc_done, 1)

            pe.wait_ge(lo_made, KD)
            run_chunks(pe, ln, transpose, project)



def project_qkv(nc, w_in, q_g, k_g, rope, identr, ht_hi_dram, ht_lo_dram, k_hi, k_lo, v_all, q_dram):
    with ExitStack() as ctx:
        sb = lambda n, s, d=F32: ctx.enter_context(nc.sbuf_tensor(n, s, d))
        ps = lambda n, s, d=F32: ctx.enter_context(nc.psum_tensor(n, s, d))
        sem = ctx.enter_context(semaphores(nc, "b_"))
        w_hi = sb("wq_hi", [P, KD, QKVW], F32R)
        w_lo = sb("wq_lo", [P, KD, QKVW], F32R)
        raw = [sb(f"wq_raw{j}", [P, QKVW]) for j in range(2)]
        g_b = sb("qk_g_b", [P, 2, HD])
        tab = sb("rope_tab", [P, TPS, 2, HD])
        c_hi = [sb(f"c_hi{u}", [P, KD, P], F32R) for u in range(2)]
        c_lo = [sb(f"c_lo{u}", [P, KD, P], F32R) for u in range(2)]
        sq = raw[0][:, 0:QKW]
        rb = raw[1][:, 0:QKW]
        ss = sb("ss", [P, NH])
        ms = sb("ms", [P, NH])
        tmp = sb("tmp_qk", [P, NH])
        rs = sb("rs", [P, NH])
        xr = [sb(f"xr{u}", [P, QKW]) for u in range(2)]
        rt = [sb(f"rt{u}", [P, QKW]) for u in range(2)]
        q_st = [sb(f"q_st{u}", [P, NQ, 2, HD], F32R) for u in range(2)]
        k_st = [sb(f"k_st{u}", [P, 2, NKV, 2, HD], F32R) for u in range(2)]
        q_t = sb("q_t", [P, NQ, P], F32R)
        pj = [ps(f"pj{u}", [P, 1024]) for u in range(2)]
        tr = ps("tr", [P, NQ + 2 * NKV, P], F32R)

        go = sem("go_b")
        w_raw = [sem(f"wq_raw_loaded{j}") for j in range(2)]
        rows_in = sem("qk_rows_loaded")
        hi_made = sem("wq_hi_made")
        lo_made = sem("wq_lo_made")
        c_in = [sem(f"chunk_loaded{u}") for u in range(2)]
        dve_link = sem("dve_link_b")
        pj_done = sem("pj_done")
        sq_done = sem("sq_done")
        ss_done = sem("ss_done")
        v_done = sem("v_done")
        xr_done = sem("xr_done")
        xg_done = sem("xg_done")
        a_done = sem("rope_a_done")
        b_done = sem("rope_b_done")
        rt_done = sem("rope_done")
        hi_done = sem("qk_hi_done")
        lo_done = sem("qk_lo_done")
        tr_done = sem("qk_transposed")
        qt_done = sem("q_t_done")
        kt_done = sem("k_t_done")
        q_stored = sem("q_stored")
        block = ctx.enter_context(nc.Block())

        def run_tiles(eng, front, back):
            front(0, 0)
            with eng.Fori(0, NT // 2 - 1) as n:
                for u in range(2):
                    front(2 * n + u + 1, 1 - u)
                    back(2 * n + u, u)
            front(NT - 1, 1)
            back(NT - 2, 0)
            back(NT - 1, 1)

        @block.sync
        def _(sp):
            sp.sem_inc(go, 1)
            w_rows = w_in[0].rearrange("(k p) n -> p k n", p=P)

            def load(n, u):
                for dst, src in ((c_hi, ht_hi_dram), (c_lo, ht_lo_dram)):
                    part = src[bass.ds(n, 1)].rearrange("o p (k t) -> (o p) k t", k=KD)[:, :, u * P:(u + 1) * P]
                    sp.dma_start(dst[u][:].bitcast(F32), part).then_inc(c_in[u], 16)

            for k in range(KD):
                if k >= 2:
                    sp.wait_ge(lo_made, k - 1)
                sp.dma_start(raw[k % 2][:], w_rows[:, k, 0:QKVW]).then_inc(w_raw[k % 2], 16)
                if k == 1:
                    load(0, 0)
                    load(0, 1)
            sp.dma_start(g_b[:, 0, :], row(q_g[0], HD)).then_inc(rows_in, 16)
            sp.dma_start(g_b[:, 1, :], row(k_g[0], HD)).then_inc(rows_in, 16)
            sp.dma_start(tab[:].rearrange("p t c d -> p (t c d)"), rope).then_inc(rows_in, 16)
            with sp.Fori(1, NT // 2) as n:
                for u in range(2):
                    sp.wait_ge(pj_done, 2 * n + u - 1)
                    load(n, u)

        @block.scalar
        def _(act):
            act.sem_inc(q_stored, 16)
            act.sem_inc(v_done, 2)
            act.sem_inc(qt_done, 1)
            for k in range(KD):
                act.wait_ge(w_raw[k % 2], 16 * (k // 2 + 1))
                act.activation(w_hi[:, k, :], raw[k % 2][:], ACT.Copy).then_inc(hi_made, 1)
            act.wait_ge(lo_made, KD)

            def front(t, u):
                act.wait_ge(pj_done, t + 1)
                act.wait_ge(ss_done, t + 1)
                act.activation(sq, pj[u][:, 0:QKW], ACT.Square).then_inc(sq_done, 1)
                act.activation(v_all[:, bass.ds(t, 1), :].rearrange("p o n -> p (o n)"), pj[u][:, QKW:QKVW],
                               ACT.Copy).then_inc(v_done, 1)
                act.wait_ge(rt_done, t + 2)
                act.wait_ge(tr_done, t + 1)
                rows = rt[u][:].rearrange("p (h d) -> p h d", h=NH)
                act.activation(q_st[u][:, :, 0, :], rows[:, 0:NQ, :], ACT.Copy)
                act.activation(k_st[u][:, 0], rows[:, NQ:NH, :].unsqueeze(2).broadcast_to([P, NKV, 2, HD]), ACT.Copy)\
                   .then_inc(hi_done, 1)

            def back(t, u):
                act.wait_ge(tr_done, t + 3)
                act.wait_ge(q_stored, 16 * t + 16)
                act.activation(q_t[:], tr[:, 0:NQ, :].bitcast(F32), ACT.Copy).then_inc(qt_done, 1)
                act.wait_ge(qt_done, t + 2)
                act.dma_start(q_dram[bass.ds(t, 1)].rearrange("o p n -> (o p) n"),
                              q_t[:].rearrange("p h t -> p (h t)").bitcast(F32)).then_inc(q_stored, 16)

            run_tiles(act, front, back)
            act.wait_ge(q_stored, 16 + 16 * NT)

        @block.vector
        def _(dve):
            dve.sem_inc(ss_done, 1)
            dve.sem_inc(xr_done, 2)
            dve.sem_inc(rt_done, 1)
            dve.sem_inc(kt_done, 1)
            for k in range(KD):
                dve.wait_ge(hi_made, k + 1)
                dve.tensor_tensor(w_lo[:, k, :], raw[k % 2][:], w_hi[:, k, :].bitcast(F32), ALU.subtract)\
                   .then_inc(lo_made, 1)
            dve.wait_ge(rows_in, 48)
            links = 1 + RSQRT_LINKS

            def front(t, u):
                link = Chain(dve, dve_link, t * links)
                dve.wait_ge(sq_done, t + 1)
                dve.tensor_reduce(ss[:], sq.rearrange("p (h d) -> p h d", h=NH), AX, ALU.add).then_inc(ss_done, 1)
                dve.wait_ge(ss_done, t + 2)
                link(dve.tensor_scalar(ms[:], ss[:], 1.0 / HD, QK_EPS, ALU.mult, ALU.add))
                rsqrt(dve, link, ms[:], rs[:], tmp[:])
                assert link.n == links
                dve.wait_ge(b_done, t + 1)
                dve.wait_ge(v_done, t + 3)
                dve.tensor_tensor(xr[u][:].rearrange("p (h d) -> p h d", h=NH),
                                  pj[u][:, 0:QKW].rearrange("p (h d) -> p h d", h=NH),
                                  rs[:].unsqueeze(2).broadcast_to([P, NH, HD]), ALU.mult).then_inc(xr_done, 1)
                dve.wait_ge(xg_done, t + 1)
                dve.wait_ge(lo_done, t + 1)
                dve.tensor_tensor(rt[u][:].rearrange("p (h d) -> p h d", h=NH),
                                  xr[u][:].rearrange("p (h d) -> p h d", h=NH),
                                  tab[:, bass.ds(t % TPS, 1), 0, :].broadcast_to([P, NH, HD]), ALU.mult).then_inc(a_done, 1)
                dve.wait_ge(a_done, t + 1)
                dve.wait_ge(b_done, t + 3)
                dve.tensor_tensor(rt[u][:], rt[u][:], rb, ALU.add).then_inc(rt_done, 1)

            def back(t, u):
                dve.wait_ge(tr_done, t + 3)
                dve.wait_ge(go, 1)
                dve.tensor_copy(k_hi[:, :, bass.ds(t * P, P)], tr[:, NQ:NQ + NKV, :].bitcast(F32))
                dve.tensor_copy(k_lo[:, :, bass.ds(t * P, P)], tr[:, NQ + NKV:, :].bitcast(F32)).then_inc(kt_done, 1)

            run_tiles(dve, front, back)

        @block.gpsimd
        def _(pool):
            pool.sem_inc(b_done, 2)
            pool.sem_inc(lo_done, 2)
            pool.wait_ge(lo_made, KD)
            pool.wait_ge(rows_in, 48)

            def front(t, u):
                x5 = xr[u][:].rearrange("p (h s f d) -> p h s f d", h=NH, s=2, f=2)
                b5 = rb.rearrange("p (h s f d) -> p h s f d", h=NH, s=2, f=2)
                s5 = tab[:, bass.ds(t % TPS, 1), 1, :].rearrange("p o (s f d) -> p o s f d", s=2, f=2)
                pool.wait_ge(xr_done, t + 3)
                heads = xr[u][:].rearrange("p (h d) -> p h d", h=NH)
                for c, a, b in ((0, 0, NQ), (1, NQ, NH)):
                    last = pool.tensor_tensor(heads[:, a:b], heads[:, a:b],
                                              g_b[:, c:c + 1, :].broadcast_to([P, b - a, HD]), ALU.mult)
                last.then_inc(xg_done, 1)
                pool.wait_ge(xg_done, t + 1)
                pool.wait_ge(rt_done, t + 1)
                pool.wait_ge(go, 1)
                for f in range(2):
                    last = pool.tensor_tensor(b5[:, :, :, f, :], x5[:, :, :, 1 - f, :],
                                              s5[:, :, :, f, :].broadcast_to([P, NH, 2, HD // 4]), ALU.mult)
                last.then_inc(b_done, 1)
                rows = rt[u][:].rearrange("p (h d) -> p h d", h=NH)
                pool.wait_ge(hi_done, t + 1)
                pool.tensor_tensor(q_st[u][:, :, 1, :], rows[:, 0:NQ, :], q_st[u][:, :, 0, :].bitcast(F32), ALU.subtract)
                pool.tensor_tensor(k_st[u][:, 1], rows[:, NQ:NH, :].unsqueeze(2).broadcast_to([P, NKV, 2, HD]),
                                   k_st[u][:, 0].bitcast(F32), ALU.subtract).then_inc(lo_done, 1)

            def back(t, u):
                pass

            run_tiles(pool, front, back)

        @block.tensor
        def _(pe):
            pe.sem_inc(tr_done, 2)
            pe.wait_ge(lo_made, KD)

            def front(t, u):
                pe.wait_ge(c_in[u], 16 * (t - u) + 32)
                pe.wait_ge(v_done, t + 1)
                pe.wait_ge(xr_done, t + 1)
                for a, b in ((0, QW), (QW, QKVW)):
                    for k in range(KD):
                        last = three_pass(pe, pj[u][:, a:b], (c_hi[u][:, k, :], c_lo[u][:, k, :]),
                                          (w_hi[:, k, a:b], w_lo[:, k, a:b]), k == 0, k == KD - 1)
                last.then_inc(pj_done, 1)

            def back(t, u):
                pe.wait_ge(lo_done, t + 3)
                pe.wait_ge(qt_done, t + 1)
                pe.wait_ge(kt_done, t + 1)
                for h in range(NQ):
                    pe.transpose(tr[:, h, :], q_st[u][:, h].rearrange("p c d -> p (c d)"), identr[:])
                for c in range(2):
                    for h in range(NKV):
                        last = pe.transpose(tr[:, NQ + NKV * c + h, :], k_st[u][:, c, h].rearrange("p c d -> p (c d)"),
                                            identr[:])
                last.then_inc(tr_done, 1)

            run_tiles(pe, front, back)


def lru(nc, conv_w, conv_b, lru_wa, lru_ba, lru_wx, lru_bx, lru_lambda, x_all, y_all):
    with ExitStack() as ctx:
        sb = lambda n, s, d=F32: ctx.enter_context(nc.sbuf_tensor(n, s, d))
        sem = ctx.enter_context(semaphores(nc, "c_"))
        UNITS = [(s, f) for s in range(SEQS) for f in range(FT)]
        NG = 4
        gw = sb("gate_w", [P, FT, NG, P])
        gb = sb("gate_b", [P, NG, FT])
        cw = sb("conv_w_t", [P, TAPS, FT])
        cb = sb("conv_b_t", [P, FT])
        lam = sb("lam_t", [P, 2, FT])
        neg = sb("neg_lam", [P, 2, FT])
        mag = sb("abs_lam", [P, 2, FT])
        e = sb("exp_lam", [P, 2, FT])
        z = sb("z_lam", [P, 2, FT])
        z2 = sb("z2_lam", [P, 2, FT])
        ser = sb("series", [P, 2, FT])
        decay = sb("decay", [P, 2, FT])
        ndecay = sb("ndecay", [P, 2, FT])
        xc = [sb(f"xc{u}", [P, SEQ]) for u in range(2)]
        r = [sb(f"r{u}", [P, 2, SEQ]) for u in range(3)]
        i = [sb(f"i{u}", [P, 2, SEQ]) for u in range(3)]
        th = [sb(f"th{u}", [P, 2, SEQ]) for u in range(3)]
        a2 = sb("a2", [P, 2, SEQ])
        gp = ctx.enter_context(nc.psum_tensor("gp", [P, NG, SEQ], F32))

        gw_zero = sem("gate_w_zeroed")
        rows_in = sem("lru_rows_loaded")
        gw_in = sem("gate_w_loaded")
        dve_link = sem("dve_link_c")
        act_link = sem("act_link_c")
        mag_done = sem("abs_lam_done")
        e_done = sem("exp_lam_done")
        decay_done = sem("decay_done")
        xc_done = sem("conv_done")
        gates_done = sem("gates_done")
        sig_done = sem("sigmoids_done")
        th_done = sem("tanh_done")
        a_done = sem("a_done")
        ix_done = sem("ix_done")
        a2_done = sem("a2_done")
        w_done = sem("one_minus_a2_done")
        root_done = sem("root_done")
        scans_done = sem("scans_done")
        sum_done = sem("sum_done")
        gelu_done = sem("gelu_done")
        out_done = sem("lru_done")
        block = ctx.enter_context(nc.Block())

        @block.sync
        def _(sp):
            with nc.allow_non_contiguous_dma("small per-feature vectors"):
                sp.dma_start(lam[:], lru_lambda[0].rearrange("d (f p) -> p d f", p=P)).then_inc(rows_in, 16)
                for w in range(TAPS):
                    sp.dma_start(cw[:, w], conv_w[0, w].rearrange("(f p) -> p f", p=P)).then_inc(rows_in, 16)
                sp.dma_start(cb[:], conv_b[0].rearrange("(f p) -> p f", p=P)).then_inc(rows_in, 16)
                for n, src in enumerate((lru_ba, lru_bx)):
                    for d in range(2):
                        sp.dma_start(gb[:, 2 * d + n], src[0, d].rearrange("h i -> (h i)").rearrange("(f p) -> p f", p=P))\
                          .then_inc(rows_in, 16)
            sp.wait_ge(gw_zero, 1)
            for n, src in enumerate((lru_wa, lru_wx)):
                for d in range(2):
                    for c in range(2):
                        part = src[0, d].rearrange("(f c) i j -> c i f j", c=2)[c]
                        sp.dma_start(gw[c * LHD:(c + 1) * LHD, :, 2 * d + n, c * LHD:(c + 1) * LHD], part)\
                          .then_inc(gw_in, 16)

        def run_units(conv, front, w, back, out):
            conv(0)
            conv(1)
            front(0)
            for n in range(len(UNITS)):
                w(n)
                if n:
                    out(n - 1)
                if n + 1 < len(UNITS):
                    front(n + 1)
                if n + 2 < len(UNITS):
                    conv(n + 2)
                back(n)
            out(len(UNITS) - 1)

        def skip(n):
            pass

        @block.vector
        def _(dve):
            link = Chain(dve, dve_link)
            dve.wait_ge(rows_in, 160)
            link(dve.tensor_scalar(neg[:], lam[:], -1.0, None, ALU.mult))
            dve.tensor_tensor(mag[:], lam[:], neg[:], ALU.max).then_inc(mag_done, 1)
            dve.wait_ge(e_done, 1)
            link(dve.tensor_scalar(z2[:], e[:], 2.0, None, ALU.add))
            link(dve.reciprocal(z2[:], z2[:]))
            link(dve.tensor_tensor(z[:], e[:], z2[:], ALU.mult))
            link(dve.tensor_tensor(z2[:], z[:], z[:], ALU.mult))
            link(dve.tensor_scalar(ser[:], z2[:], 1 / 19, 1 / 17, ALU.mult, ALU.add))
            for odd in range(15, 0, -2):
                link(dve.tensor_tensor(ser[:], ser[:], z2[:], ALU.mult))
                link(dve.tensor_scalar(ser[:], ser[:], 1 / odd, None, ALU.add))
            link(dve.tensor_tensor(ser[:], ser[:], z[:], ALU.mult))
            link(dve.tensor_scalar(neg[:], neg[:], 0.0, LRU_C, ALU.max, ALU.mult))
            link(dve.scalar_tensor_tensor(decay[:], ser[:], 2.0 * LRU_C, neg[:], ALU.mult, ALU.add))
            dve.tensor_scalar(ndecay[:], decay[:], -1.0, None, ALU.mult).then_inc(decay_done, 1)

            def conv(n):
                s, f = UNITS[n]
                c = xc[n % 2]
                xs = x_all[:, f, s * SEQ:(s + 1) * SEQ]
                if n >= 2:
                    dve.wait_ge(ix_done, n - 1)
                    dve.wait_ge(gates_done, NG * (n - 1))
                link(dve.tensor_scalar(c[:], xs, cw[:, 2, f:f + 1], cb[:, f:f + 1], ALU.mult, ALU.add))
                link(dve.scalar_tensor_tensor(c[:, 2:], xs[:, :SEQ - 2], cw[:, 0, f:f + 1], c[:, 2:],
                                              ALU.mult, ALU.add))
                link(dve.scalar_tensor_tensor(c[:, 1:], xs[:, :SEQ - 1], cw[:, 1, f:f + 1], c[:, 1:],
                                              ALU.mult, ALU.add))
                dve.scalar_tensor_tensor(c[:, :SEQ - 1], xs[:, 1:], cw[:, 3, f:f + 1], c[:, :SEQ - 1],
                                         ALU.mult, ALU.add).then_inc(xc_done, 1)

            def w(n):
                u = n % 3
                dve.wait_ge(a2_done, n + 1)
                dve.wait_ge(th_done, 2 * n + 2)
                dve.scalar_tensor_tensor(th[u][:], a2[:], 1.0, th[u][:], ALU.add, ALU.mult).then_inc(w_done, 1)

            def back(n):
                u = n % 3
                dve.wait_ge(root_done, n + 1)
                dve.wait_ge(ix_done, n + 1)
                link(dve.tensor_tensor(i[u][:], i[u][:], th[u][:], ALU.mult))
                dve.tensor_tensor_scan(i[u][:, 0], r[u][:, 0], i[u][:, 0], 0.0, ALU.mult, ALU.add)
                dve.tensor_tensor_scan(i[u][:, 1, ::-1], r[u][:, 1, ::-1], i[u][:, 1, ::-1], 0.0, ALU.mult, ALU.add)\
                   .then_inc(scans_done, 1)

            def out(n):
                s, f = UNITS[n]
                ys = y_all[:, f, s * SEQ:(s + 1) * SEQ]
                dve.wait_ge(sum_done, n + 1)
                dve.wait_ge(gelu_done, 1)
                dve.tensor_tensor(ys, ys, i[n % 3][:, 0], ALU.mult).then_inc(out_done, 1)

            run_units(conv, skip, w, back, out)

        @block.gpsimd
        def _(pool):
            pool.memset(gw[:], 0.0).then_inc(gw_zero, 1)

            def front(n):
                u = n % 3
                pool.wait_ge(a_done, n + 1)
                if n:
                    pool.wait_ge(w_done, n)
                pool.tensor_tensor(a2[:], r[u][:], r[u][:], ALU.mult).then_inc(a2_done, 1)
                pool.wait_ge(sig_done, NG * n + NG)
                pool.wait_ge(xc_done, n + 1)
                for d in range(2):
                    last = pool.tensor_tensor(i[u][:, d], i[u][:, d], xc[n % 2][:], ALU.mult)
                last.then_inc(ix_done, 1)

            def back(n):
                u = n % 3
                pool.wait_ge(scans_done, n + 1)
                pool.tensor_tensor(i[u][:, 0], i[u][:, 0], i[u][:, 1], ALU.add).then_inc(sum_done, 1)

            run_units(skip, front, skip, back, skip)

        @block.scalar
        def _(act):
            act.wait_ge(mag_done, 1)
            act.activation(e[:], mag[:], ACT.Exp, scale=-1.0).then_inc(e_done, 1)
            act.activation(y_all[:], y_all[:], ACT.Gelu_apprx_tanh).then_inc(gelu_done, 1)
            act.wait_ge(decay_done, 1)

            def front(n):
                s, f = UNITS[n]
                u = n % 3
                if n >= 3:
                    act.wait_ge(out_done, n - 2)
                for g in range(NG):
                    act.wait_ge(gates_done, NG * n + g + 1)
                    dst = (r, i)[g % 2][u][:, g // 2]
                    act.activation(dst, gp[:, g], ACT.Sigmoid, bias=gb[:, g, f:f + 1]).then_inc(sig_done, 1)
                act.wait_ge(sig_done, NG * n + NG)
                for d in range(2):
                    act.activation(th[u][:, d], r[u][:, d], ACT.Tanh, scale=decay[:, d, f:f + 1]).then_inc(th_done, 1)
                act.wait_ge(th_done, 2 * n + 2)
                for d in range(2):
                    last = act.activation(r[u][:, d], r[u][:, d], ACT.Exp, scale=ndecay[:, d, f:f + 1])
                last.then_inc(a_done, 1)

            def back(n):
                act.wait_ge(w_done, n + 1)
                act.activation(th[n % 3][:], th[n % 3][:], ACT.Sqrt).then_inc(root_done, 1)

            run_units(skip, front, skip, back, skip)

        @block.tensor
        def _(pe):
            pe.wait_ge(gw_in, 128)

            def front(n):
                s, f = UNITS[n]
                u = n % 2
                pe.wait_ge(xc_done, n + 1)
                for g in range(NG):
                    if n:
                        pe.wait_ge(sig_done, NG * (n - 1) + g + 1)
                    for c in range(2):
                        last = pe.matmul(gp[:, g, c * 512:(c + 1) * 512], gw[:, f, g, :], xc[u][:, c * 512:(c + 1) * 512],
                                         start=True, stop=True)
                    last.then_inc(gates_done, 1)

            run_units(skip, front, skip, skip, skip)


def need(eng, sem, value):
    if not (isinstance(value, int) and value < 1):
        eng.wait_ge(sem, value)


def attend(nc, w_out, attn_g, lru_g, ln_g, ln_b, router_wg, router_bg, router_we, router_be, ident,
           k_hi, k_lo, v_all, y_all, h_dram, q_dram, h1_dram, logits):
    with ExitStack() as ctx:
        sb = lambda n, s, d=F32: ctx.enter_context(nc.sbuf_tensor("d_" + n, s, d))
        ps = lambda n, s, d=F32: ctx.enter_context(nc.psum_tensor("d_" + n, s, d))
        sem = ctx.enter_context(semaphores(nc, "d_"))
        GQ = NQ // NKV
        HALF = TPS // 2
        w_hi = sb("wo_hi", [P, KD, D], F32R)
        w_lo = sb("wo_lo", [P, KD, D], F32R)
        out_g = sb("out_g", [P, KD])
        g_b = sb("ln1_g_b", [P, D])
        b_b = sb("ln1_b_b", [P, D])
        wr = sb("router_w", [P, KD, RW])
        rb_b = sb("router_b", [P, RW])
        ones = sb("ones", [P, 2])
        q_t = [sb(f"q_tile{u}", [P, NQ, P], F32R) for u in range(2)]
        pr = [sb(f"probs{j}", [P, SEQ]) for j in range(2)]
        pt = [sb(f"probs_t{j}", [P, TPS, P]) for j in range(2)]
        mx = sb("mx", [P, 2, NQ])
        nm = sb("neg_max", [P, 2, NQ])
        rsum = sb("rsum", [P, 2, NQ])
        rinv = sb("rinv", [P, NQ])
        o_n = sb("o_n", [P, QW])
        junk = sb("junk", [P, QW])
        m_hi = sb("m_hi", [P, KD, P], F32R)
        m_lo = sb("m_lo", [P, KD, P], F32R)
        lsq = sb("lru_sq", [P, FT, P])
        ssa = sb("ssa", [P, 1])
        var = sb("vars", [P, 2])
        rr = sb("rstds", [P, 2])
        tmp2 = sb("tmp2", [P, 2])
        hb = sb("h_tile", [P, D])
        s_t = sb("s_tile", [P, D])
        h1 = sb("h1_tile", [P, D])
        h1t = sb("h1_t", [P, KD, P])
        stats = sb("stats1", [P, 12])
        mv = sb("mv1", [P, 2])
        var1 = sb("var1", [P, 1])
        tmp1 = sb("tmp1", [P, 1])
        rstd1 = sb("rstd1", [P, 1])
        shift1 = sb("shift1", [P, 1])
        raw = [s_t, h1]
        s_ps = [ps(f"s_ps{j}", [P, SEQ]) for j in range(2)]
        pt_ps = [ps(f"pt_ps{c}", [P, HALF, P]) for c in range(2)]
        o_ps = ps("o_ps", [P, QW])
        m_ps = ps("m_ps", [P, 512])

        rows_in = sem("rows_loaded_d")
        raw_in = [sem(f"wo_raw_loaded{j}") for j in range(2)]
        ones_made = sem("ones_made")
        act_link = sem("act_link_d")
        dve_link = sem("dve_link_d")
        hi_made = sem("wo_hi_made")
        lo_made = sem("wo_lo_made")
        q_in = [sem(f"q_loaded{u}") for u in range(2)]
        s_done = sem("scores_done")
        mx_done = sem("max_done")
        nm_done = sem("neg_max_done")
        p_done = sem("probs_done")
        tr_done = [sem(f"probs_transposed{c}") for c in range(2)]
        pt_done = [sem(f"probs_t_done{c}") for c in range(2)]
        o_done = sem("o_done")
        rinv_done = sem("rinv_done")
        on_done = sem("o_norm_done")
        ssa_done = sem("ssa_done")
        m_done = sem("m_bank_written")
        m_free = sem("m_bank_read")
        mh_done = sem("m_hi_done")
        lh_done = sem("lru_hi_done")
        ll_done = sem("lru_lo_done")
        lsq_done = sem("lru_sq_done")
        h_in = sem("h_loaded")
        ah_done = sem("alpha_h_done")
        ln_done = sem("ln1_stats_done")
        xn_done = sem("ln1_normalised")
        hg_done = sem("ln1_gain_done")
        h1_done = sem("h1_done")
        h1_stored = sem("h1_stored")
        USES = 9
        block = ctx.enter_context(nc.Block())

        def run_heads(eng, first, head, post):
            def tile(t, u, is_first=False, is_last=False):
                for h in range(NQ):
                    nxt = (t, u, h + 1) if h < NQ - 1 else None if is_last else (t + 1, 1 - u, 0)
                    head(t, u, h, nxt, is_first)
                if not is_first:
                    post(t - 1, 1 - u, NQ)
            first()
            tile(0, 0, is_first=True)
            with eng.Fori(0, NT // 2 - 1) as n:
                tile(2 * n + 1, 1)
                tile(2 * n + 2, 0)
            tile(NT - 1, 1, is_last=True)
            for step in range(-1, USES):
                post(NT - 1, 1, step)

        @block.sync
        def _(sp):
            def load_q(t, u):
                sp.dma_start(q_t[u][:].rearrange("p h t -> p (h t)").bitcast(F32),
                             q_dram[bass.ds(t, 1)].rearrange("o p n -> (o p) n")).then_inc(q_in[u], 16)

            def load_h(t):
                sp.dma_start(hb[:], h_dram[bass.ds(t * P, P), :]).then_inc(h_in, 16)

            def store_h1(t):
                sp.wait_ge(h1_done, t + 1)
                sp.dma_start(h1_dram[bass.ds(t * P, P), :], h1[:]).then_inc(h1_stored, 16)

            sp.sem_inc(h1_stored, 16)
            load_q(0, 0)
            load_q(1, 1)
            load_h(0)
            with nc.allow_non_contiguous_dma("small per-feature vectors and router columns"):
                sp.dma_start(out_g[:, 0:FT], attn_g[0].rearrange("(f p) -> p f", p=P)).then_inc(rows_in, 16)
                sp.dma_start(out_g[:, FT:KD], lru_g[0].rearrange("(f p) -> p f", p=P)).then_inc(rows_in, 16)
                sp.dma_start(wr[:, :, 0:G], router_wg[0].rearrange("(k p) g -> p k g", p=P)).then_inc(rows_in, 16)
                sp.dma_start(wr[:, :, G:RW], router_we[0].rearrange("(k p) g e -> p k (g e)", p=P)).then_inc(rows_in, 16)
            sp.dma_start(rb_b[:, 0:G], row(router_bg[0], G)).then_inc(rows_in, 16)
            sp.dma_start(rb_b[:, G:RW], row(router_be[0].rearrange("g e -> (g e)"), NE)).then_inc(rows_in, 16)
            sp.dma_start(g_b[:], row(ln_g[0], D)).then_inc(rows_in, 16)
            sp.dma_start(b_b[:], row(ln_b[0], D)).then_inc(rows_in, 16)
            for k in range(KD):
                need(sp, lo_made, k - 1)
                sp.dma_start(raw[k % 2][:], w_out[0, k * P:(k + 1) * P, :]).then_inc(raw_in[k % 2], 16)

            def during(t, u):
                if u is not None:
                    sp.wait_ge(s_done, NQ * t)
                    load_q(t + 1, u)
                sp.wait_ge(m_free, USES * (t - 1) + 5)
                load_h(t)
                store_h1(t - 1)

            with sp.Fori(0, NT // 2 - 1) as n:
                during(2 * n + 1, 0)
                during(2 * n + 2, 1)
            during(NT - 1, None)
            store_h1(NT - 1)
            sp.wait_ge(h1_stored, 16 * NT + 16)

        @block.tensor
        def _(pe):
            pe.wait_ge(ones_made, 1)

            def scores(t, u, h):
                n = NQ * t + h
                if h == 0:
                    pe.wait_ge(q_in[u], 8 * (t - u) + 16)
                need(pe, p_done, n - 1)
                for c in range(2):
                    out = s_ps[h % 2][:, c * 512:(c + 1) * 512]
                    keys = bass.ds((t // TPS) * SEQ + c * 512, 512)
                    pe.matmul(out, q_t[u][:, h, :], k_hi[:, h // GQ, keys], start=True, stop=False)
                    last = pe.matmul(out, q_t[u][:, h, :], k_lo[:, h // GQ, keys], start=False, stop=True)
                last.then_inc(s_done, 1)

            def head(t, u, h, nxt, is_first):
                n = NQ * t + h
                if nxt:
                    scores(*nxt)
                pe.wait_ge(p_done, n + 1)
                for c in range(2):
                    need(pe, pt_done[c], n)
                    for j in range(HALF):
                        k = c * HALF + j
                        last = pe.transpose(pt_ps[c][:, j, :], pr[h % 2][:, k * P:(k + 1) * P], ident[:])
                    last.then_inc(tr_done[c], 1)
                if not is_first:
                    post(t - 1, 1 - u, h)
                if h == 0:
                    need(pe, on_done, t)
                for k in range(TPS):
                    if k % HALF == 0:
                        pe.wait_ge(pt_done[k // HALF], n + 1)
                    v_rows = v_all[:, bass.ds((t // TPS) * TPS + k, 1), (h // GQ) * HD:(h // GQ + 1) * HD]
                    last = pe.matmul(o_ps[:, h * HD:(h + 1) * HD], pt[h % 2][:, k, :],
                                     v_rows.rearrange("p o d -> p (o d)"), start=k == 0, stop=k == TPS - 1)
                last.then_inc(o_done, 1)

            def project(first_k, half):
                for k in range(FT):
                    kk = first_k + k
                    cols = slice(half * 512, (half + 1) * 512)
                    last = three_pass(pe, m_ps[:], (m_hi[:, kk, :], m_lo[:, kk, :]),
                                      (w_hi[:, kk, cols], w_lo[:, kk, cols]), k == 0, k == FT - 1)
                last.then_inc(m_done, 1)

            def post(t, u, step):
                use = USES * t
                if step == 0:
                    pe.wait_ge(on_done, t + 1)
                    for k in range(FT):
                        last = pe.transpose(m_ps[:, k * P:(k + 1) * P], o_n[:, k * P:(k + 1) * P], ident[:])
                    last.then_inc(m_done, 1)
                if step == 1:
                    pe.wait_ge(lsq_done, t + 1)
                    pe.wait_ge(m_free, use + 1)
                    for k in range(FT):
                        last = pe.matmul(m_ps[:, 0:1], lsq[:, k, :], ones[:, 0:1], start=k == 0, stop=k == FT - 1)
                    last.then_inc(m_done, 1)
                    pe.wait_ge(lo_made, KD)
                    pe.wait_ge(m_free, use + 2)
                    project(0, 0)
                if step == 2:
                    pe.wait_ge(ll_done, t + 1)
                    pe.wait_ge(m_free, use + 3)
                    project(FT, 0)
                if step == 3:
                    pe.wait_ge(m_free, use + 4)
                    project(0, 1)
                if step == 4:
                    pe.wait_ge(m_free, use + 5)
                    project(FT, 1)
                if step in (6, 7):
                    pe.wait_ge(h1_done, t + 1)
                    pe.wait_ge(m_free, use + step)
                    for j in range(FT):
                        k = (step - 6) * FT + j
                        last = pe.transpose(m_ps[:, j * P:(j + 1) * P], h1[:, k * P:(k + 1) * P], ident[:])
                    last.then_inc(m_done, 1)
                if step == 8:
                    pe.wait_ge(m_free, use + 8)
                    for k in range(KD):
                        last = pe.matmul(m_ps[:, 0:RW], h1t[:, k, :], wr[:, k, :], start=k == 0, stop=k == KD - 1)
                    last.then_inc(m_done, 1)

            pe.wait_ge(rows_in, 128)
            run_heads(pe, lambda: scores(0, 0, 0), head, post)

        @block.scalar
        def _(act):
            def exp(t, u, h):
                n = NQ * t + h
                act.wait_ge(nm_done, n + 1)
                need(act, tr_done[1], n - 1)
                act.activation(pr[h % 2][:], s_ps[h % 2][:], ACT.Exp, bias=nm[:, u, h:h + 1], scale=SCALE,
                               accum_out=rsum[:, u, h:h + 1]).then_inc(p_done, 1)

            def head(t, u, h, nxt, is_first):
                n = NQ * t + h
                act.wait_ge(tr_done[0], n + 1)
                need(act, o_done, n - 1)
                act.activation(pt[h % 2][:, 0:HALF], pt_ps[0][:], ACT.Copy).then_inc(pt_done[0], 1)
                if nxt:
                    exp(*nxt)
                if is_first:
                    act.wait_ge(raw_in[h % 2], 16 * (h // 2 + 1))
                    act.wait_ge(rows_in, 128)
                    act.activation(raw[h % 2][:], raw[h % 2][:], ACT.Copy, scale=out_g[:, h:h + 1]).then_inc(act_link, 1)
                    act.wait_ge(act_link, h + 1)
                    act.activation(w_hi[:, h, :], raw[h % 2][:], ACT.Copy).then_inc(hi_made, 1)
                else:
                    post(t - 1, 1 - u, h)

            def post(t, u, step):
                use = USES * t
                if step == 0:
                    act.wait_ge(on_done, t + 1)
                    act.activation(junk[:], o_n[:], ACT.Square, accum_out=ssa[:]).then_inc(ssa_done, 1)
                    act.wait_ge(m_done, use + 1)
                    act.activation(m_hi[:, 0:FT], m_ps[:].rearrange("p (k t) -> p k t", k=FT), ACT.Copy)\
                       .then_inc(mh_done, 1)
                    act.activation(m_hi[:, FT:KD], y_all[:, :, bass.ds(t * P, P)], ACT.Copy).then_inc(lh_done, 1)
                    act.wait_ge(h_in, 16 * t + 16)
                    act.activation(hb[:], hb[:], ACT.Copy, scale=ALPHA).then_inc(ah_done, 1)
                if step == 5:
                    act.wait_ge(ln_done, t + 1)
                    act.activation(s_t[:], s_t[:], ACT.Identity, bias=shift1[:], scale=rstd1[:]).then_inc(xn_done, 1)
                if step in (6, 7):
                    act.wait_ge(m_done, use + step + 1)
                    act.activation(h1t[:, (step - 6) * FT:(step - 5) * FT], m_ps[:].rearrange("p (k t) -> p k t", k=FT),
                                   ACT.Copy).then_inc(m_free, 1)

            run_heads(act, lambda: exp(0, 0, 0), head, post)

        @block.vector
        def _(dve):
            dve.memset(ones[:], 1.0).then_inc(ones_made, 1)
            links = (1 + RSQRT_LINKS) + (4 + RSQRT_LINKS)

            def neg_max(t, u, h):
                n = NQ * t + h
                dve.wait_ge(s_done, n + 1)
                dve.tensor_reduce(mx[:, u, h:h + 1], s_ps[h % 2][:], AX, ALU.max).then_inc(mx_done, 1)
                dve.wait_ge(mx_done, n + 1)
                dve.tensor_scalar(nm[:, u, h:h + 1], mx[:, u, h:h + 1], -SCALE, None, ALU.mult).then_inc(nm_done, 1)

            def head(t, u, h, nxt, is_first):
                n = NQ * t + h
                if nxt:
                    neg_max(*nxt)
                if h == 0 and not is_first:
                    post(t - 1, 1 - u, -1)
                dve.wait_ge(tr_done[1], n + 1)
                need(dve, o_done, n - 1)
                dve.tensor_copy(pt[h % 2][:, HALF:], pt_ps[1][:]).then_inc(pt_done[1], 1)
                if is_first:
                    dve.wait_ge(hi_made, h + 1)
                    dve.tensor_tensor(w_lo[:, h, :], raw[h % 2][:], w_hi[:, h, :].bitcast(F32), ALU.subtract)\
                       .then_inc(lo_made, 1)
                else:
                    post(t - 1, 1 - u, h)

            def post(t, u, step):
                use = USES * t
                if step == -1:
                    dve.wait_ge(o_done, NQ * t + NQ)
                    dve.wait_ge(p_done, NQ * t + NQ)
                    dve.reciprocal(rinv[:], rsum[:, u]).then_inc(rinv_done, 1)
                    dve.wait_ge(rinv_done, t + 1)
                    dve.tensor_tensor(o_n[:].rearrange("p (h d) -> p h d", h=NQ),
                                      o_ps[:].rearrange("p (h d) -> p h d", h=NQ),
                                      rinv[:].unsqueeze(2).broadcast_to([P, NQ, HD]), ALU.mult).then_inc(on_done, 1)
                if step == 0:
                    dve.wait_ge(lh_done, t + 1)
                    dve.nop(nofuse=True)
                    dve.tensor_tensor(m_lo[:, FT:KD], y_all[:, :, bass.ds(t * P, P)], m_hi[:, FT:KD].bitcast(F32),
                                      ALU.subtract).then_inc(ll_done, 1)
                    dve.wait_ge(mh_done, t + 1)
                    dve.tensor_tensor(m_lo[:, 0:FT], m_ps[:].rearrange("p (k t) -> p k t", k=FT),
                                      m_hi[:, 0:FT].bitcast(F32), ALU.subtract).then_inc(m_free, 1)
                if step == 1:
                    link = Chain(dve, dve_link, links * t)
                    dve.wait_ge(m_done, use + 2)
                    dve.tensor_scalar(var[:, 1:2], m_ps[:, 0:1], 1.0 / LW, LN_EPS, ALU.mult, ALU.add).then_inc(m_free, 1)
                    dve.wait_ge(m_free, use + 2)
                    dve.wait_ge(ssa_done, t + 1)
                    link(dve.tensor_scalar(var[:, 0:1], ssa[:], 1.0 / QW, LN_EPS, ALU.mult, ALU.add))
                    rsqrt(dve, link, var[:], rr[:], tmp2[:])
                    dve.wait_ge(m_done, use + 3)
                    dve.wait_ge(ah_done, t + 1)
                    dve.scalar_tensor_tensor(s_t[:, 0:512], m_ps[:], rr[:, 0:1], hb[:, 0:512], ALU.mult, ALU.add)\
                       .then_inc(m_free, 1)
                if step == 2:
                    dve.wait_ge(m_done, use + 4)
                    dve.wait_ge(m_free, use + 3)
                    dve.scalar_tensor_tensor(s_t[:, 0:512], m_ps[:], rr[:, 1:2], s_t[:, 0:512], ALU.mult, ALU.add)\
                       .then_inc(m_free, 1)
                if step == 3:
                    dve.wait_ge(m_done, use + 5)
                    dve.scalar_tensor_tensor(s_t[:, 512:], m_ps[:], rr[:, 0:1], hb[:, 512:], ALU.mult, ALU.add)\
                       .then_inc(m_free, 1)
                if step == 4:
                    link = Chain(dve, dve_link, links * t + 1 + RSQRT_LINKS)
                    dve.wait_ge(m_done, use + 6)
                    dve.wait_ge(m_free, use + 5)
                    dve.scalar_tensor_tensor(s_t[:, 512:], m_ps[:], rr[:, 1:2], s_t[:, 512:], ALU.mult, ALU.add)\
                       .then_inc(m_free, 1)
                    dve.wait_ge(m_free, use + 6)
                    for half in range(2):
                        link(dve.bn_stats(stats[:, 6 * half:6 * half + 6], s_t[:, 512 * half:512 * half + 512]))
                    dve.nop(nofuse=True)
                    link(dve.bn_aggr(mv[:], stats[:]))
                    link(dve.tensor_scalar(var1[:], mv[:, 1:2], LN_EPS, None, ALU.add))
                    rsqrt(dve, link, var1[:], rstd1[:], tmp1[:])
                    dve.tensor_scalar(shift1[:], mv[:, 0:1], rstd1[:], -1.0, ALU.mult, ALU.mult).then_inc(ln_done, 1)
                if step == 5:
                    dve.wait_ge(xn_done, t + 1)
                    dve.wait_ge(h1_stored, 16 * t + 16)
                    dve.tensor_tensor(h1[:], s_t[:], g_b[:], ALU.mult).then_inc(hg_done, 1)
                if step == 8:
                    dve.wait_ge(m_done, use + 9)
                    dve.nop(nofuse=True)
                    dve.tensor_tensor(logits[:, bass.ds(t, 1), :].rearrange("p o n -> p (o n)"), m_ps[:, 0:RW], rb_b[:],
                                      ALU.add).then_inc(m_free, 1)

            run_heads(dve, lambda: neg_max(0, 0, 0), head, post)

        @block.gpsimd
        def _(pool):
            def post(t, step):
                if step == 0:
                    need(pool, m_done, USES * (t - 1) + 2)
                    pool.nop(nofuse=True)
                    part = y_all[:, :, bass.ds(t * P, P)]
                    pool.tensor_tensor(lsq[:], part, part, ALU.mult).then_inc(lsq_done, 1)
                if step == 5:
                    pool.wait_ge(hg_done, t + 1)
                    pool.tensor_tensor(h1[:], h1[:], b_b[:], ALU.add).then_inc(h1_done, 1)

            pool.wait_ge(rows_in, 128)
            post(0, 0)
            with pool.Fori(1, NT) as t:
                post(t, 0)
                post(t - 1, 5)
            post(NT - 1, 5)


def route(nc, ident, logits, list_dram, slots, weights, lists, tile_expert, tiles_to):
    with ExitStack() as ctx:
        sb = lambda n, s, d=F32: ctx.enter_context(nc.sbuf_tensor("r_" + n, s, d))
        sem = ctx.enter_context(semaphores(nc, "r_"))
        gl = logits[:, :, 0:G]
        el = logits[:, :, G:RW].rearrange("p t (g e) -> p t g e", g=G)
        top = sb("top", [P, NT])
        gd = sb("gd", [P, NT, G])
        ge = sb("ge", [P, NT, G])
        gsum = sb("gsum", [P, NT])
        gprob = sb("gprob", [P, NT])
        eq = sb("eq", [P, NT, G])
        seen = sb("seen", [P, NT])
        oh_g = sb("oh_g", [P, NT, G])
        oh_e = [sb(f"oh_e{c}", [P, NT, E_IN_G]) for c in range(2)]
        prod = sb("prod", [P, NT, G, E_IN_G])
        es = sb("es", [P, NT, E_IN_G])
        m1 = sb("m1", [P, NT])
        m2 = sb("m2", [P, NT])
        gap = sb("gap", [P, NT])
        x2 = sb("x2", [P, NT])
        hot = [sb(f"hot{c}", [P, NT, G, E_IN_G]) for c in range(2)]
        both = sb("both", [P, NT, NE])
        tri = sb("tri", [P, P])
        ones = sb("ones", [P, P])
        offs = sb("offs", [P, NT + 1, NE])
        thr_i = sb("thr_i", [P, NT], I32)
        thr = sb("thr", [P, NT])
        over = sb("over", [P, NE, NT])
        n_tiles = sb("n_tiles", [P, NE])
        upto = sb("upto", [P, NE])
        start = sb("start", [P, NE])
        base = sb("base", [P, NT, NE])
        slot_f = sb("slot_f", [P, 2, NT])
        tile_i = sb("tile_i", [P, MT], I32)
        tile_f = sb("tile_f", [P, MT])
        past = sb("past", [P, MT, NE])
        exp_f = sb("exp_f", [P, MT])
        tok_i = sb("tok_i", [P, NT], I32)
        tok = sb("tok", [P, NT])
        zero = sb("zero", [MT, P])
        rows = sb("rows", [MT, P])
        rank_ps = ctx.enter_context(nc.psum_tensor("rank_ps", [P, NT * NE], F32))
        tot_ps = ctx.enter_context(nc.psum_tensor("tot_ps", [P, NT * NE], F32))
        list_ps = ctx.enter_context(nc.psum_tensor("list_ps", [P, MT], F32))

        dve_link = sem("dve_link")
        pool_link = sem("pool_link")
        made = sem("constants_made")
        gd_done = sem("gd_done")
        ge_done = sem("ge_done")
        gap_done = sem("gap_done")
        x2_done = sem("x2_done")
        both_done = sem("both_done")
        counted = sem("counted")
        slots_done = sem("slots_done")
        zeroed = sem("list_zeroed")
        scattered = sem("list_scattered")
        rows_in = sem("list_loaded")
        turned = sem("list_transposed")
        block = ctx.enter_context(nc.Block())

        @block.gpsimd
        def _(pool):
            link = Chain(pool, pool_link)
            pool.memset(zero[:], 0.0).then_inc(made, 1)
            pool.memset(ones[:], 1.0).then_inc(made, 1)
            pool.iota(thr_i[:], [[P, NT]], base=0, channel_multiplier=0).then_inc(made, 1)
            pool.iota(tile_i[:], [[1, MT]], base=0, channel_multiplier=0).then_inc(made, 1)
            pool.iota(tok_i[:], [[P, NT]], base=0, channel_multiplier=1).then_inc(made, 1)
            link(pool.memset(tri[:], 1.0))
            pool.affine_select(out=tri[:], in_=tri[:], compare_op=ALU.is_gt, fill=0.0, base=0,
                               pattern=[[1, P]], channel_multiplier=-1).then_inc(made, 1)
            pool.wait_ge(zeroed, 16)
            pool.wait_ge(slots_done, 1)
            for c in range(2):
                for t in range(NT):
                    pool.indirect_dma_start(list_dram, bass.IndirectOffsetOnAxis(slots[:, c, t:t + 1], 0),
                                            tok[:, t:t + 1], None).then_inc(scattered, 16)

        @block.sync
        def _(sp):
            list_rows = list_dram.rearrange("(j p) o -> j (p o)", p=P)
            sp.wait_ge(made, 1)
            sp.dma_start(list_rows, zero[:]).then_inc(zeroed, 16)
            sp.wait_ge(scattered, 16 * 2 * NT)
            sp.dma_start(rows[:], list_rows).then_inc(rows_in, 16)

        @block.scalar
        def _(act):
            act.wait_ge(gd_done, 1)
            act.activation(ge[:], gd[:], ACT.Exp).then_inc(ge_done, 1)
            act.wait_ge(gap_done, 1)
            act.activation(x2[:], gap[:], ACT.Exp).then_inc(x2_done, 1)

        @block.vector
        def _(dve):
            link = Chain(dve, dve_link)
            over_g = lambda v: v[:].unsqueeze(2).broadcast_to([P, NT, G])

            def first_hot(out):
                link(dve.tensor_copy(out[:, :, 0], eq[:, :, 0]))
                link(dve.tensor_copy(seen[:], eq[:, :, 0]))
                for j in range(1, G):
                    link(dve.scalar_tensor_tensor(out[:, :, j], seen[:], 0.5, eq[:, :, j], ALU.is_lt, ALU.mult))
                    link(dve.tensor_tensor(seen[:], seen[:], eq[:, :, j], ALU.max))

            link(dve.tensor_reduce(top[:], gl, AX, ALU.max))
            dve.tensor_tensor(gd[:], gl, over_g(top), ALU.subtract).then_inc(gd_done, 1)
            link(dve.tensor_tensor(eq[:], gl, over_g(top), ALU.is_equal))
            first_hot(oh_g)
            dve.wait_ge(ge_done, 1)
            link(dve.tensor_reduce(gsum[:], ge[:], AX, ALU.add))
            link(dve.reciprocal(gprob[:], gsum[:]))
            group_hot = oh_g[:].unsqueeze(3).broadcast_to([P, NT, G, E_IN_G])
            link(dve.tensor_tensor(prod[:], el, group_hot, ALU.mult))
            link(dve.tensor_reduce(es[:], prod[:].rearrange("p t g e -> p t e g"), AX, ALU.add))
            link(dve.tensor_reduce(m1[:], es[:], AX, ALU.max))
            link(dve.tensor_tensor(eq[:], es[:], over_g(m1), ALU.is_equal))
            first_hot(oh_e[0])
            link(dve.scalar_tensor_tensor(es[:], oh_e[0][:], -3e38, es[:], ALU.mult, ALU.add))
            link(dve.tensor_reduce(m2[:], es[:], AX, ALU.max))
            link(dve.tensor_tensor(eq[:], es[:], over_g(m2), ALU.is_equal))
            first_hot(oh_e[1])
            dve.tensor_tensor(gap[:], m2[:], m1[:], ALU.subtract).then_inc(gap_done, 1)
            for c in range(2):
                link(dve.tensor_tensor(hot[c][:], group_hot, oh_e[c][:].unsqueeze(2).broadcast_to([P, NT, G, E_IN_G]),
                                       ALU.mult))
            dve.tensor_tensor(both[:], hot[0][:].rearrange("p t g e -> p t (g e)"),
                              hot[1][:].rearrange("p t g e -> p t (g e)"), ALU.add).then_inc(both_done, 1)
            dve.wait_ge(x2_done, 1)
            link(dve.tensor_scalar(m1[:], x2[:], 1.0, None, ALU.add))
            link(dve.reciprocal(m2[:], m1[:]))
            link(dve.tensor_tensor(weights[:, 0], m2[:], gprob[:], ALU.mult))
            link(dve.tensor_tensor(weights[:, 1], weights[:, 0], x2[:], ALU.mult))
            dve.wait_ge(made, 6)
            link(dve.tensor_copy(thr[:], thr_i[:]))
            link(dve.tensor_copy(tile_f[:], tile_i[:]))
            link(dve.tensor_copy(tok[:], tok_i[:]))
            dve.wait_ge(counted, 2)
            link(dve.memset(offs[:, 0], 0.0))
            for t in range(NT):
                link(dve.tensor_tensor(offs[:, t + 1], offs[:, t], tot_ps[:, t * NE:(t + 1) * NE], ALU.add))
            link(dve.tensor_tensor(over[:], offs[:, NT].unsqueeze(2).broadcast_to([P, NE, NT]),
                                   thr[:].unsqueeze(1).broadcast_to([P, NE, NT]), ALU.is_gt))
            link(dve.tensor_reduce(n_tiles[:], over[:], AX, ALU.add))
            link(dve.tensor_tensor_scan(upto[:], ones[:, 0:NE], n_tiles[:], 0.0, ALU.mult, ALU.add))
            link(dve.tensor_copy(tiles_to[:], upto[:]))
            link(dve.tensor_tensor(start[:], upto[:], n_tiles[:], ALU.subtract))
            link(dve.tensor_scalar(start[:], start[:], float(P), None, ALU.mult))
            link(dve.tensor_tensor(base[:], rank_ps[:].rearrange("p (t e) -> p t e", t=NT), offs[:, 0:NT], ALU.add))
            link(dve.tensor_tensor(base[:], base[:], start[:].unsqueeze(1).broadcast_to([P, NT, NE]), ALU.add))
            for c in range(2):
                pick = hot[c][:].rearrange("p t g e -> p t (g e)")
                link(dve.tensor_tensor(both[:], base[:], pick, ALU.mult))
                link(dve.tensor_reduce(slot_f[:, c], both[:], AX, ALU.add))
            dve.tensor_copy(slots[:], slot_f[:]).then_inc(slots_done, 1)
            link(dve.tensor_tensor(past[:], upto[:].unsqueeze(1).broadcast_to([P, MT, NE]),
                                   tile_f[:].unsqueeze(2).broadcast_to([P, MT, NE]), ALU.is_le))
            link(dve.tensor_reduce(exp_f[:], past[:], AX, ALU.add))
            link(dve.tensor_scalar(exp_f[:], exp_f[:], float(NE - 1), None, ALU.min))
            link(dve.tensor_copy(tile_expert[:], exp_f[:]))
            dve.wait_ge(turned, 1)
            link(dve.tensor_copy(lists[:], list_ps[:]))

        @block.tensor
        def _(pe):
            pe.wait_ge(both_done, 1)
            pe.wait_ge(made, 6)
            m = both[:].rearrange("p t e -> p (t e)")
            pe.matmul(rank_ps[:], tri[:], m, start=True, stop=True).then_inc(counted, 1)
            pe.matmul(tot_ps[:], ones[:], m, start=True, stop=True).then_inc(counted, 1)
            pe.wait_ge(rows_in, 16)
            pe.transpose(list_ps[:], rows[:], ident[0:MT, 0:MT]).then_inc(turned, 1)


def experts(nc, exp_w1, exp_w3, exp_w2, ident, lists, tile_expert, tiles_to, h1_dram, y_dram):
    with ExitStack() as ctx:
        sb = lambda n, s, d=F32: ctx.enter_context(nc.sbuf_tensor("e_" + n, s, d))
        ps = lambda n, s, d=F32: ctx.enter_context(nc.psum_tensor("e_" + n, s, d))
        sem = ctx.enter_context(semaphores(nc, "e_"))
        WB = 4
        HALF = KD // 2
        w13 = sb("w13", [P, WB, KD, 2 * DE])
        w2 = sb("w2", [P, WB, KE, D])
        ix = [sb(f"ix{u}", [P, 1], U32) for u in range(2)]
        xg = [sb(f"xg{u}", [P, D]) for u in range(2)]
        xt = [sb(f"xt{u}", [P, KD, P]) for u in range(2)]
        sg = sb("sg", [P, DE])
        hid = sb("hid", [P, DE])
        ht = sb("ht", [P, KE, P])
        yt = [sb(f"yt{u}", [P, D]) for u in range(2)]
        t_ps = [ps(f"t_ps{c}", [P, HALF, P]) for c in range(2)]
        a_ps = [ps(f"a_ps{u}", [P, 2 * DE]) for u in range(2)]
        h_ps = ps("h_ps", [P, KE, P])
        y_ps = [ps(f"y_ps{c}", [P, 512]) for c in range(2)]

        ix_done = sem("index_ready")
        x_in = [sem(f"rows_gathered{u}") for u in range(2)]
        w_in = [sem(f"weights_loaded{b}") for b in range(WB)]
        w_ready = sem("weights_ready")
        t_done = [sem(f"x_transposed{c}") for c in range(2)]
        xt_done = [sem(f"xt_done{c}") for c in range(2)]
        a_done = sem("a_done")
        sg_done = sem("silu_done")
        hid_done = sem("hid_done")
        h_done = sem("hid_transposed")
        ht_done = sem("ht_done")
        y_done = [sem(f"y_done{c}") for c in range(2)]
        yt_done = [sem(f"yt_done{c}") for c in range(2)]
        y_stored = [sem(f"y_stored{u}") for u in range(2)]
        tile_done = y_done[1]
        block = ctx.enter_context(nc.Block())

        def run_tiles(eng, gather, up, down):
            gather(0, 0)
            with eng.Fori(0, MT // 2 - 1) as n:
                for u in range(2):
                    up(2 * n + u, u)
                    gather(2 * n + u + 1, 1 - u)
                    down(2 * n + u, u)
            up(MT - 2, 0)
            gather(MT - 1, 1)
            down(MT - 2, 0)
            up(MT - 1, 1)
            down(MT - 1, 1)

        def skip(j, u):
            pass

        @block.sync
        def _(sp):
            def load(e, b):
                part = lambda w: w[0][bass.ds(e, 1)].rearrange("o (k p) n -> p (o k) n", p=P)
                sp.dma_start(w13[:, b, :, 0:DE], part(exp_w1)).then_inc(w_in[b], 16)
                sp.dma_start(w13[:, b, :, DE:2 * DE], part(exp_w3)).then_inc(w_in[b], 16)
                sp.dma_start(w2[:, b], part(exp_w2)).then_inc(w_in[b], 16)

            for b in range(WB):
                load(b, b)
            with sp.Fori(0, NE // WB - 1) as n:
                for b in range(WB):
                    sp.wait_ge(w_in[b], 48 * n + 48)
                    sp.sem_inc(w_ready, 1)
                    used = sp.value_load(tiles_to[0:1, bass.ds(WB * n + b, 1)], min_val=0, max_val=MT)
                    sp.wait_ge(tile_done, used + 1)
                    load(WB * n + WB + b, b)
            for b in range(WB):
                sp.wait_ge(w_in[b], 48 * (NE // WB))
                sp.sem_inc(w_ready, 1)

        @block.gpsimd
        def _(pool):
            def gather(j, u):
                pool.wait_ge(ix_done, j + 1)
                pool.wait_ge(t_done[1], j + 1)
                pool.nop(nofuse=True)
                pool.indirect_dma_start(xg[u][:], None, h1_dram, bass.IndirectOffsetOnAxis(ix[u][:, 0:1], 0))\
                    .then_inc(x_in[u], 16)

            run_tiles(pool, gather, skip, skip)

        @block.tensor
        def _(pe):
            pe.sem_inc(t_done[1], 2)
            pe.sem_inc(a_done, 2)
            pe.sem_inc(h_done, 1)
            pe.sem_inc(tile_done, 1)

            def gather(j, u):
                pe.wait_ge(x_in[u], 8 * (j - u) + 16)
                for c in range(2):
                    pe.wait_ge(xt_done[c], j + 1)
                    for i in range(HALF):
                        k = c * HALF + i
                        last = pe.transpose(t_ps[c][:, i, :], xg[u][:, k * P:(k + 1) * P], ident[:])
                    last.then_inc(t_done[c], 1)

            def up(j, u):
                e = pe.value_load(tile_expert[0:1, bass.ds(j, 1)], min_val=0, max_val=NE - 1)
                pe.wait_ge(w_ready, e + 1)
                pe.wait_ge(hid_done, j + 1)
                for k in range(KD):
                    if k % HALF == 0:
                        pe.wait_ge(xt_done[k // HALF], j + 2)
                    rhs = w13[:, bass.ds(e % WB, 1), k, :].rearrange("p o n -> p (o n)")
                    last = pe.matmul(a_ps[u][:], xt[u][:, k, :], rhs, start=k == 0, stop=k == KD - 1)
                last.then_inc(a_done, 1)

            def down(j, u):
                e = pe.value_load(tile_expert[0:1, bass.ds(j, 1)], min_val=0, max_val=NE - 1)
                pe.wait_ge(hid_done, j + 3)
                pe.wait_ge(ht_done, j + 1)
                for k in range(KE):
                    last = pe.transpose(h_ps[:, k, :], hid[:, k * P:(k + 1) * P], ident[:])
                last.then_inc(h_done, 1)
                pe.wait_ge(ht_done, j + 2)
                for c in range(2):
                    pe.wait_ge(yt_done[c], j + 1)
                    for k in range(KE):
                        rhs = w2[:, bass.ds(e % WB, 1), k, c * 512:(c + 1) * 512].rearrange("p o n -> p (o n)")
                        last = pe.matmul(y_ps[c][:], ht[:, k, :], rhs, start=k == 0, stop=k == KE - 1)
                    last.then_inc(y_done[c], 1)

            run_tiles(pe, gather, up, down)

        @block.scalar
        def _(act):
            act.sem_inc(xt_done[0], 1)
            act.sem_inc(ht_done, 1)
            act.sem_inc(yt_done[0], 1)
            for u in range(2):
                act.sem_inc(y_stored[u], 16)

            def gather(j, u):
                act.wait_ge(a_done, j + 1)
                act.wait_ge(t_done[0], j + 1)
                act.activation(xt[u][:, 0:HALF], t_ps[0][:], ACT.Copy).then_inc(xt_done[0], 1)

            def up(j, u):
                act.wait_ge(a_done, j + 3)
                act.wait_ge(hid_done, j + 2)
                act.activation(sg[:], a_ps[u][:, 0:DE], ACT.Silu).then_inc(sg_done, 1)

            def down(j, u):
                act.wait_ge(h_done, j + 2)
                act.activation(ht[:], h_ps[:], ACT.Copy).then_inc(ht_done, 1)
                act.wait_ge(y_done[0], j + 1)
                act.wait_ge(y_stored[u], 8 * (j - u) + 16)
                act.activation(yt[u][:, 0:512], y_ps[0][:], ACT.Copy).then_inc(yt_done[0], 1)
                act.wait_ge(yt_done[0], j + 2)
                act.wait_ge(yt_done[1], j + 2)
                act.dma_start(y_dram[bass.ds(j * P, P), :], yt[u][:]).then_inc(y_stored[u], 16)

            run_tiles(act, gather, up, down)
            for u in range(2):
                act.wait_ge(y_stored[u], 16 + 8 * MT)

        @block.vector
        def _(dve):
            dve.sem_inc(xt_done[1], 1)
            dve.sem_inc(hid_done, 2)
            dve.sem_inc(yt_done[1], 1)

            def index(j, u):
                dve.wait_ge(t_done[1], j + 1)
                dve.nop(nofuse=True)
                dve.tensor_copy(ix[u][:], lists[:, bass.ds(j, 1)]).then_inc(ix_done, 1)

            def gather(j, u):
                dve.wait_ge(a_done, j + 1)
                dve.wait_ge(t_done[1], j + 3)
                dve.tensor_copy(xt[u][:, HALF:], t_ps[1][:]).then_inc(xt_done[1], 1)

            def up(j, u):
                if not (isinstance(j, int) and j == MT - 1):
                    index(j + 1, 1 - u)
                dve.wait_ge(sg_done, j + 1)
                dve.wait_ge(h_done, j + 1)
                dve.tensor_tensor(hid[:], sg[:], a_ps[u][:, DE:2 * DE], ALU.mult).then_inc(hid_done, 1)

            def down(j, u):
                dve.wait_ge(y_done[1], j + 2)
                dve.wait_ge(y_stored[u], 8 * (j - u) + 16)
                dve.tensor_copy(yt[u][:, 512:], y_ps[1][:]).then_inc(yt_done[1], 1)

            index(0, 0)
            run_tiles(dve, gather, up, down)


def combine(nc, ln_g, ln_b, slots, weights, h1_dram, y_dram, out):
    with ExitStack() as ctx:
        sb = lambda n, s, d=F32: ctx.enter_context(nc.sbuf_tensor("c_" + n, s, d))
        sem = ctx.enter_context(semaphores(nc, "c_"))
        NB = 4
        g_b = sb("g_b", [P, D])
        b_b = sb("b_b", [P, D])
        ix = [sb(f"ix{u}", [P, 2], U32) for u in range(NB)]
        h1 = [sb(f"h1{u}", [P, D]) for u in range(NB)]
        y1 = [sb(f"y1{u}", [P, D]) for u in range(NB)]
        y2 = [sb(f"y2{u}", [P, D]) for u in range(NB)]
        wt = [sb(f"wt{u}", [P, 2]) for u in range(NB)]
        stats = sb("stats", [P, 12])
        mv = sb("mv", [P, 2])
        var = sb("var", [P, 1])
        tmp = sb("tmp", [P, 1])
        rstd = [sb(f"rstd{u}", [P, 1]) for u in range(NB)]
        shift = [sb(f"shift{u}", [P, 1]) for u in range(NB)]
        rows_in = sem("rows_loaded")
        ix_done = sem("index_ready")
        h_in = [sem(f"h1_loaded{u}") for u in range(NB)]
        y_in = [sem(f"y_gathered{u}") for u in range(NB)]
        dve_link = sem("dve_link")
        ah_done = sem("alpha_h_done")
        ln_done = sem("stats_done")
        xn_done = sem("normalised")
        hg_done = sem("gain_done")
        o_done = sem("out_done")
        stored = [sem(f"stored{u}") for u in range(NB)]
        block = ctx.enter_context(nc.Block())

        @block.sync
        def _(sp):
            for u in range(NB):
                sp.sem_inc(stored[u], 16)
            sp.dma_start(g_b[:], row(ln_g, D)).then_inc(rows_in, 16)
            sp.dma_start(b_b[:], row(ln_b, D)).then_inc(rows_in, 16)
            with sp.Fori(0, NT // NB) as n:
                for u in range(NB):
                    t = NB * n + u
                    sp.wait_ge(stored[u], 16 * n + 16)
                    sp.dma_start(h1[u][:], h1_dram[bass.ds(t * P, P), :]).then_inc(h_in[u], 16)
            for u in range(NB):
                sp.wait_ge(stored[u], 16 + 16 * (NT // NB))

        def run_tiles(eng, load, norm, finish):
            for u in range(NB - 1):
                load(u, u)
            norm(0, 0, 0)
            with eng.Fori(0, NT // NB - 1) as n:
                for u in range(NB):
                    t = NB * n + u
                    load(t + NB - 1, (u + NB - 1) % NB)
                    norm(t + 1, (u + 1) % NB, 0)
                    finish(t, u)
            for u in range(NB):
                t = NT - NB + u
                if u == 0:
                    load(NT - 1, NB - 1)
                if u < NB - 1:
                    norm(t + 1, u + 1, 0)
                finish(t, u)

        @block.gpsimd
        def _(pool):
            pool.wait_ge(rows_in, 32)

            def load(t, u):
                pool.wait_ge(ix_done, t + 1)
                pool.wait_ge(ln_done, t + 1)
                pool.nop(nofuse=True)
                for c, y in enumerate((y1, y2)):
                    pool.indirect_dma_start(y[u][:], None, y_dram, bass.IndirectOffsetOnAxis(ix[u][:, c:c + 1], 0))\
                        .then_inc(y_in[u], 16)

            def finish(t, u):
                pool.wait_ge(hg_done, t + 1)
                pool.tensor_tensor(h1[u][:], h1[u][:], b_b[:], ALU.add).then_inc(o_done, 1)

            run_tiles(pool, load, lambda t, u, z: None, finish)

        @block.vector
        def _(dve):
            dve.sem_inc(ln_done, NB)
            links = 2 + 4 + RSQRT_LINKS

            def load(t, u):
                dve.wait_ge(ln_done, t + 1)
                dve.nop(nofuse=True)
                dve.tensor_copy(wt[u][:], weights[:, :, bass.ds(t, 1)].rearrange("p c o -> p (c o)"))
                dve.tensor_copy(ix[u][:], slots[:, :, bass.ds(t, 1)].rearrange("p c o -> p (c o)")).then_inc(ix_done, 1)

            def norm(t, u, z):
                link = Chain(dve, dve_link, links * t)
                dve.wait_ge(ah_done, t + 1)
                dve.wait_ge(ix_done, t + 1)
                dve.wait_ge(y_in[u], 8 * (t - u) + 32)
                link(dve.scalar_tensor_tensor(h1[u][:], y1[u][:], wt[u][:, 0:1], h1[u][:], ALU.mult, ALU.add))
                link(dve.scalar_tensor_tensor(h1[u][:], y2[u][:], wt[u][:, 1:2], h1[u][:], ALU.mult, ALU.add))
                for half in range(2):
                    link(dve.bn_stats(stats[:, 6 * half:6 * half + 6], h1[u][:, 512 * half:512 * half + 512]))
                dve.nop(nofuse=True)
                link(dve.bn_aggr(mv[:], stats[:]))
                link(dve.tensor_scalar(var[:], mv[:, 1:2], LN_EPS, None, ALU.add))
                rsqrt(dve, link, var[:], rstd[u][:], tmp[:])
                dve.tensor_scalar(shift[u][:], mv[:, 0:1], rstd[u][:], -1.0, ALU.mult, ALU.mult).then_inc(ln_done, 1)

            def finish(t, u):
                dve.wait_ge(xn_done, t + 1)
                dve.tensor_tensor(h1[u][:], h1[u][:], g_b[:], ALU.mult).then_inc(hg_done, 1)

            dve.wait_ge(rows_in, 32)
            run_tiles(dve, load, norm, finish)

        @block.scalar
        def _(act):
            def load(t, u):
                act.wait_ge(h_in[u], 4 * (t - u) + 16)
                act.activation(h1[u][:], h1[u][:], ACT.Copy, scale=ALPHA).then_inc(ah_done, 1)

            def norm(t, u, z):
                act.wait_ge(ln_done, t + NB + 1)
                act.activation(h1[u][:], h1[u][:], ACT.Identity, bias=shift[u][:], scale=rstd[u][:]).then_inc(xn_done, 1)

            def finish(t, u):
                act.wait_ge(o_done, t + 1)
                act.dma_start(out[bass.ds(t * P, P), :], h1[u][:]).then_inc(stored[u], 16)

            run_tiles(act, load, norm, finish)


_NAMES = ["ln_in_g", "ln_in_b", "w_in", "conv_w", "conv_b", "lru_wa", "lru_ba", "lru_wx", "lru_bx", "lru_lambda",
          "q_norm_g", "k_norm_g", "attn_out_g", "lru_out_g", "w_out", "ln1_g", "ln1_b", "router_wg", "router_bg",
          "router_we", "router_be", "exp_w1", "exp_w3", "exp_w2", "ln2_g", "ln2_b"]


def rope_table():
    import numpy as np

    grid_w, theta, half = 64, 10000.0, HD // 4
    inv_freq = (theta ** (-np.arange(half, dtype=np.float32) / half)).astype(np.float32)
    pos = np.arange(SEQ)
    tab = np.zeros((P, TPS, 2, 2, 2, half), np.float32)
    for sec, where in enumerate((pos // grid_w, pos % grid_w)):
        ang = where.astype(np.float32)[:, None] * inv_freq
        cos = np.cos(ang).reshape(TPS, P, half).transpose(1, 0, 2)
        sin = np.sin(ang).reshape(TPS, P, half).transpose(1, 0, 2)
        for f in range(2):
            tab[:, :, 0, sec, f] = cos
            tab[:, :, 1, sec, f] = sin if f else -sin
    return tab.reshape(P, TPS * 2 * HD)


def kernel(**inputs):
    import numpy as np
    import concourse.bacc as bacc
    from concourse.bass_utils import run_bass_kernel_spmd

    nc = bacc.Bacc("TRN2", target_bir_lowering=False, num_devices=1)
    arrays = {"in_x": np.concatenate([inputs["x_prompt"][0], inputs["x_sample"][0]])}
    for name in _NAMES:
        arrays[f"in_{name}"] = np.ascontiguousarray(inputs[name])
    arrays["in_rope"] = rope_table()
    args = [nc.dram_tensor(n, a.shape, mybir.dt.from_np(a.dtype), kind="ExternalInput").ap() for n, a in arrays.items()]
    args.append(nc.dram_tensor("out", (T, D), F32, kind="ExternalOutput").ap())
    build(nc, *args)
    got = run_bass_kernel_spmd(nc, [arrays], core_ids=[0]).results[0]["out"]
    return got[None, 0:SEQ], got[None, SEQ:T]
```

```python
from contextlib import ExitStack, contextmanager

import concourse.bass as bass
from concourse import mybir

F32 = mybir.dt.float32
F32R = mybir.dt.float32r
I32 = mybir.dt.int32
U32 = mybir.dt.uint32
ALU = mybir.AluOpType
ACT = mybir.ActivationFunctionType
AX = mybir.AxisListType.X

P = 128
D = 1024
KD = D // P
SEQS = 2
SEQ = 1024
T = SEQS * SEQ
NT = T // P
TPS = SEQ // P
CH = 256
NC = T // CH
CPS = SEQ // CH
HD = 64
NQ = 8
NKV = 2
NH = NQ + NKV
QW = NQ * HD
KVW = NKV * HD
QKVW = QW + 2 * KVW
QKW = QW + KVW
LW = 512
FT = LW // P
LHD = 64
TAPS = 4
G = 4
E_IN_G = 4
NE = G * E_IN_G
DE = 256
KE = DE // P
RW = G + NE
MT = 2 * NT + NE
SLOTS = MT * P
LN_EPS = 1e-5
QK_EPS = 1e-6
LRU_C = 8.0
ALPHA = 2.0 ** 0.25
SCALE = HD ** -0.5
NEWTON = 3


class Chain:

    def __init__(self, eng, sem, done=0):
        self.eng, self.sem, self.done, self.n = eng, sem, done, 0

    def __call__(self, ins):
        self.n += 1
        ins.then_inc(self.sem, 1)
        self.eng.wait_ge(self.sem, self.done + self.n)


def rsqrt(dve, link, x, y, t):
    link(dve.tensor_scalar(t.bitcast(I32), x.bitcast(I32), 1, None, ALU.logical_shift_right))
    link(dve.tensor_scalar(y.bitcast(I32), t.bitcast(I32), -1.0, float(0x5F3759DF), ALU.mult, ALU.add))
    link(dve.tensor_scalar(x, x, -0.5, None, ALU.mult))
    for _ in range(NEWTON):
        if x.shape[-1] == 1:
            link(dve.scalar_tensor_tensor(t, y, x, y, ALU.mult, ALU.mult))
        else:
            link(dve.tensor_tensor(t, y, y, ALU.mult))
            link(dve.tensor_tensor(t, t, x, ALU.mult))
        link(dve.scalar_tensor_tensor(y, t, 1.5, y, ALU.add, ALU.mult))


RSQRT_LINKS = 3 + 2 * NEWTON
RSQRT_LINKS_WIDE = 3 + 3 * NEWTON


def three_pass(pe, out, lhs, rhs, first, last):
    pe.matmul(out, lhs[0], rhs[0], start=first, stop=False)
    pe.matmul(out, lhs[0], rhs[1], start=False, stop=False)
    return pe.matmul(out, lhs[1], rhs[0], start=False, stop=last)


def build(nc, x, ln_in_g, ln_in_b, w_in, conv_w, conv_b, lru_wa, lru_ba, lru_wx, lru_bx, lru_lambda,
          q_norm_g, k_norm_g, attn_out_g, lru_out_g, w_out, ln1_g, ln1_b, router_wg, router_bg,
          router_we, router_be, exp_w1, exp_w3, exp_w2, ln2_g, ln2_b, rope, out):
    h_dram = nc.dram_tensor("h_dram", (T, D), F32, kind="Internal").ap()
    ht_hi_dram = nc.dram_tensor("ht_hi_dram", (NC, P, KD * CH), F32, kind="Internal").ap()
    ht_lo_dram = nc.dram_tensor("ht_lo_dram", (NC, P, KD * CH), F32, kind="Internal").ap()
    q_dram = nc.dram_tensor("q_dram", (NT, P, NQ * P), F32, kind="Internal").ap()
    h1_dram = nc.dram_tensor("h1_dram", (T, D), F32, kind="Internal").ap()
    list_dram = nc.dram_tensor("list_dram", (SLOTS, 1), F32, kind="Internal").ap()
    y_dram = nc.dram_tensor("y_dram", (SLOTS, D), F32, kind="Internal").ap()

    with ExitStack() as whole:
        sb = lambda n, s, d=F32: whole.enter_context(nc.sbuf_tensor(n, s, d))
        ident = sb("ident", [P, P])
        identr = sb("identr", [P, P], F32R)
        logits = sb("logits", [P, NT, RW])
        with ExitStack() as kept:
            sb = lambda n, s, d=F32: kept.enter_context(nc.sbuf_tensor(n, s, d))
            k_hi = sb("k_hi", [P, NKV, T], F32R)
            k_lo = sb("k_lo", [P, NKV, T], F32R)
            v_all = sb("v_all", [P, NT, KVW])
            y_all = sb("y_all", [P, FT, T])
            with nc.sbuf_tensor("x_all", [P, FT, T], F32) as x_all:
                project_lru(nc, x, ln_in_g, ln_in_b, w_in, ident, identr, x_all, y_all, k_hi, k_lo, h_dram,
                            ht_hi_dram, ht_lo_dram)
                project_qkv(nc, w_in, q_norm_g, k_norm_g, rope, identr, ht_hi_dram, ht_lo_dram,
                            k_hi, k_lo, v_all, q_dram)
                lru(nc, conv_w, conv_b, lru_wa, lru_ba, lru_wx, lru_bx, lru_lambda, x_all, y_all)
            attend(nc, w_out, attn_out_g, lru_out_g, ln1_g, ln1_b, router_wg, router_bg, router_we,
                   router_be, ident, k_hi, k_lo, v_all, y_all, h_dram, q_dram, h1_dram, logits)
        sb = lambda n, s, d=F32: whole.enter_context(nc.sbuf_tensor(n, s, d))
        slots = sb("slots", [P, 2, NT], U32)
        weights = sb("weights", [P, 2, NT])
        lists = sb("lists", [P, MT + 2], U32)
        tile_expert = sb("tile_expert", [P, MT], I32)
        split_at = sb("split_at", [P, MT], I32)
        pair_live = sb("pair_live", [P, MT // 2], I32)
        last_tile = sb("last_tile", [P, 1], I32)
        tables = (lists, tile_expert, split_at, pair_live, last_tile)
        route(nc, ident, logits, list_dram, slots, weights, *tables)
        experts(nc, exp_w1, exp_w3, exp_w2, ident, *tables, h1_dram, y_dram)
        combine(nc, ln2_g[0], ln2_b[0], slots, weights, h1_dram, y_dram, out)


@contextmanager
def semaphores(nc, prefix):
    held = []

    def sem(name):
        held.append(nc.alloc_semaphore(prefix + name))
        return held[-1]

    yield sem
    nc.clear_and_free_semaphores(held)
    nc.all_engine_barrier()


def row(ap, n):
    return ap.rearrange("(o n) -> o n", o=1).broadcast_to([P, n])


def run_chunks(eng, ln, transpose, project):
    ln(0, 0)
    transpose(0, 0)
    ln(1, 1)
    with eng.Fori(0, (NC - 2) // 2) as n:
        for u in range(2):
            c = 2 * n + u
            transpose(c + 1, 1 - u)
            project(c, u, 0)
            ln(c + 2, u)
            project(c, u, 1)
    transpose(NC - 1, 1)
    for u in range(2):
        project(NC - 2 + u, u, 0)
        project(NC - 2 + u, u, 1)


def project_lru(nc, x, ln_g, ln_b, w_in, ident, identr, x_all, y_all, k_hi, k_lo, h_dram,
                ht_hi_dram, ht_lo_dram):
    with ExitStack() as ctx:
        sb = lambda n, s, d=F32: ctx.enter_context(nc.sbuf_tensor(n, s, d))
        ps = lambda n, s, d=F32: ctx.enter_context(nc.psum_tensor(n, s, d))
        sem = ctx.enter_context(semaphores(nc, "a_"))
        NF = 2 * FT
        w_hi = sb("wl_hi", [P, KD, NF * P], F32R)
        w_lo = sb("wl_lo", [P, KD, NF * P], F32R)
        raw = x_all[:].rearrange("p f t -> p (f t)").rearrange("p (k n) -> p k n", k=KD)
        g_b = sb("ln_in_g_b", [P, D])
        b_b = sb("ln_in_b_b", [P, D])
        xt = [sb(f"xt{j}", [P, D]) for j in range(2)]
        ht = [sb(f"ht{j}", [P, D]) for j in range(2)]
        t_hi = [k_hi[:, u, :].rearrange("p (k n) -> p k n", k=KD) for u in range(2)]
        t_lo = [k_lo[:, u, :].rearrange("p (k n) -> p k n", k=KD) for u in range(2)]
        stats = sb("stats", [P, 12])
        mv = sb("mv", [P, 2])
        var = sb("var", [P, 1])
        tmp = sb("tmp", [P, 1])
        rstd = [sb(f"rstd{j}", [P, 1]) for j in range(2)]
        shift = [sb(f"shift{j}", [P, 1]) for j in range(2)]
        tps = [ps(f"tps{j}", [P, KD, P]) for j in range(2)]
        acc = [ps(f"acc{j}", [P, 512]) for j in range(4)]

        go = sem("go_a")
        w_in_sem = sem("w_raw_loaded")
        ln_sem = sem("ln_rows_loaded")
        id_sem = sem("ident_made")
        hi_made = sem("w_hi_made")
        lo_made = sem("w_lo_made")
        x_in = [sem(f"x_tile_loaded{j}") for j in range(2)]
        dve_link = sem("dve_link_a")
        stats_done = sem("stats_done")
        xn_done = sem("normalised")
        hg_done = sem("gain_applied")
        h_done = sem("h_done")
        h_stored = [sem(f"h_stored{j}") for j in range(2)]
        tr_done = sem("h_transposed")
        hi_done = sem("t_hi_done")
        lo_done = sem("t_lo_done")
        t_stored = [sem(f"t_stored{c}") for c in range(2)]
        acc_done = sem("acc_done")
        acc_free = sem("acc_free")
        block = ctx.enter_context(nc.Block())

        @block.sync
        def _(sp):
            sp.sem_inc(go, 1)
            w_rows = w_in[0].rearrange("(k p) n -> p k n", p=P)[:, :, QKVW:QKVW + NF * P]
            for j in range(2):
                sp.dma_start(xt[j][:], x[j * P:(j + 1) * P, :]).then_inc(x_in[j], 16)
            sp.dma_start(g_b[:], row(ln_g, D)).then_inc(ln_sem, 16)
            sp.dma_start(b_b[:], row(ln_b, D)).then_inc(ln_sem, 16)
            for k in range(KD):
                sp.dma_start(raw[:, k, :], w_rows[:, k, :]).then_inc(w_in_sem, 16)
            with sp.Fori(0, NC - 1) as c:
                for j in range(2):
                    sp.wait_ge(hg_done, 2 * c + j + 1)
                    sp.dma_start(xt[j][:], x[bass.ds((2 * c + j + 2) * P, P), :]).then_inc(x_in[j], 16)

        @block.gpsimd
        def _(pool):
            pool.memset(ident[:], 0.0).then_inc(id_sem, 1)
            pool.wait_ge(id_sem, 1)
            pool.affine_select(out=ident[:], in_=ident[:], compare_op=ALU.not_equal, fill=1.0, base=0,
                               pattern=[[-1, P]], channel_multiplier=1).then_inc(id_sem, 1)
            pool.wait_ge(ln_sem, 32)
            with pool.Fori(0, NC) as c:
                for j in range(2):
                    pool.wait_ge(hg_done, 2 * c + j + 1)
                    pool.tensor_tensor(ht[j][:], ht[j][:], b_b[:], ALU.add).then_inc(h_done, 1)

        @block.vector
        def _(dve):
            dve.wait_ge(id_sem, 2)
            dve.tensor_copy(identr[:], ident[:]).then_inc(id_sem, 1)
            dve.wait_ge(ln_sem, 32)
            links = 2 * (4 + RSQRT_LINKS)

            def ln(c, u):
                link = Chain(dve, dve_link, c * links)
                for j in range(2):
                    dve.wait_ge(x_in[j], 16 * c + 16)
                    for half in range(2):
                        link(dve.bn_stats(stats[:, 6 * half:6 * half + 6], xt[j][:, 512 * half:512 * half + 512]))
                    dve.nop(nofuse=True)
                    link(dve.bn_aggr(mv[:], stats[:]))
                    link(dve.tensor_scalar(var[:], mv[:, 1:2], LN_EPS, None, ALU.add))
                    rsqrt(dve, link, var[:], rstd[j][:], tmp[:])
                    dve.tensor_scalar(shift[j][:], mv[:, 0:1], rstd[j][:], -1.0, ALU.mult, ALU.mult)\
                       .then_inc(stats_done, 1)
                assert link.n == links
                for j in range(2):
                    dve.wait_ge(xn_done, 2 * c + j + 1)
                    dve.wait_ge(h_stored[j], 16 * c + 16)
                    dve.wait_ge(tr_done, 2 * c + j + 1)
                    dve.tensor_tensor(ht[j][:], xt[j][:], g_b[:], ALU.mult).then_inc(hg_done, 1)

            def transpose(c, u):
                for j in range(2):
                    dve.wait_ge(hi_done, 2 * c + j + 1)
                    part = slice(j * P, (j + 1) * P)
                    dve.tensor_tensor(t_lo[u][:, :, part], tps[j][:], t_hi[u][:, :, part].bitcast(F32),
                                      ALU.subtract).then_inc(lo_done, 1)

            def project(c, u, half):
                pass

            for k in range(KD):
                dve.wait_ge(hi_made, k + 1)
                dve.tensor_tensor(w_lo[:, k, :], raw[:, k, :], w_hi[:, k, :].bitcast(F32), ALU.subtract)\
                   .then_inc(lo_made, 1)
            run_chunks(dve, ln, transpose, project)

        @block.scalar
        def _(act):
            for j in range(2):
                act.sem_inc(h_stored[j], 16)
                act.sem_inc(t_stored[j], 32)
            for k in range(KD):
                act.wait_ge(w_in_sem, 16 * KD)
                act.activation(w_hi[:, k, :], raw[:, k, :], ACT.Copy).then_inc(hi_made, 1)

            def ln(c, u):
                for j in range(2):
                    act.wait_ge(stats_done, 2 * c + j + 1)
                    act.activation(xt[j][:], xt[j][:], ACT.Identity, bias=shift[j][:], scale=rstd[j][:])\
                       .then_inc(xn_done, 1)

            def transpose(c, u):
                for j in range(2):
                    act.wait_ge(tr_done, 2 * c + j + 3)
                    if j == 0:
                        act.wait_ge(acc_done, NF * c + NF)
                        act.wait_ge(t_stored[u], 32 + 16 * (c - u))
                    act.activation(t_hi[u][:, :, j * P:(j + 1) * P], tps[j][:], ACT.Copy).then_inc(hi_done, 1)
                    act.wait_ge(h_done, 2 * c + j + 1)
                    act.dma_start(h_dram[bass.ds((2 * c + j) * P, P), :], ht[j][:]).then_inc(h_stored[j], 16)
                act.wait_ge(hi_done, 2 * c + 2)
                act.dma_start(ht_hi_dram[bass.ds(c, 1)].rearrange("o p n -> (o p) n"),
                              k_hi[:, u, :].bitcast(F32)).then_inc(t_stored[u], 16)
                act.wait_ge(lo_done, 2 * c + 4)
                act.dma_start(ht_lo_dram[bass.ds(c, 1)].rearrange("o p n -> (o p) n"),
                              k_lo[:, u, :].bitcast(F32)).then_inc(t_stored[u], 16)

            def project(c, u, half):
                for f in range(half * FT, (half + 1) * FT):
                    act.wait_ge(acc_done, 2 * NF + NF * c + f + 1)
                    act.wait_ge(go, 1)
                    dst = x_all if f < FT else y_all
                    act.activation(dst[:, f % FT, bass.ds(c * CH, CH)], acc[f % 4][:, 0:CH], ACT.Copy)\
                       .then_inc(acc_free, 1)

            act.wait_ge(lo_made, KD)
            run_chunks(act, ln, transpose, project)
            for c in range(2):
                act.wait_ge(t_stored[c], 32 + 32 * (NC // 2))
            for j in range(2):
                act.wait_ge(h_stored[j], 16 + 16 * NC)

        @block.tensor
        def _(pe):
            pe.sem_inc(tr_done, 2)
            pe.sem_inc(lo_done, 2)
            pe.sem_inc(acc_done, 2 * NF)
            pe.sem_inc(acc_free, 4)
            pe.wait_ge(id_sem, 3)

            def ln(c, u):
                pass

            def transpose(c, u):
                for j in range(2):
                    pe.wait_ge(h_done, 2 * c + j + 1)
                    pe.wait_ge(lo_done, 2 * c + j + 1)
                    for k in range(KD):
                        last = pe.transpose(tps[j][:, k, :], ht[j][:, k * P:(k + 1) * P], ident[:])
                    last.then_inc(tr_done, 1)

            def project(c, u, half):
                if half == 0:
                    pe.wait_ge(lo_done, 2 * c + 4)
                for f in range(half * FT, (half + 1) * FT):
                    pe.wait_ge(acc_free, NF * c + f + 1)
                    cols = slice(f * P, (f + 1) * P)
                    for k in range(KD):
                        last = three_pass(pe, acc[f % 4][:, 0:CH], (w_hi[:, k, cols], w_lo[:, k, cols]),
                                          (t_hi[u][:, k, :], t_lo[u][:, k, :]), k == 0, k == KD - 1)
                    last.then_inc(acc_done, 1)

            pe.wait_ge(lo_made, KD)
            run_chunks(pe, ln, transpose, project)



def project_qkv(nc, w_in, q_g, k_g, rope, identr, ht_hi_dram, ht_lo_dram, k_hi, k_lo, v_all, q_dram):
    with ExitStack() as ctx:
        sb = lambda n, s, d=F32: ctx.enter_context(nc.sbuf_tensor(n, s, d))
        ps = lambda n, s, d=F32: ctx.enter_context(nc.psum_tensor(n, s, d))
        sem = ctx.enter_context(semaphores(nc, "b_"))
        w_hi = sb("wq_hi", [P, KD, QKVW], F32R)
        w_lo = sb("wq_lo", [P, KD, QKVW], F32R)
        raw = [sb(f"wq_raw{j}", [P, QKVW]) for j in range(2)]
        g_b = sb("qk_g_b", [P, 2, HD])
        tab = sb("rope_tab", [P, TPS, 2, HD])
        c_hi = [sb(f"c_hi{u}", [P, KD, P], F32R) for u in range(2)]
        c_lo = [sb(f"c_lo{u}", [P, KD, P], F32R) for u in range(2)]
        sq = raw[0][:, 0:QKW]
        rb = raw[1][:, 0:QKW]
        ss = sb("ss", [P, NH])
        ms = sb("ms", [P, NH])
        tmp = sb("tmp_qk", [P, NH])
        rs = sb("rs", [P, NH])
        xr = [sb(f"xr{u}", [P, QKW]) for u in range(2)]
        rt = [sb(f"rt{u}", [P, QKW]) for u in range(2)]
        q_st = [sb(f"q_st{u}", [P, NQ, 2, HD], F32R) for u in range(2)]
        k_st = [sb(f"k_st{u}", [P, 2, NKV, 2, HD], F32R) for u in range(2)]
        q_t = sb("q_t", [P, NQ, P], F32R)
        pj = [ps(f"pj{u}", [P, 1024]) for u in range(2)]
        tr = ps("tr", [P, NQ + 2 * NKV, P], F32R)

        go = sem("go_b")
        w_raw = [sem(f"wq_raw_loaded{j}") for j in range(2)]
        rows_in = sem("qk_rows_loaded")
        hi_made = sem("wq_hi_made")
        lo_made = sem("wq_lo_made")
        c_in = [sem(f"chunk_loaded{u}") for u in range(2)]
        dve_link = sem("dve_link_b")
        pj_done = sem("pj_done")
        sq_done = sem("sq_done")
        ss_done = sem("ss_done")
        v_done = sem("v_done")
        xr_done = sem("xr_done")
        xg_done = sem("xg_done")
        a_done = sem("rope_a_done")
        b_done = sem("rope_b_done")
        rt_done = sem("rope_done")
        hi_done = sem("qk_hi_done")
        lo_done = sem("qk_lo_done")
        tr_done = sem("qk_transposed")
        qt_done = sem("q_t_done")
        kt_done = sem("k_t_done")
        q_stored = sem("q_stored")
        block = ctx.enter_context(nc.Block())

        def run_tiles(eng, front, back):
            front(0, 0)
            with eng.Fori(0, NT // 2 - 1) as n:
                for u in range(2):
                    front(2 * n + u + 1, 1 - u)
                    back(2 * n + u, u)
            front(NT - 1, 1)
            back(NT - 2, 0)
            back(NT - 1, 1)

        @block.sync
        def _(sp):
            sp.sem_inc(go, 1)
            w_rows = w_in[0].rearrange("(k p) n -> p k n", p=P)

            def load(n, u):
                for dst, src in ((c_hi, ht_hi_dram), (c_lo, ht_lo_dram)):
                    part = src[bass.ds(n, 1)].rearrange("o p (k t) -> (o p) k t", k=KD)[:, :, u * P:(u + 1) * P]
                    sp.dma_start(dst[u][:].bitcast(F32), part).then_inc(c_in[u], 16)

            for k in range(KD):
                if k >= 2:
                    sp.wait_ge(lo_made, k - 1)
                sp.dma_start(raw[k % 2][:], w_rows[:, k, 0:QKVW]).then_inc(w_raw[k % 2], 16)
                if k == 1:
                    load(0, 0)
                    load(0, 1)
            sp.dma_start(g_b[:, 0, :], row(q_g[0], HD)).then_inc(rows_in, 16)
            sp.dma_start(g_b[:, 1, :], row(k_g[0], HD)).then_inc(rows_in, 16)
            sp.dma_start(tab[:].rearrange("p t c d -> p (t c d)"), rope).then_inc(rows_in, 16)
            with sp.Fori(1, NT // 2) as n:
                for u in range(2):
                    sp.wait_ge(pj_done, 2 * n + u - 1)
                    load(n, u)

        @block.scalar
        def _(act):
            act.sem_inc(q_stored, 16)
            act.sem_inc(v_done, 2)
            act.sem_inc(qt_done, 1)
            for k in range(KD):
                act.wait_ge(w_raw[k % 2], 16 * (k // 2 + 1))
                act.activation(w_hi[:, k, :], raw[k % 2][:], ACT.Copy).then_inc(hi_made, 1)
            act.wait_ge(lo_made, KD)

            def front(t, u):
                act.wait_ge(pj_done, t + 1)
                act.wait_ge(ss_done, t + 1)
                act.activation(sq, pj[u][:, 0:QKW], ACT.Square).then_inc(sq_done, 1)
                act.activation(v_all[:, bass.ds(t, 1), :].rearrange("p o n -> p (o n)"), pj[u][:, QKW:QKVW],
                               ACT.Copy).then_inc(v_done, 1)
                act.wait_ge(rt_done, t + 2)
                act.wait_ge(tr_done, t + 1)
                rows = rt[u][:].rearrange("p (h d) -> p h d", h=NH)
                act.activation(q_st[u][:, :, 0, :], rows[:, 0:NQ, :], ACT.Copy)
                act.activation(k_st[u][:, 0], rows[:, NQ:NH, :].unsqueeze(2).broadcast_to([P, NKV, 2, HD]), ACT.Copy)\
                   .then_inc(hi_done, 1)

            def back(t, u):
                act.wait_ge(tr_done, t + 3)
                act.wait_ge(q_stored, 16 * t + 16)
                act.activation(q_t[:], tr[:, 0:NQ, :].bitcast(F32), ACT.Copy).then_inc(qt_done, 1)
                act.wait_ge(qt_done, t + 2)
                act.dma_start(q_dram[bass.ds(t, 1)].rearrange("o p n -> (o p) n"),
                              q_t[:].rearrange("p h t -> p (h t)").bitcast(F32)).then_inc(q_stored, 16)

            run_tiles(act, front, back)
            act.wait_ge(q_stored, 16 + 16 * NT)

        @block.vector
        def _(dve):
            dve.sem_inc(ss_done, 1)
            dve.sem_inc(xr_done, 2)
            dve.sem_inc(rt_done, 1)
            dve.sem_inc(kt_done, 1)
            for k in range(KD):
                dve.wait_ge(hi_made, k + 1)
                dve.tensor_tensor(w_lo[:, k, :], raw[k % 2][:], w_hi[:, k, :].bitcast(F32), ALU.subtract)\
                   .then_inc(lo_made, 1)
            dve.wait_ge(rows_in, 48)
            links = 1 + RSQRT_LINKS_WIDE

            def front(t, u):
                link = Chain(dve, dve_link, t * links)
                dve.wait_ge(sq_done, t + 1)
                dve.tensor_reduce(ss[:], sq.rearrange("p (h d) -> p h d", h=NH), AX, ALU.add).then_inc(ss_done, 1)
                dve.wait_ge(ss_done, t + 2)
                link(dve.tensor_scalar(ms[:], ss[:], 1.0 / HD, QK_EPS, ALU.mult, ALU.add))
                rsqrt(dve, link, ms[:], rs[:], tmp[:])
                assert link.n == links
                dve.wait_ge(b_done, t + 1)
                dve.wait_ge(v_done, t + 3)
                dve.tensor_tensor(xr[u][:].rearrange("p (h d) -> p h d", h=NH),
                                  pj[u][:, 0:QKW].rearrange("p (h d) -> p h d", h=NH),
                                  rs[:].unsqueeze(2).broadcast_to([P, NH, HD]), ALU.mult).then_inc(xr_done, 1)
                dve.wait_ge(xg_done, t + 1)
                dve.wait_ge(lo_done, t + 1)
                dve.tensor_tensor(rt[u][:].rearrange("p (h d) -> p h d", h=NH),
                                  xr[u][:].rearrange("p (h d) -> p h d", h=NH),
                                  tab[:, bass.ds(t % TPS, 1), 0, :].broadcast_to([P, NH, HD]), ALU.mult).then_inc(a_done, 1)
                dve.wait_ge(a_done, t + 1)
                dve.wait_ge(b_done, t + 3)
                dve.tensor_tensor(rt[u][:], rt[u][:], rb, ALU.add).then_inc(rt_done, 1)

            def back(t, u):
                dve.wait_ge(tr_done, t + 3)
                dve.wait_ge(go, 1)
                dve.tensor_copy(k_hi[:, :, bass.ds(t * P, P)], tr[:, NQ:NQ + NKV, :].bitcast(F32))
                dve.tensor_copy(k_lo[:, :, bass.ds(t * P, P)], tr[:, NQ + NKV:, :].bitcast(F32)).then_inc(kt_done, 1)

            run_tiles(dve, front, back)

        @block.gpsimd
        def _(pool):
            pool.sem_inc(b_done, 2)
            pool.sem_inc(lo_done, 2)
            pool.wait_ge(lo_made, KD)
            pool.wait_ge(rows_in, 48)

            def front(t, u):
                x5 = xr[u][:].rearrange("p (h s f d) -> p h s f d", h=NH, s=2, f=2)
                b5 = rb.rearrange("p (h s f d) -> p h s f d", h=NH, s=2, f=2)
                s5 = tab[:, bass.ds(t % TPS, 1), 1, :].rearrange("p o (s f d) -> p o s f d", s=2, f=2)
                pool.wait_ge(xr_done, t + 3)
                heads = xr[u][:].rearrange("p (h d) -> p h d", h=NH)
                for c, a, b in ((0, 0, NQ), (1, NQ, NH)):
                    last = pool.tensor_tensor(heads[:, a:b], heads[:, a:b],
                                              g_b[:, c:c + 1, :].broadcast_to([P, b - a, HD]), ALU.mult)
                last.then_inc(xg_done, 1)
                pool.wait_ge(xg_done, t + 1)
                pool.wait_ge(rt_done, t + 1)
                pool.wait_ge(go, 1)
                for f in range(2):
                    last = pool.tensor_tensor(b5[:, :, :, f, :], x5[:, :, :, 1 - f, :],
                                              s5[:, :, :, f, :].broadcast_to([P, NH, 2, HD // 4]), ALU.mult)
                last.then_inc(b_done, 1)
                rows = rt[u][:].rearrange("p (h d) -> p h d", h=NH)
                pool.wait_ge(hi_done, t + 1)
                pool.tensor_tensor(q_st[u][:, :, 1, :], rows[:, 0:NQ, :], q_st[u][:, :, 0, :].bitcast(F32), ALU.subtract)
                pool.tensor_tensor(k_st[u][:, 1], rows[:, NQ:NH, :].unsqueeze(2).broadcast_to([P, NKV, 2, HD]),
                                   k_st[u][:, 0].bitcast(F32), ALU.subtract).then_inc(lo_done, 1)

            def back(t, u):
                pass

            run_tiles(pool, front, back)

        @block.tensor
        def _(pe):
            pe.sem_inc(tr_done, 2)
            pe.wait_ge(lo_made, KD)

            def front(t, u):
                pe.wait_ge(c_in[u], 16 * (t - u) + 32)
                pe.wait_ge(v_done, t + 1)
                pe.wait_ge(xr_done, t + 1)
                for a, b in ((0, QW), (QW, QKVW)):
                    for k in range(KD):
                        last = three_pass(pe, pj[u][:, a:b], (c_hi[u][:, k, :], c_lo[u][:, k, :]),
                                          (w_hi[:, k, a:b], w_lo[:, k, a:b]), k == 0, k == KD - 1)
                last.then_inc(pj_done, 1)

            def back(t, u):
                pe.wait_ge(lo_done, t + 3)
                pe.wait_ge(qt_done, t + 1)
                pe.wait_ge(kt_done, t + 1)
                for h in range(NQ):
                    pe.transpose(tr[:, h, :], q_st[u][:, h].rearrange("p c d -> p (c d)"), identr[:])
                for c in range(2):
                    for h in range(NKV):
                        last = pe.transpose(tr[:, NQ + NKV * c + h, :], k_st[u][:, c, h].rearrange("p c d -> p (c d)"),
                                            identr[:])
                last.then_inc(tr_done, 1)

            run_tiles(pe, front, back)


def lru(nc, conv_w, conv_b, lru_wa, lru_ba, lru_wx, lru_bx, lru_lambda, x_all, y_all):
    with ExitStack() as ctx:
        sb = lambda n, s, d=F32: ctx.enter_context(nc.sbuf_tensor(n, s, d))
        sem = ctx.enter_context(semaphores(nc, "c_"))
        UNITS = [(s, f) for s in range(SEQS) for f in range(FT)]
        NG = 4
        gw = sb("gate_w", [P, FT, NG, P])
        gb = sb("gate_b", [P, NG, FT])
        cw = sb("conv_w_t", [P, TAPS, FT])
        cb = sb("conv_b_t", [P, FT])
        lam = sb("lam_t", [P, 2, FT])
        neg = sb("neg_lam", [P, 2, FT])
        mag = sb("abs_lam", [P, 2, FT])
        e = sb("exp_lam", [P, 2, FT])
        z = sb("z_lam", [P, 2, FT])
        z2 = sb("z2_lam", [P, 2, FT])
        ser = sb("series", [P, 2, FT])
        decay = sb("decay", [P, 2, FT])
        ndecay = sb("ndecay", [P, 2, FT])
        xc = [sb(f"xc{u}", [P, SEQ]) for u in range(2)]
        r = [sb(f"r{u}", [P, 2, SEQ]) for u in range(3)]
        i = [sb(f"i{u}", [P, 2, SEQ]) for u in range(3)]
        th = [sb(f"th{u}", [P, 2, SEQ]) for u in range(3)]
        a2 = sb("a2", [P, 2, SEQ])
        gp = ctx.enter_context(nc.psum_tensor("gp", [P, NG, SEQ], F32))

        gw_zero = sem("gate_w_zeroed")
        rows_in = sem("lru_rows_loaded")
        gw_in = sem("gate_w_loaded")
        dve_link = sem("dve_link_c")
        act_link = sem("act_link_c")
        mag_done = sem("abs_lam_done")
        e_done = sem("exp_lam_done")
        decay_done = sem("decay_done")
        xc_done = sem("conv_done")
        gates_done = sem("gates_done")
        sig_done = sem("sigmoids_done")
        th_done = sem("tanh_done")
        a_done = sem("a_done")
        ix_done = sem("ix_done")
        a2_done = sem("a2_done")
        w_done = sem("one_minus_a2_done")
        root_done = sem("root_done")
        scans_done = sem("scans_done")
        sum_done = sem("sum_done")
        gelu_done = sem("gelu_done")
        out_done = sem("lru_done")
        block = ctx.enter_context(nc.Block())

        @block.sync
        def _(sp):
            with nc.allow_non_contiguous_dma("small per-feature vectors"):
                sp.dma_start(lam[:], lru_lambda[0].rearrange("d (f p) -> p d f", p=P)).then_inc(rows_in, 16)
                for w in range(TAPS):
                    sp.dma_start(cw[:, w], conv_w[0, w].rearrange("(f p) -> p f", p=P)).then_inc(rows_in, 16)
                sp.dma_start(cb[:], conv_b[0].rearrange("(f p) -> p f", p=P)).then_inc(rows_in, 16)
                for n, src in enumerate((lru_ba, lru_bx)):
                    for d in range(2):
                        sp.dma_start(gb[:, 2 * d + n], src[0, d].rearrange("h i -> (h i)").rearrange("(f p) -> p f", p=P))\
                          .then_inc(rows_in, 16)
            sp.wait_ge(gw_zero, 1)
            for n, src in enumerate((lru_wa, lru_wx)):
                for d in range(2):
                    for c in range(2):
                        part = src[0, d].rearrange("(f c) i j -> c i f j", c=2)[c]
                        sp.dma_start(gw[c * LHD:(c + 1) * LHD, :, 2 * d + n, c * LHD:(c + 1) * LHD], part)\
                          .then_inc(gw_in, 16)

        def run_units(conv, front, w, back, out):
            conv(0)
            conv(1)
            front(0)
            for n in range(len(UNITS)):
                w(n)
                if n:
                    out(n - 1)
                if n + 1 < len(UNITS):
                    front(n + 1)
                if n + 2 < len(UNITS):
                    conv(n + 2)
                back(n)
            out(len(UNITS) - 1)

        def skip(n):
            pass

        @block.vector
        def _(dve):
            link = Chain(dve, dve_link)
            dve.wait_ge(rows_in, 160)
            link(dve.tensor_scalar(neg[:], lam[:], -1.0, None, ALU.mult))
            dve.tensor_tensor(mag[:], lam[:], neg[:], ALU.max).then_inc(mag_done, 1)
            dve.wait_ge(e_done, 1)
            link(dve.tensor_scalar(z2[:], e[:], 2.0, None, ALU.add))
            link(dve.reciprocal(z2[:], z2[:]))
            link(dve.tensor_tensor(z[:], e[:], z2[:], ALU.mult))
            link(dve.tensor_tensor(z2[:], z[:], z[:], ALU.mult))
            link(dve.tensor_scalar(ser[:], z2[:], 1 / 19, 1 / 17, ALU.mult, ALU.add))
            for odd in range(15, 0, -2):
                link(dve.tensor_tensor(ser[:], ser[:], z2[:], ALU.mult))
                link(dve.tensor_scalar(ser[:], ser[:], 1 / odd, None, ALU.add))
            link(dve.tensor_tensor(ser[:], ser[:], z[:], ALU.mult))
            link(dve.tensor_scalar(neg[:], neg[:], 0.0, LRU_C, ALU.max, ALU.mult))
            link(dve.scalar_tensor_tensor(decay[:], ser[:], 2.0 * LRU_C, neg[:], ALU.mult, ALU.add))
            dve.tensor_scalar(ndecay[:], decay[:], -1.0, None, ALU.mult).then_inc(decay_done, 1)

            def conv(n):
                s, f = UNITS[n]
                c = xc[n % 2]
                xs = x_all[:, f, s * SEQ:(s + 1) * SEQ]
                if n >= 2:
                    dve.wait_ge(ix_done, n - 1)
                    dve.wait_ge(gates_done, NG * (n - 1))
                link(dve.tensor_scalar(c[:], xs, cw[:, 2, f:f + 1], cb[:, f:f + 1], ALU.mult, ALU.add))
                link(dve.scalar_tensor_tensor(c[:, 2:], xs[:, :SEQ - 2], cw[:, 0, f:f + 1], c[:, 2:],
                                              ALU.mult, ALU.add))
                link(dve.scalar_tensor_tensor(c[:, 1:], xs[:, :SEQ - 1], cw[:, 1, f:f + 1], c[:, 1:],
                                              ALU.mult, ALU.add))
                dve.scalar_tensor_tensor(c[:, :SEQ - 1], xs[:, 1:], cw[:, 3, f:f + 1], c[:, :SEQ - 1],
                                         ALU.mult, ALU.add).then_inc(xc_done, 1)

            def w(n):
                u = n % 3
                dve.wait_ge(a2_done, n + 1)
                dve.wait_ge(th_done, 2 * n + 2)
                dve.scalar_tensor_tensor(th[u][:], a2[:], 1.0, th[u][:], ALU.add, ALU.mult).then_inc(w_done, 1)

            def back(n):
                u = n % 3
                dve.wait_ge(root_done, n + 1)
                dve.wait_ge(ix_done, n + 1)
                link(dve.tensor_tensor(i[u][:], i[u][:], th[u][:], ALU.mult))
                dve.tensor_tensor_scan(i[u][:, 0], r[u][:, 0], i[u][:, 0], 0.0, ALU.mult, ALU.add)
                dve.tensor_tensor_scan(i[u][:, 1, ::-1], r[u][:, 1, ::-1], i[u][:, 1, ::-1], 0.0, ALU.mult, ALU.add)\
                   .then_inc(scans_done, 1)

            def out(n):
                s, f = UNITS[n]
                ys = y_all[:, f, s * SEQ:(s + 1) * SEQ]
                dve.wait_ge(sum_done, n + 1)
                dve.wait_ge(gelu_done, 1)
                dve.tensor_tensor(ys, ys, i[n % 3][:, 0], ALU.mult).then_inc(out_done, 1)

            run_units(conv, skip, w, back, out)

        @block.gpsimd
        def _(pool):
            pool.memset(gw[:], 0.0).then_inc(gw_zero, 1)

            def front(n):
                u = n % 3
                pool.wait_ge(a_done, n + 1)
                if n:
                    pool.wait_ge(w_done, n)
                pool.tensor_tensor(a2[:], r[u][:], r[u][:], ALU.mult).then_inc(a2_done, 1)
                pool.wait_ge(sig_done, NG * n + NG)
                pool.wait_ge(xc_done, n + 1)
                for d in range(2):
                    last = pool.tensor_tensor(i[u][:, d], i[u][:, d], xc[n % 2][:], ALU.mult)
                last.then_inc(ix_done, 1)

            def back(n):
                u = n % 3
                pool.wait_ge(scans_done, n + 1)
                pool.tensor_tensor(i[u][:, 0], i[u][:, 0], i[u][:, 1], ALU.add).then_inc(sum_done, 1)

            run_units(skip, front, skip, back, skip)

        @block.scalar
        def _(act):
            act.wait_ge(mag_done, 1)
            act.activation(e[:], mag[:], ACT.Exp, scale=-1.0).then_inc(e_done, 1)
            act.activation(y_all[:], y_all[:], ACT.Gelu_apprx_tanh).then_inc(gelu_done, 1)
            act.wait_ge(decay_done, 1)

            def front(n):
                s, f = UNITS[n]
                u = n % 3
                if n >= 3:
                    act.wait_ge(out_done, n - 2)
                for g in range(NG):
                    act.wait_ge(gates_done, NG * n + g + 1)
                    dst = (r, i)[g % 2][u][:, g // 2]
                    act.activation(dst, gp[:, g], ACT.Sigmoid, bias=gb[:, g, f:f + 1]).then_inc(sig_done, 1)
                act.wait_ge(sig_done, NG * n + NG)
                for d in range(2):
                    act.activation(th[u][:, d], r[u][:, d], ACT.Tanh, scale=decay[:, d, f:f + 1]).then_inc(th_done, 1)
                act.wait_ge(th_done, 2 * n + 2)
                for d in range(2):
                    last = act.activation(r[u][:, d], r[u][:, d], ACT.Exp, scale=ndecay[:, d, f:f + 1])
                last.then_inc(a_done, 1)

            def back(n):
                act.wait_ge(w_done, n + 1)
                act.activation(th[n % 3][:], th[n % 3][:], ACT.Sqrt).then_inc(root_done, 1)

            run_units(skip, front, skip, back, skip)

        @block.tensor
        def _(pe):
            pe.wait_ge(gw_in, 128)

            def front(n):
                s, f = UNITS[n]
                u = n % 2
                pe.wait_ge(xc_done, n + 1)
                for g in range(NG):
                    if n:
                        pe.wait_ge(sig_done, NG * (n - 1) + g + 1)
                    for c in range(2):
                        last = pe.matmul(gp[:, g, c * 512:(c + 1) * 512], gw[:, f, g, :], xc[u][:, c * 512:(c + 1) * 512],
                                         start=True, stop=True)
                    last.then_inc(gates_done, 1)

            run_units(skip, front, skip, skip, skip)


def need(eng, sem, value):
    if not (isinstance(value, int) and value < 1):
        eng.wait_ge(sem, value)


def attend(nc, w_out, attn_g, lru_g, ln_g, ln_b, router_wg, router_bg, router_we, router_be, ident,
           k_hi, k_lo, v_all, y_all, h_dram, q_dram, h1_dram, logits):
    with ExitStack() as ctx:
        sb = lambda n, s, d=F32: ctx.enter_context(nc.sbuf_tensor("d_" + n, s, d))
        ps = lambda n, s, d=F32: ctx.enter_context(nc.psum_tensor("d_" + n, s, d))
        sem = ctx.enter_context(semaphores(nc, "d_"))
        GQ = NQ // NKV
        HALF = TPS // 2
        w_hi = sb("wo_hi", [P, KD, D], F32R)
        w_lo = sb("wo_lo", [P, KD, D], F32R)
        out_g = sb("out_g", [P, KD])
        g_b = sb("ln1_g_b", [P, D])
        b_b = sb("ln1_b_b", [P, D])
        wr = sb("router_w", [P, KD, RW])
        rb_b = sb("router_b", [P, RW])
        ones = sb("ones", [P, 2])
        q_t = [sb(f"q_tile{u}", [P, NQ, P], F32R) for u in range(2)]
        pr = [sb(f"probs{j}", [P, SEQ]) for j in range(2)]
        pt = [sb(f"probs_t{j}", [P, TPS, P]) for j in range(2)]
        mx = sb("mx", [P, 2, NQ])
        nm = sb("neg_max", [P, 2, NQ])
        rsum = sb("rsum", [P, 2, NQ])
        rinv = sb("rinv", [P, NQ])
        o_n = sb("o_n", [P, QW])
        junk = sb("junk", [P, QW])
        m_hi = sb("m_hi", [P, KD, P], F32R)
        m_lo = sb("m_lo", [P, KD, P], F32R)
        lsq = [sb(f"lru_sq{u}", [P, FT, P]) for u in range(2)]
        lvar = sb("lru_var", [P, NT])
        lrstd = sb("lru_rstd", [P, NT])
        ltmp = sb("lru_tmp", [P, NT])
        ssa = sb("ssa", [P, 1])
        var = sb("var_a", [P, 1])
        rr = sb("rstds", [P, 2])
        tmp2 = sb("tmp_a", [P, 1])
        hb = sb("h_tile", [P, D])
        s_t = sb("s_tile", [P, D])
        h1 = sb("h1_tile", [P, D])
        h1t = sb("h1_t", [P, KD, P])
        stats = sb("stats1", [P, 12])
        mv = sb("mv1", [P, 2])
        var1 = sb("var1", [P, 1])
        tmp1 = sb("tmp1", [P, 1])
        rstd1 = sb("rstd1", [P, 1])
        shift1 = sb("shift1", [P, 1])
        raw = [s_t, h1]
        s_ps = [ps(f"s_ps{j}", [P, SEQ]) for j in range(2)]
        pt_ps = [ps(f"pt_ps{c}", [P, HALF, P]) for c in range(2)]
        o_ps = ps("o_ps", [P, QW])
        m_ps = ps("m_ps", [P, 512])

        rows_in = sem("rows_loaded_d")
        raw_in = [sem(f"wo_raw_loaded{j}") for j in range(2)]
        ones_made = sem("ones_made")
        act_link = sem("act_link_d")
        dve_link = sem("dve_link_d")
        hi_made = sem("wo_hi_made")
        lo_made = sem("wo_lo_made")
        q_in = [sem(f"q_loaded{u}") for u in range(2)]
        s_done = sem("scores_done")
        mx_done = sem("max_done")
        nm_done = sem("neg_max_done")
        p_done = sem("probs_done")
        tr_done = [sem(f"probs_transposed{c}") for c in range(2)]
        pt_done = [sem(f"probs_t_done{c}") for c in range(2)]
        o_done = sem("o_done")
        rinv_done = sem("rinv_done")
        on_done = sem("o_norm_done")
        ssa_done = sem("ssa_done")
        m_done = sem("m_bank_written")
        m_free = sem("m_bank_read")
        late_done = sem("m_bank_written_late")
        late_free = sem("m_bank_read_late")
        mh_done = sem("m_hi_done")
        lh_done = sem("lru_hi_done")
        ll_done = sem("lru_lo_done")
        lsq_done = sem("lru_sq_done")
        lss_done = sem("lru_sq_summed")
        lr_link = sem("lru_rstd_link")
        h_in = sem("h_loaded")
        ah_done = sem("alpha_h_done")
        ln_done = sem("ln1_stats_done")
        xn_done = sem("ln1_normalised")
        hg_done = sem("ln1_gain_done")
        h1_done = sem("h1_done")
        h1_stored = sem("h1_stored")
        USES = 5
        LATE = 3
        block = ctx.enter_context(nc.Block())

        def run_heads(eng, first, head, post, late):
            def tile(t, u, stage=2, is_last=False):
                for h in range(NQ):
                    nxt = [(t, u, i) if i < NQ else None if is_last else (t + 1, 1 - u, i - NQ) for i in (h + 1, h + 2)]
                    head(t, u, h, nxt, stage)
                    if stage == 2 and h < LATE:
                        late(t - 2, h, False)

            first()
            tile(0, 0, stage=0)
            tile(1, 1, stage=1)
            with eng.Fori(1, NT // 2 - 1) as n:
                tile(2 * n, 0)
                tile(2 * n + 1, 1)
            tile(NT - 2, 0)
            tile(NT - 1, 1, is_last=True)
            for step in range(-1, NQ):
                post(NT - 1, 1, step)
                if step in range(LATE):
                    late(NT - 2, step, False)
            for step in range(LATE):
                late(NT - 1, step, True)

        @block.sync
        def _(sp):
            def load_q(t, u):
                sp.dma_start(q_t[u][:].rearrange("p h t -> p (h t)").bitcast(F32),
                             q_dram[bass.ds(t, 1)].rearrange("o p n -> (o p) n")).then_inc(q_in[u], 16)

            def load_h(t):
                sp.dma_start(hb[:], h_dram[bass.ds(t * P, P), :]).then_inc(h_in, 16)

            def store_h1(t):
                sp.wait_ge(h1_done, 2 * t + 2)
                sp.dma_start(h1_dram[bass.ds(t * P, P), :], h1[:]).then_inc(h1_stored, 16)

            sp.sem_inc(h1_stored, 16)
            load_q(0, 0)
            load_q(1, 1)
            load_h(0)
            with nc.allow_non_contiguous_dma("small per-feature vectors and router columns"):
                sp.dma_start(out_g[:, 0:FT], attn_g[0].rearrange("(f p) -> p f", p=P)).then_inc(rows_in, 16)
                sp.dma_start(out_g[:, FT:KD], lru_g[0].rearrange("(f p) -> p f", p=P)).then_inc(rows_in, 16)
                sp.dma_start(wr[:, :, 0:G], router_wg[0].rearrange("(k p) g -> p k g", p=P)).then_inc(rows_in, 16)
                sp.dma_start(wr[:, :, G:RW], router_we[0].rearrange("(k p) g e -> p k (g e)", p=P)).then_inc(rows_in, 16)
            sp.dma_start(rb_b[:, 0:G], row(router_bg[0], G)).then_inc(rows_in, 16)
            sp.dma_start(rb_b[:, G:RW], row(router_be[0].rearrange("g e -> (g e)"), NE)).then_inc(rows_in, 16)
            sp.dma_start(g_b[:], row(ln_g[0], D)).then_inc(rows_in, 16)
            sp.dma_start(b_b[:], row(ln_b[0], D)).then_inc(rows_in, 16)
            for k in range(KD):
                need(sp, lo_made, k - 1)
                sp.dma_start(raw[k % 2][:], w_out[0, k * P:(k + 1) * P, :]).then_inc(raw_in[k % 2], 16)

            def during(t, u):
                if u is not None:
                    sp.wait_ge(s_done, NQ * t)
                    load_q(t + 1, u)
                sp.wait_ge(m_free, USES * (t - 1) + 5)
                load_h(t)
                store_h1(t - 1)

            with sp.Fori(0, NT // 2 - 1) as n:
                during(2 * n + 1, 0)
                during(2 * n + 2, 1)
            during(NT - 1, None)
            store_h1(NT - 1)
            sp.wait_ge(h1_stored, 16 * NT + 16)

        @block.tensor
        def _(pe):
            pe.wait_ge(ones_made, 1)
            pe.sem_inc(m_done, 1)

            def scores(t, u, h):
                n = NQ * t + h
                if h == 0:
                    pe.wait_ge(q_in[u], 8 * (t - u) + 16)
                for c in range(2):
                    out = s_ps[h % 2][:, c * 512:(c + 1) * 512]
                    keys = bass.ds((t // TPS) * SEQ + c * 512, 512)
                    pe.matmul(out, q_t[u][:, h, :], k_hi[:, h // GQ, keys], start=True, stop=False)
                    last = pe.matmul(out, q_t[u][:, h, :], k_lo[:, h // GQ, keys], start=False, stop=True)
                last.then_inc(s_done, 1)

            def head(t, u, h, nxt, stage):
                n = NQ * t + h
                pe.wait_ge(p_done, n + 1)
                for c in range(2):
                    need(pe, pt_done[c], n)
                    for j in range(HALF):
                        k = c * HALF + j
                        last = pe.transpose(pt_ps[c][:, j, :], pr[h % 2][:, k * P:(k + 1) * P], ident[:])
                    last.then_inc(tr_done[c], 1)
                if nxt[1]:
                    scores(*nxt[1])
                if stage == 0:
                    for tt in (2 * h, 2 * h + 1):
                        pe.wait_ge(lsq_done, tt + 1)
                        for k in range(FT):
                            last = pe.matmul(m_ps[:, tt:tt + 1], lsq[tt % 2][:, k, :], ones[:, 0:1], start=k == 0, stop=k == FT - 1)
                        last.then_inc(lss_done, 1)
                else:
                    post(t - 1, 1 - u, h)
                if h == 0:
                    need(pe, on_done, t)
                for k in range(TPS):
                    if k % HALF == 0:
                        pe.wait_ge(pt_done[k // HALF], n + 1)
                    v_rows = v_all[:, bass.ds((t // TPS) * TPS + k, 1), (h // GQ) * HD:(h // GQ + 1) * HD]
                    last = pe.matmul(o_ps[:, h * HD:(h + 1) * HD], pt[h % 2][:, k, :],
                                     v_rows.rearrange("p o d -> p (o d)"), start=k == 0, stop=k == TPS - 1)
                last.then_inc(o_done, 1)

            def project(first_k, half):
                for k in range(FT):
                    kk = first_k + k
                    cols = slice(half * 512, (half + 1) * 512)
                    last = three_pass(pe, m_ps[:], (m_hi[:, kk, :], m_lo[:, kk, :]),
                                      (w_hi[:, kk, cols], w_lo[:, kk, cols]), k == 0, k == FT - 1)
                last.then_inc(m_done, 1)

            def post(t, u, step):
                use = USES * t + 1
                if step == 0:
                    pe.wait_ge(on_done, t + 1)
                    for k in range(FT):
                        last = pe.transpose(m_ps[:, k * P:(k + 1) * P], o_n[:, k * P:(k + 1) * P], ident[:])
                    last.then_inc(m_done, 1)
                if step in (1, 2, 3) and not (isinstance(t, int) and t == 0):
                    pe.wait_ge(late_free, LATE * (t - 1) + step)
                if step == 1:
                    pe.wait_ge(lo_made, KD)
                    pe.wait_ge(m_free, use + 1)
                    project(0, 0)
                if step == 2:
                    pe.wait_ge(ll_done, t + 1)
                    pe.wait_ge(m_free, use + 2)
                    project(FT, 0)
                if step == 3:
                    pe.wait_ge(m_free, use + 3)
                    project(0, 1)
                if step == 4:
                    pe.wait_ge(m_free, use + 4)
                    project(FT, 1)
            def late(t, step, alone):
                pe.wait_ge(m_free, USES * (t + 1) + 1 + (0 if alone else step + 1))
                if step > 0:
                    pe.wait_ge(late_free, LATE * t + step)
                if step < 2:
                    pe.wait_ge(h1_done, 2 * t + step + 1)
                    for j in range(FT):
                        k = step * FT + j
                        last = pe.transpose(m_ps[:, j * P:(j + 1) * P], h1[:, k * P:(k + 1) * P], ident[:])
                else:
                    for k in range(KD):
                        last = pe.matmul(m_ps[:, 0:RW], h1t[:, k, :], wr[:, k, :], start=k == 0, stop=k == KD - 1)
                last.then_inc(late_done, 1)

            pe.wait_ge(rows_in, 128)
            run_heads(pe, lambda: (scores(0, 0, 0), scores(0, 0, 1)), head, post, late)

        @block.scalar
        def _(act):
            def exp(t, u, h):
                n = NQ * t + h
                act.wait_ge(nm_done, n + 1)
                need(act, tr_done[1], n - 1)
                act.activation(pr[h % 2][:], s_ps[h % 2][:], ACT.Exp, bias=nm[:, u, h:h + 1], scale=SCALE,
                               accum_out=rsum[:, u, h:h + 1]).then_inc(p_done, 1)

            def head(t, u, h, nxt, stage):
                n = NQ * t + h
                act.wait_ge(tr_done[0], n + 1)
                need(act, o_done, n - 1)
                act.activation(pt[h % 2][:, 0:HALF], pt_ps[0][:], ACT.Copy).then_inc(pt_done[0], 1)
                if nxt[0]:
                    exp(*nxt[0])
                if stage == 0:
                    act.wait_ge(raw_in[h % 2], 16 * (h // 2 + 1))
                    act.wait_ge(rows_in, 128)
                    act.activation(raw[h % 2][:], raw[h % 2][:], ACT.Copy, scale=out_g[:, h:h + 1]).then_inc(act_link, 1)
                    act.wait_ge(act_link, h + 1)
                    act.activation(w_hi[:, h, :], raw[h % 2][:], ACT.Copy).then_inc(hi_made, 1)
                else:
                    post(t - 1, 1 - u, h)

            def post(t, u, step):
                use = USES * t + 1
                if step == 0:
                    act.wait_ge(on_done, t + 1)
                    act.activation(junk[:], o_n[:], ACT.Square, accum_out=ssa[:]).then_inc(ssa_done, 1)
                    act.wait_ge(m_done, use + 1)
                    act.activation(m_hi[:, 0:FT], m_ps[:].rearrange("p (k t) -> p k t", k=FT), ACT.Copy)\
                       .then_inc(mh_done, 1)
                    act.activation(m_hi[:, FT:KD], y_all[:, :, bass.ds(t * P, P)], ACT.Copy).then_inc(lh_done, 1)
                    act.wait_ge(h_in, 16 * t + 16)
                    act.activation(hb[:], hb[:], ACT.Copy, scale=ALPHA).then_inc(ah_done, 1)
                if step == 6:
                    act.wait_ge(ln_done, t + 1)
                    act.activation(s_t[:], s_t[:], ACT.Identity, bias=shift1[:], scale=rstd1[:]).then_inc(xn_done, 1)

            def late(t, step, alone):
                if step < 2:
                    act.wait_ge(late_done, LATE * t + step + 1)
                    act.activation(h1t[:, step * FT:(step + 1) * FT], m_ps[:].rearrange("p (k t) -> p k t", k=FT),
                                   ACT.Copy).then_inc(late_free, 1)

            run_heads(act, lambda: exp(0, 0, 0), head, post, late)

        @block.vector
        def _(dve):
            dve.memset(ones[:], 1.0).then_inc(ones_made, 1)
            links = (2 + RSQRT_LINKS) + (4 + RSQRT_LINKS)

            def neg_max(t, u, h):
                n = NQ * t + h
                dve.wait_ge(s_done, n + 1)
                dve.tensor_reduce(mx[:, u, h:h + 1], s_ps[h % 2][:], AX, ALU.max).then_inc(mx_done, 1)
                dve.wait_ge(mx_done, n + 1)
                dve.tensor_scalar(nm[:, u, h:h + 1], mx[:, u, h:h + 1], -SCALE, None, ALU.mult).then_inc(nm_done, 1)

            def head(t, u, h, nxt, stage):
                n = NQ * t + h
                if h == 0 and stage > 0:
                    post(t - 1, 1 - u, -1)
                dve.wait_ge(tr_done[1], n + 1)
                need(dve, o_done, n - 1)
                dve.tensor_copy(pt[h % 2][:, HALF:], pt_ps[1][:]).then_inc(pt_done[1], 1)
                if nxt[1]:
                    neg_max(*nxt[1])
                if stage == 0:
                    dve.wait_ge(hi_made, h + 1)
                    dve.tensor_tensor(w_lo[:, h, :], raw[h % 2][:], w_hi[:, h, :].bitcast(F32), ALU.subtract)\
                       .then_inc(lo_made, 1)
                    if h == NQ - 1:
                        link = Chain(dve, lr_link)
                        dve.wait_ge(lss_done, NT)
                        dve.tensor_scalar(lvar[:], m_ps[:, 0:NT], 1.0 / LW, LN_EPS, ALU.mult, ALU.add).then_inc(m_free, 1)
                        dve.wait_ge(m_free, 1)
                        rsqrt(dve, link, lvar[:], lrstd[:], ltmp[:])
                else:
                    post(t - 1, 1 - u, h)

            def post(t, u, step):
                use = USES * t + 1
                if step == -1:
                    dve.wait_ge(o_done, NQ * t + NQ)
                    dve.wait_ge(p_done, NQ * t + NQ)
                    dve.reciprocal(rinv[:], rsum[:, u]).then_inc(rinv_done, 1)
                    dve.wait_ge(rinv_done, t + 1)
                    dve.tensor_tensor(o_n[:].rearrange("p (h d) -> p h d", h=NQ),
                                      o_ps[:].rearrange("p (h d) -> p h d", h=NQ),
                                      rinv[:].unsqueeze(2).broadcast_to([P, NQ, HD]), ALU.mult).then_inc(on_done, 1)
                if step == 0:
                    dve.wait_ge(lh_done, t + 1)
                    dve.nop(nofuse=True)
                    dve.tensor_tensor(m_lo[:, FT:KD], y_all[:, :, bass.ds(t * P, P)], m_hi[:, FT:KD].bitcast(F32),
                                      ALU.subtract).then_inc(ll_done, 1)
                    dve.wait_ge(mh_done, t + 1)
                    dve.tensor_tensor(m_lo[:, 0:FT], m_ps[:].rearrange("p (k t) -> p k t", k=FT),
                                      m_hi[:, 0:FT].bitcast(F32), ALU.subtract).then_inc(m_free, 1)
                if step == 1:
                    link = Chain(dve, dve_link, links * t)
                    dve.wait_ge(ssa_done, t + 1)
                    dve.nop(nofuse=True)
                    link(dve.tensor_copy(rr[:, 1:2], lrstd[:, bass.ds(t, 1)]))
                    link(dve.tensor_scalar(var[:], ssa[:], 1.0 / QW, LN_EPS, ALU.mult, ALU.add))
                    rsqrt(dve, link, var[:], rr[:, 0:1], tmp2[:])
                    dve.wait_ge(m_done, use + 2)
                    dve.wait_ge(ah_done, t + 1)
                    dve.scalar_tensor_tensor(s_t[:, 0:512], m_ps[:], rr[:, 0:1], hb[:, 0:512], ALU.mult, ALU.add)\
                       .then_inc(m_free, 1)
                if step == 2:
                    dve.wait_ge(m_done, use + 3)
                    dve.wait_ge(m_free, use + 2)
                    dve.scalar_tensor_tensor(s_t[:, 0:512], m_ps[:], rr[:, 1:2], s_t[:, 0:512], ALU.mult, ALU.add)\
                       .then_inc(m_free, 1)
                if step == 3:
                    dve.wait_ge(m_done, use + 4)
                    dve.scalar_tensor_tensor(s_t[:, 512:], m_ps[:], rr[:, 0:1], hb[:, 512:], ALU.mult, ALU.add)\
                       .then_inc(m_free, 1)
                if step == 4:
                    link = Chain(dve, dve_link, links * t + 2 + RSQRT_LINKS)
                    dve.wait_ge(m_done, use + 5)
                    dve.wait_ge(m_free, use + 4)
                    dve.scalar_tensor_tensor(s_t[:, 512:], m_ps[:], rr[:, 1:2], s_t[:, 512:], ALU.mult, ALU.add)\
                       .then_inc(m_free, 1)
                    dve.wait_ge(m_free, use + 5)
                    for half in range(2):
                        link(dve.bn_stats(stats[:, 6 * half:6 * half + 6], s_t[:, 512 * half:512 * half + 512]))
                if step == 5:
                    link = Chain(dve, dve_link, links * t + 4 + RSQRT_LINKS)
                    dve.nop(nofuse=True)
                    link(dve.bn_aggr(mv[:], stats[:]))
                    link(dve.tensor_scalar(var1[:], mv[:, 1:2], LN_EPS, None, ALU.add))
                    rsqrt(dve, link, var1[:], rstd1[:], tmp1[:])
                    dve.tensor_scalar(shift1[:], mv[:, 0:1], rstd1[:], -1.0, ALU.mult, ALU.mult).then_inc(ln_done, 1)
                if step == 7:
                    dve.wait_ge(xn_done, t + 1)
                    dve.wait_ge(h1_stored, 16 * t + 16)
                    if not (isinstance(t, int) and t == 0):
                        dve.wait_ge(late_done, LATE * (t - 1) + 2)
                    for half in range(2):
                        part = slice(half * 512, (half + 1) * 512)
                        dve.tensor_tensor(h1[:, part], s_t[:, part], g_b[:, part], ALU.mult).then_inc(hg_done, 1)

            def late(t, step, alone):
                if step == 2:
                    dve.wait_ge(late_done, LATE * t + 3)
                    dve.nop(nofuse=True)
                    dve.tensor_tensor(logits[:, bass.ds(t, 1), :].rearrange("p o n -> p (o n)"), m_ps[:, 0:RW], rb_b[:],
                                      ALU.add).then_inc(late_free, 1)

            run_heads(dve, lambda: (neg_max(0, 0, 0), neg_max(0, 0, 1)), head, post, late)

        @block.gpsimd
        def _(pool):
            for t in range(NT):
                need(pool, lss_done, t - 1)
                part = y_all[:, :, t * P:(t + 1) * P]
                pool.tensor_tensor(lsq[t % 2][:], part, part, ALU.mult).then_inc(lsq_done, 1)
            pool.wait_ge(rows_in, 128)
            with pool.Fori(0, NT) as t:
                for half in range(2):
                    part = slice(half * 512, (half + 1) * 512)
                    pool.wait_ge(hg_done, 2 * t + half + 1)
                    pool.tensor_tensor(h1[:, part], h1[:, part], b_b[:, part], ALU.add).then_inc(h1_done, 1)


def route(nc, ident, logits, list_dram, slots, weights, lists, tile_expert, split_at, pair_live, last_tile):
    with ExitStack() as ctx:
        sb = lambda n, s, d=F32: ctx.enter_context(nc.sbuf_tensor("r_" + n, s, d))
        sem = ctx.enter_context(semaphores(nc, "r_"))
        gl = logits[:, :, 0:G]
        el = logits[:, :, G:RW].rearrange("p t (g e) -> p t g e", g=G)
        top = sb("top", [P, NT])
        gd = sb("gd", [P, NT, G])
        ge = sb("ge", [P, NT, G])
        gsum = sb("gsum", [P, NT])
        gprob = sb("gprob", [P, NT])
        eq = sb("eq", [P, NT, G])
        seen = sb("seen", [P, NT])
        oh_g = sb("oh_g", [P, NT, G])
        oh_e = [sb(f"oh_e{c}", [P, NT, E_IN_G]) for c in range(2)]
        prod = sb("prod", [P, NT, G, E_IN_G])
        es = sb("es", [P, NT, E_IN_G])
        m1 = sb("m1", [P, NT])
        m2 = sb("m2", [P, NT])
        gap = sb("gap", [P, NT])
        x2 = sb("x2", [P, NT])
        hot = [sb(f"hot{c}", [P, NT, G, E_IN_G]) for c in range(2)]
        both = sb("both", [P, NT, NE])
        tri = sb("tri", [P, P])
        ones = sb("ones", [P, P])
        offs = sb("offs", [P, NT + 1, NE])
        thr_i = sb("thr_i", [P, NT], I32)
        thr = sb("thr", [P, NT])
        over = sb("over", [P, NE, NT])
        n_tiles = sb("n_tiles", [P, NE])
        upto = sb("upto", [P, NE])
        first_tile = sb("first_tile", [P, NE])
        start = sb("start", [P, NE])
        base = sb("base", [P, NT, NE])
        slot_f = sb("slot_f", [P, 2, NT])
        tile_i = sb("tile_i", [P, MT], I32)
        tile_f = sb("tile_f", [P, MT])
        past = sb("past", [P, MT, NE])
        splits = sb("splits", [P, MT])
        live = sb("live", [P, MT // 2])
        last_f = sb("last_f", [P, 1])
        exp_f = sb("exp_f", [P, MT])
        tok_i = sb("tok_i", [P, NT], I32)
        tok = sb("tok", [P, NT])
        zero = sb("zero", [MT, P])
        rows = sb("rows", [MT, P])
        rank_ps = ctx.enter_context(nc.psum_tensor("rank_ps", [P, NT * NE], F32))
        tot_ps = ctx.enter_context(nc.psum_tensor("tot_ps", [P, NT * NE], F32))
        list_ps = ctx.enter_context(nc.psum_tensor("list_ps", [P, MT], F32))

        dve_link = sem("dve_link")
        pool_link = sem("pool_link")
        made = sem("constants_made")
        gd_done = sem("gd_done")
        ge_done = sem("ge_done")
        gap_done = sem("gap_done")
        x2_done = sem("x2_done")
        both_done = sem("both_done")
        counted = sem("counted")
        slots_done = sem("slots_done")
        zeroed = sem("list_zeroed")
        scattered = sem("list_scattered")
        rows_in = sem("list_loaded")
        turned = sem("list_transposed")
        block = ctx.enter_context(nc.Block())

        @block.gpsimd
        def _(pool):
            link = Chain(pool, pool_link)
            pool.memset(zero[:], 0.0).then_inc(made, 1)
            pool.memset(ones[:], 1.0).then_inc(made, 1)
            pool.iota(thr_i[:], [[P, NT]], base=0, channel_multiplier=0).then_inc(made, 1)
            pool.iota(tile_i[:], [[1, MT]], base=0, channel_multiplier=0).then_inc(made, 1)
            pool.iota(tok_i[:], [[P, NT]], base=0, channel_multiplier=1).then_inc(made, 1)
            link(pool.memset(tri[:], 1.0))
            pool.affine_select(out=tri[:], in_=tri[:], compare_op=ALU.is_gt, fill=0.0, base=0,
                               pattern=[[1, P]], channel_multiplier=-1).then_inc(made, 1)
            pool.wait_ge(zeroed, 16)
            pool.wait_ge(slots_done, 1)
            for c in range(2):
                for t in range(NT):
                    pool.indirect_dma_start(list_dram, bass.IndirectOffsetOnAxis(slots[:, c, t:t + 1], 0),
                                            tok[:, t:t + 1], None).then_inc(scattered, 16)

        @block.sync
        def _(sp):
            list_rows = list_dram.rearrange("(j p) o -> j (p o)", p=P)
            sp.wait_ge(made, 1)
            sp.dma_start(list_rows, zero[:]).then_inc(zeroed, 16)
            sp.wait_ge(scattered, 16 * 2 * NT)
            sp.dma_start(rows[:], list_rows).then_inc(rows_in, 16)

        @block.scalar
        def _(act):
            act.wait_ge(gd_done, 1)
            act.activation(ge[:], gd[:], ACT.Exp).then_inc(ge_done, 1)
            act.wait_ge(gap_done, 1)
            act.activation(x2[:], gap[:], ACT.Exp).then_inc(x2_done, 1)

        @block.vector
        def _(dve):
            link = Chain(dve, dve_link)
            over_g = lambda v: v[:].unsqueeze(2).broadcast_to([P, NT, G])

            def first_hot(out):
                link(dve.tensor_copy(out[:, :, 0], eq[:, :, 0]))
                link(dve.tensor_copy(seen[:], eq[:, :, 0]))
                for j in range(1, G):
                    link(dve.scalar_tensor_tensor(out[:, :, j], seen[:], 0.5, eq[:, :, j], ALU.is_lt, ALU.mult))
                    link(dve.tensor_tensor(seen[:], seen[:], eq[:, :, j], ALU.max))

            link(dve.tensor_reduce(top[:], gl, AX, ALU.max))
            dve.tensor_tensor(gd[:], gl, over_g(top), ALU.subtract).then_inc(gd_done, 1)
            link(dve.tensor_tensor(eq[:], gl, over_g(top), ALU.is_equal))
            first_hot(oh_g)
            dve.wait_ge(ge_done, 1)
            link(dve.tensor_reduce(gsum[:], ge[:], AX, ALU.add))
            link(dve.reciprocal(gprob[:], gsum[:]))
            group_hot = oh_g[:].unsqueeze(3).broadcast_to([P, NT, G, E_IN_G])
            link(dve.tensor_tensor(prod[:], el, group_hot, ALU.mult))
            link(dve.tensor_reduce(es[:], prod[:].rearrange("p t g e -> p t e g"), AX, ALU.add))
            link(dve.tensor_reduce(m1[:], es[:], AX, ALU.max))
            link(dve.tensor_tensor(eq[:], es[:], over_g(m1), ALU.is_equal))
            first_hot(oh_e[0])
            link(dve.scalar_tensor_tensor(es[:], oh_e[0][:], -3e38, es[:], ALU.mult, ALU.add))
            link(dve.tensor_reduce(m2[:], es[:], AX, ALU.max))
            link(dve.tensor_tensor(eq[:], es[:], over_g(m2), ALU.is_equal))
            first_hot(oh_e[1])
            dve.tensor_tensor(gap[:], m2[:], m1[:], ALU.subtract).then_inc(gap_done, 1)
            for c in range(2):
                link(dve.tensor_tensor(hot[c][:], group_hot, oh_e[c][:].unsqueeze(2).broadcast_to([P, NT, G, E_IN_G]),
                                       ALU.mult))
            dve.tensor_tensor(both[:], hot[0][:].rearrange("p t g e -> p t (g e)"),
                              hot[1][:].rearrange("p t g e -> p t (g e)"), ALU.add).then_inc(both_done, 1)
            dve.wait_ge(x2_done, 1)
            link(dve.tensor_scalar(m1[:], x2[:], 1.0, None, ALU.add))
            link(dve.reciprocal(m2[:], m1[:]))
            link(dve.tensor_tensor(weights[:, 0], m2[:], gprob[:], ALU.mult))
            link(dve.tensor_tensor(weights[:, 1], weights[:, 0], x2[:], ALU.mult))
            dve.wait_ge(made, 6)
            link(dve.tensor_copy(thr[:], thr_i[:]))
            link(dve.tensor_copy(tile_f[:], tile_i[:]))
            link(dve.tensor_copy(tok[:], tok_i[:]))
            dve.wait_ge(counted, 2)
            link(dve.memset(offs[:, 0], 0.0))
            for t in range(NT):
                link(dve.tensor_tensor(offs[:, t + 1], offs[:, t], tot_ps[:, t * NE:(t + 1) * NE], ALU.add))
            link(dve.tensor_tensor(over[:], offs[:, NT].unsqueeze(2).broadcast_to([P, NE, NT]),
                                   thr[:].unsqueeze(1).broadcast_to([P, NE, NT]), ALU.is_gt))
            link(dve.tensor_reduce(n_tiles[:], over[:], AX, ALU.add))
            link(dve.tensor_scalar(n_tiles[:], n_tiles[:], 1.0, None, ALU.max))
            link(dve.tensor_tensor_scan(upto[:], ones[:, 0:NE], n_tiles[:], 0.0, ALU.mult, ALU.add))
            link(dve.tensor_tensor(first_tile[:], upto[:], n_tiles[:], ALU.subtract))
            link(dve.tensor_scalar(start[:], first_tile[:], float(P), None, ALU.mult))
            link(dve.tensor_tensor(base[:], rank_ps[:].rearrange("p (t e) -> p t e", t=NT), offs[:, 0:NT], ALU.add))
            link(dve.tensor_tensor(base[:], base[:], start[:].unsqueeze(1).broadcast_to([P, NT, NE]), ALU.add))
            for c in range(2):
                pick = hot[c][:].rearrange("p t g e -> p t (g e)")
                link(dve.tensor_tensor(both[:], base[:], pick, ALU.mult))
                link(dve.tensor_reduce(slot_f[:, c], both[:], AX, ALU.add))
            dve.tensor_copy(slots[:], slot_f[:]).then_inc(slots_done, 1)
            link(dve.tensor_tensor(past[:], upto[:].unsqueeze(1).broadcast_to([P, MT, NE]),
                                   tile_f[:].unsqueeze(2).broadcast_to([P, MT, NE]), ALU.is_le))
            link(dve.tensor_reduce(exp_f[:], past[:], AX, ALU.add))
            link(dve.tensor_scalar(exp_f[:], exp_f[:], float(NE - 1), None, ALU.min))
            link(dve.tensor_copy(tile_expert[:], exp_f[:]))
            link(dve.tensor_tensor(past[:, :, 0:NE - 1], first_tile[:, 0:NE - 1].unsqueeze(1).broadcast_to([P, MT, NE - 1]),
                                   tile_f[:].unsqueeze(2).broadcast_to([P, MT, NE - 1]), ALU.is_equal))
            link(dve.tensor_reduce(splits[:], past[:, :, 0:NE - 1], AX, ALU.add))
            link(dve.tensor_copy(split_at[:], splits[:]))
            evens = tile_f[:].rearrange("p (n u) -> p n u", u=2)[:, :, 0]
            link(dve.tensor_tensor(live[:], evens, upto[:, NE - 1:NE].broadcast_to([P, MT // 2]), ALU.is_lt))
            link(dve.tensor_copy(pair_live[:], live[:]))
            link(dve.tensor_reduce(last_f[:], live[:], AX, ALU.add))
            link(dve.tensor_scalar(last_f[:], last_f[:], 2.0, -1.0, ALU.mult, ALU.add))
            link(dve.tensor_copy(last_tile[:], last_f[:]))
            link(dve.memset(lists[:, MT:], 0))
            dve.wait_ge(turned, 1)
            link(dve.tensor_copy(lists[:, 0:MT], list_ps[:]))

        @block.tensor
        def _(pe):
            pe.wait_ge(both_done, 1)
            pe.wait_ge(made, 6)
            m = both[:].rearrange("p t e -> p (t e)")
            pe.matmul(rank_ps[:], tri[:], m, start=True, stop=True).then_inc(counted, 1)
            pe.matmul(tot_ps[:], ones[:], m, start=True, stop=True).then_inc(counted, 1)
            pe.wait_ge(rows_in, 16)
            pe.transpose(list_ps[:], rows[:], ident[0:MT, 0:MT]).then_inc(turned, 1)


def experts(nc, exp_w1, exp_w3, exp_w2, ident, lists, tile_expert, split_at, pair_live, last_tile, h1_dram, y_dram):
    with ExitStack() as ctx:
        sb = lambda n, s, d=F32: ctx.enter_context(nc.sbuf_tensor("e_" + n, s, d))
        ps = lambda n, s, d=F32: ctx.enter_context(nc.psum_tensor("e_" + n, s, d))
        sem = ctx.enter_context(semaphores(nc, "e_"))
        HALF = KD // 2
        UP_PARTS = 4
        DOWN_PARTS = KE
        up_raw = sb("up_raw", [P, 2, KD, 2 * DE])
        up_hi = sb("up_hi", [P, 2, KD, 2 * DE], F32R)
        up_lo = sb("up_lo", [P, 2, KD, 2 * DE], F32R)
        down_raw = sb("down_raw", [P, 2, KE, D])
        down_hi = sb("down_hi", [P, 2, KE, D], F32R)
        down_lo = sb("down_lo", [P, 2, KE, D], F32R)
        ix = [sb(f"ix{u}", [P, 1], U32) for u in range(2)]
        xg = [sb(f"xg{u}", [P, D]) for u in range(2)]
        xt_hi = [sb(f"xt_hi{u}", [P, KD, P], F32R) for u in range(2)]
        xt_lo = [sb(f"xt_lo{u}", [P, KD, P], F32R) for u in range(2)]
        sg = sb("sg", [P, DE])
        hid = sb("hid", [P, DE])
        ht_hi = sb("ht_hi", [P, KE, P], F32R)
        ht_lo = sb("ht_lo", [P, KE, P], F32R)
        yt = [sb(f"yt{u}", [P, D]) for u in range(2)]
        t_ps = [ps(f"t_ps{c}", [P, HALF, P]) for c in range(2)]
        a_ps = ps("a_ps", [P, 2 * DE])
        h_ps = ps("h_ps", [P, KE, P])
        y_ps = [ps(f"y_ps{c}", [P, 512]) for c in range(2)]

        go = sem("go")
        ix_done = sem("index_ready")
        x_in = [sem(f"rows_gathered{u}") for u in range(2)]
        w_in = [sem(f"weights_loaded{b}") for b in range(2)]
        w_ready = sem("raw_weights_ready")
        up_hi_made = sem("up_hi_made")
        up_lo_made = sem("up_lo_made")
        down_hi_made = sem("down_hi_made")
        down_lo_made = sem("down_lo_made")
        t_done = [sem(f"x_transposed{c}") for c in range(2)]
        xh_done = [sem(f"xt_hi_done{c}") for c in range(2)]
        xl_done = [sem(f"xt_lo_done{c}") for c in range(2)]
        a_done = sem("a_done")
        sg_done = sem("silu_done")
        hid_done = sem("hid_done")
        h_done = sem("hid_transposed")
        hh_done = sem("ht_hi_done")
        hl_done = sem("ht_lo_done")
        y_done = [sem(f"y_done{c}") for c in range(2)]
        yt_done = [sem(f"yt_done{c}") for c in range(2)]
        y_stored = [sem(f"y_stored{u}") for u in range(2)]
        filled = sem("unused_rows_filled")
        block = ctx.enter_context(nc.Block())

        def buffer(w, e, rows):
            return w[:, bass.ds(e % 2, 1), rows, :].rearrange("p o k n -> p (o k) n")

        def expert_of(eng, j):
            return eng.value_load(tile_expert[0:1, bass.ds(j, 1)], min_val=0, max_val=NE - 1)

        def beside_first_tile(eng, j, split):
            flag = eng.value_load(split_at[0:1, bass.ds(j, 1)], min_val=0, max_val=1)
            with eng.If(flag > 0):
                split(eng.value_load(tile_expert[0:1, bass.ds(j, 1)], min_val=0, max_val=NE - 2) + 1)

        def run_tiles(eng, ahead, split_up, up, turn, down, turn_hid, split_down, fill=None):
            def tile(j, u, is_first=False):
                ahead(j + 2, u)
                if split_up:
                    beside_first_tile(eng, j, split_up)
                up(j, u)
                turn(j + 1, 1 - u)
                if not is_first:
                    down(j - 1, 1 - u)
                turn_hid(j, u)
                if split_down:
                    beside_first_tile(eng, j, split_down)

            turn(0, 0)
            tile(0, 0, is_first=True)
            tile(1, 1)
            with eng.Fori(1, MT // 2) as n:
                flag = eng.value_load(pair_live[0:1, bass.ds(n, 1)], min_val=0, max_val=1)
                with eng.If(flag > 0):
                    for u in range(2):
                        tile(2 * n + u, u)
                    if fill:
                        eng.sem_inc(filled, 32)
                if fill:
                    with eng.Else():
                        fill(n)
            last = eng.value_load(last_tile[0:1, 0:1], min_val=1, max_val=MT - 1)
            down(last, 1)
            return last

        def skip(j, u):
            pass

        @block.sync
        def _(sp):
            def load(e, b):
                part = lambda w: w[0][bass.ds(e, 1)].rearrange("o (k p) n -> p (o k) n", p=P)
                sp.dma_start(up_raw[:, b, :, 0:DE], part(exp_w1)).then_inc(w_in[b], 16)
                sp.dma_start(up_raw[:, b, :, DE:2 * DE], part(exp_w3)).then_inc(w_in[b], 16)
                sp.dma_start(down_raw[:, b], part(exp_w2)).then_inc(w_in[b], 16)

            for b in range(2):
                load(b, b)
            with sp.Fori(0, NE // 2 - 1) as n:
                for b in range(2):
                    sp.wait_ge(w_in[b], 48 * n + 48)
                    sp.sem_inc(w_ready, 1)
                    sp.wait_ge(up_lo_made, UP_PARTS * (2 * n + b + 1))
                    sp.nop(nofuse=True)
                    sp.wait_ge(down_lo_made, DOWN_PARTS * (2 * n + b + 1))
                    sp.nop(nofuse=True)
                    load(2 * n + 2 + b, b)
            for b in range(2):
                sp.wait_ge(w_in[b], 48 * (NE // 2))
                sp.sem_inc(w_ready, 1)

        @block.gpsimd
        def _(pool):
            def ahead(j, u):
                pool.wait_ge(ix_done, j + 1)
                pool.nop(nofuse=True)
                pool.indirect_dma_start(xg[u][:], None, h1_dram, bass.IndirectOffsetOnAxis(ix[u][:, 0:1], 0))\
                    .then_inc(x_in[u], 16)

            ahead(0, 0)
            ahead(1, 1)
            last = run_tiles(pool, ahead, None, skip, skip, skip, skip, None)
            pool.wait_ge(x_in[1], 8 * (last - 1) + 32)

        @block.tensor
        def _(pe):
            def turn(j, u):
                pe.wait_ge(x_in[u], 8 * (j - u) + 16)
                for c in range(2):
                    pe.wait_ge(xl_done[c], j + 1)
                    for i in range(HALF):
                        k = c * HALF + i
                        last = pe.transpose(t_ps[c][:, i, :], xg[u][:, k * P:(k + 1) * P], ident[:])
                    last.then_inc(t_done[c], 1)

            def up(j, u):
                e = expert_of(pe, j)
                pe.wait_ge(up_lo_made, UP_PARTS * e + UP_PARTS)
                for k in range(KD):
                    if k % HALF == 0:
                        pe.wait_ge(xl_done[k // HALF], j + 2)
                    w = [buffer(part, e, slice(k, k + 1)).rearrange("p o n -> p (o n)") for part in (up_hi, up_lo)]
                    last = three_pass(pe, a_ps[:], (xt_hi[u][:, k, :], xt_lo[u][:, k, :]), w, k == 0, k == KD - 1)
                last.then_inc(a_done, 1)

            def turn_hid(j, u):
                pe.wait_ge(hid_done, j + 2)
                pe.wait_ge(hl_done, j + 1)
                for k in range(KE):
                    last = pe.transpose(h_ps[:, k, :], hid[:, k * P:(k + 1) * P], ident[:])
                last.then_inc(h_done, 1)

            def down(j, u):
                e = expert_of(pe, j)
                pe.wait_ge(down_lo_made, DOWN_PARTS * e + DOWN_PARTS)
                pe.wait_ge(hl_done, j + 2)
                for c in range(2):
                    pe.wait_ge(yt_done[c], j + 1)
                    for k in range(KE):
                        w = [buffer(part, e, slice(k, k + 1)).rearrange("p o n -> p (o n)")[:, c * 512:(c + 1) * 512]
                             for part in (down_hi, down_lo)]
                        last = three_pass(pe, y_ps[c][:], (ht_hi[:, k, :], ht_lo[:, k, :]), w, k == 0, k == KE - 1)
                    last.then_inc(y_done[c], 1)

            run_tiles(pe, skip, None, up, turn, down, turn_hid, None)

        @block.scalar
        def _(act):
            act.sem_inc(go, 1)
            for c in range(2):
                act.sem_inc(yt_done[c], 1)
            for u in range(2):
                act.sem_inc(y_stored[u], 16)

            def split_up(e):
                act.wait_ge(w_ready, e + 1)
                for i in range(UP_PARTS):
                    rows = slice(i * (KD // UP_PARTS), (i + 1) * (KD // UP_PARTS))
                    act.wait_ge(go, 1)
                    act.activation(buffer(up_hi, e, rows), buffer(up_raw, e, rows), ACT.Copy).then_inc(up_hi_made, 1)

            def split_down(e):
                for k in range(DOWN_PARTS):
                    act.wait_ge(go, 1)
                    act.activation(buffer(down_hi, e, slice(k, k + 1)), buffer(down_raw, e, slice(k, k + 1)), ACT.Copy)\
                       .then_inc(down_hi_made, 1)

            def ahead(j, u):
                act.wait_ge(a_done, j - 1)
                act.wait_ge(go, 1)

            def up(j, u):
                act.wait_ge(a_done, j + 2)
                act.wait_ge(hid_done, j + 1)
                act.activation(sg[:], a_ps[:, 0:DE], ACT.Silu).then_inc(sg_done, 1)

            def turn(j, u):
                for c in range(2):
                    act.wait_ge(t_done[c], j + 1)
                    act.activation(xt_hi[u][:, c * HALF:(c + 1) * HALF], t_ps[c][:], ACT.Copy).then_inc(xh_done[c], 1)

            def down(j, u):
                act.wait_ge(y_stored[u], 8 * (j - u) + 16)
                for c in range(2):
                    act.wait_ge(y_done[c], j + 1)
                    act.activation(yt[u][:, c * 512:(c + 1) * 512], y_ps[c][:], ACT.Copy).then_inc(yt_done[c], 1)
                act.wait_ge(yt_done[0], j + 2)
                act.wait_ge(yt_done[1], j + 2)
                act.dma_start(y_dram[bass.ds(j * P, P), :], yt[u][:]).then_inc(y_stored[u], 16)

            def turn_hid(j, u):
                act.wait_ge(h_done, j + 1)
                act.activation(ht_hi[:], h_ps[:], ACT.Copy).then_inc(hh_done, 1)

            split_up(0)
            split_down(0)
            def fill(n):
                for u in range(2):
                    act.dma_start(y_dram[bass.ds((2 * n + u) * P, P), :], yt[0][:]).then_inc(filled, 16)

            last = run_tiles(act, ahead, split_up, up, turn, down, turn_hid, split_down, fill)
            stores = 8 * last + 24
            for u in range(2):
                act.wait_ge(y_stored[u], stores)
                act.nop(nofuse=True)
            act.wait_ge(filled, 16 * (MT - 2))

        @block.vector
        def _(dve):
            dve.sem_inc(a_done, 1)
            dve.sem_inc(hid_done, 1)
            dve.sem_inc(hl_done, 1)
            for c in range(2):
                dve.sem_inc(xl_done[c], 1)

            def index(j, u):
                dve.nop(nofuse=True)
                dve.tensor_copy(ix[u][:], lists[:, bass.ds(j, 1)]).then_inc(ix_done, 1)

            def ahead(j, u):
                dve.wait_ge(t_done[1], j - 1)
                index(j, u)

            def split_up(e):
                for i in range(UP_PARTS):
                    rows = slice(i * (KD // UP_PARTS), (i + 1) * (KD // UP_PARTS))
                    dve.wait_ge(up_hi_made, UP_PARTS * e + i + 1)
                    dve.nop(nofuse=True)
                    dve.tensor_tensor(buffer(up_lo, e, rows), buffer(up_raw, e, rows), buffer(up_hi, e, rows).bitcast(F32),
                                      ALU.subtract).then_inc(up_lo_made, 1)

            def split_down(e):
                for k in range(DOWN_PARTS):
                    row_k = slice(k, k + 1)
                    dve.wait_ge(down_hi_made, DOWN_PARTS * e + k + 1)
                    dve.nop(nofuse=True)
                    dve.tensor_tensor(buffer(down_lo, e, row_k), buffer(down_raw, e, row_k),
                                      buffer(down_hi, e, row_k).bitcast(F32), ALU.subtract).then_inc(down_lo_made, 1)

            def up(j, u):
                dve.wait_ge(sg_done, j + 1)
                dve.tensor_tensor(hid[:], sg[:], a_ps[:, DE:2 * DE], ALU.mult).then_inc(hid_done, 1)

            def turn(j, u):
                for c in range(2):
                    part = slice(c * HALF, (c + 1) * HALF)
                    dve.wait_ge(xh_done[c], j + 1)
                    dve.tensor_tensor(xt_lo[u][:, part], t_ps[c][:], xt_hi[u][:, part].bitcast(F32), ALU.subtract)\
                       .then_inc(xl_done[c], 1)

            def turn_hid(j, u):
                dve.wait_ge(hh_done, j + 1)
                dve.tensor_tensor(ht_lo[:], h_ps[:], ht_hi[:].bitcast(F32), ALU.subtract).then_inc(hl_done, 1)

            index(0, 0)
            index(1, 1)
            split_up(0)
            split_down(0)
            run_tiles(dve, ahead, split_up, up, turn, skip, turn_hid, split_down)


def combine(nc, ln_g, ln_b, slots, weights, h1_dram, y_dram, out):
    with ExitStack() as ctx:
        sb = lambda n, s, d=F32: ctx.enter_context(nc.sbuf_tensor("c_" + n, s, d))
        sem = ctx.enter_context(semaphores(nc, "c_"))
        NB = 4
        g_b = sb("g_b", [P, D])
        b_b = sb("b_b", [P, D])
        ix = [sb(f"ix{u}", [P, 2], U32) for u in range(NB)]
        h1 = [sb(f"h1{u}", [P, D]) for u in range(NB)]
        y1 = [sb(f"y1{u}", [P, D]) for u in range(NB)]
        y2 = [sb(f"y2{u}", [P, D]) for u in range(NB)]
        wt = [sb(f"wt{u}", [P, 2]) for u in range(NB)]
        stats = sb("stats", [P, 12])
        mv = sb("mv", [P, 2])
        var = sb("var", [P, 1])
        tmp = sb("tmp", [P, 1])
        rstd = [sb(f"rstd{u}", [P, 1]) for u in range(NB)]
        shift = [sb(f"shift{u}", [P, 1]) for u in range(NB)]
        rows_in = sem("rows_loaded")
        ix_done = sem("index_ready")
        h_in = [sem(f"h1_loaded{u}") for u in range(NB)]
        y_in = [sem(f"y_gathered{u}") for u in range(NB)]
        dve_link = sem("dve_link")
        ah_done = sem("alpha_h_done")
        ln_done = sem("stats_done")
        xn_done = sem("normalised")
        hg_done = sem("gain_done")
        o_done = sem("out_done")
        stored = [sem(f"stored{u}") for u in range(NB)]
        block = ctx.enter_context(nc.Block())

        @block.sync
        def _(sp):
            for u in range(NB):
                sp.sem_inc(stored[u], 16)
            sp.dma_start(g_b[:], row(ln_g, D)).then_inc(rows_in, 16)
            sp.dma_start(b_b[:], row(ln_b, D)).then_inc(rows_in, 16)
            with sp.Fori(0, NT // NB) as n:
                for u in range(NB):
                    t = NB * n + u
                    sp.wait_ge(stored[u], 16 * n + 16)
                    sp.dma_start(h1[u][:], h1_dram[bass.ds(t * P, P), :]).then_inc(h_in[u], 16)
            for u in range(NB):
                sp.wait_ge(stored[u], 16 + 16 * (NT // NB))

        def run_tiles(eng, load, norm, finish):
            for u in range(NB - 1):
                load(u, u)
            norm(0, 0, 0)
            with eng.Fori(0, NT // NB - 1) as n:
                for u in range(NB):
                    t = NB * n + u
                    load(t + NB - 1, (u + NB - 1) % NB)
                    norm(t + 1, (u + 1) % NB, 0)
                    finish(t, u)
            for u in range(NB):
                t = NT - NB + u
                if u == 0:
                    load(NT - 1, NB - 1)
                if u < NB - 1:
                    norm(t + 1, u + 1, 0)
                finish(t, u)

        @block.gpsimd
        def _(pool):
            pool.wait_ge(rows_in, 32)

            def load(t, u):
                pool.wait_ge(ix_done, t + 1)
                pool.wait_ge(ln_done, t + 1)
                pool.nop(nofuse=True)
                for c, y in enumerate((y1, y2)):
                    pool.indirect_dma_start(y[u][:], None, y_dram, bass.IndirectOffsetOnAxis(ix[u][:, c:c + 1], 0))\
                        .then_inc(y_in[u], 16)

            def finish(t, u):
                pool.wait_ge(hg_done, t + 1)
                pool.tensor_tensor(h1[u][:], h1[u][:], b_b[:], ALU.add).then_inc(o_done, 1)

            run_tiles(pool, load, lambda t, u, z: None, finish)

        @block.vector
        def _(dve):
            dve.sem_inc(ln_done, NB)
            links = 2 + 4 + RSQRT_LINKS

            def load(t, u):
                dve.wait_ge(ln_done, t + 1)
                dve.nop(nofuse=True)
                dve.tensor_copy(wt[u][:], weights[:, :, bass.ds(t, 1)].rearrange("p c o -> p (c o)"))
                dve.tensor_copy(ix[u][:], slots[:, :, bass.ds(t, 1)].rearrange("p c o -> p (c o)")).then_inc(ix_done, 1)

            def norm(t, u, z):
                link = Chain(dve, dve_link, links * t)
                dve.wait_ge(ah_done, t + 1)
                dve.wait_ge(ix_done, t + 1)
                dve.wait_ge(y_in[u], 8 * (t - u) + 32)
                link(dve.scalar_tensor_tensor(h1[u][:], y1[u][:], wt[u][:, 0:1], h1[u][:], ALU.mult, ALU.add))
                link(dve.scalar_tensor_tensor(h1[u][:], y2[u][:], wt[u][:, 1:2], h1[u][:], ALU.mult, ALU.add))
                for half in range(2):
                    link(dve.bn_stats(stats[:, 6 * half:6 * half + 6], h1[u][:, 512 * half:512 * half + 512]))
                dve.nop(nofuse=True)
                link(dve.bn_aggr(mv[:], stats[:]))
                link(dve.tensor_scalar(var[:], mv[:, 1:2], LN_EPS, None, ALU.add))
                rsqrt(dve, link, var[:], rstd[u][:], tmp[:])
                dve.tensor_scalar(shift[u][:], mv[:, 0:1], rstd[u][:], -1.0, ALU.mult, ALU.mult).then_inc(ln_done, 1)

            def finish(t, u):
                dve.wait_ge(xn_done, t + 1)
                dve.tensor_tensor(h1[u][:], h1[u][:], g_b[:], ALU.mult).then_inc(hg_done, 1)

            dve.wait_ge(rows_in, 32)
            run_tiles(dve, load, norm, finish)

        @block.scalar
        def _(act):
            def load(t, u):
                act.wait_ge(h_in[u], 4 * (t - u) + 16)
                act.activation(h1[u][:], h1[u][:], ACT.Copy, scale=ALPHA).then_inc(ah_done, 1)

            def norm(t, u, z):
                act.wait_ge(ln_done, t + NB + 1)
                act.activation(h1[u][:], h1[u][:], ACT.Identity, bias=shift[u][:], scale=rstd[u][:]).then_inc(xn_done, 1)

            def finish(t, u):
                act.wait_ge(o_done, t + 1)
                act.dma_start(out[bass.ds(t * P, P), :], h1[u][:]).then_inc(stored[u], 16)

            run_tiles(act, load, norm, finish)


_NAMES = ["ln_in_g", "ln_in_b", "w_in", "conv_w", "conv_b", "lru_wa", "lru_ba", "lru_wx", "lru_bx", "lru_lambda",
          "q_norm_g", "k_norm_g", "attn_out_g", "lru_out_g", "w_out", "ln1_g", "ln1_b", "router_wg", "router_bg",
          "router_we", "router_be", "exp_w1", "exp_w3", "exp_w2", "ln2_g", "ln2_b"]


def rope_table():
    import numpy as np

    grid_w, theta, half = 64, 10000.0, HD // 4
    inv_freq = (theta ** (-np.arange(half, dtype=np.float32) / half)).astype(np.float32)
    pos = np.arange(SEQ)
    tab = np.zeros((P, TPS, 2, 2, 2, half), np.float32)
    for sec, where in enumerate((pos // grid_w, pos % grid_w)):
        ang = where.astype(np.float32)[:, None] * inv_freq
        cos = np.cos(ang).reshape(TPS, P, half).transpose(1, 0, 2)
        sin = np.sin(ang).reshape(TPS, P, half).transpose(1, 0, 2)
        for f in range(2):
            tab[:, :, 0, sec, f] = cos
            tab[:, :, 1, sec, f] = sin if f else -sin
    return tab.reshape(P, TPS * 2 * HD)


def kernel(**inputs):
    import numpy as np
    import concourse.bacc as bacc
    from concourse.bass_utils import run_bass_kernel_spmd

    nc = bacc.Bacc("TRN2", target_bir_lowering=False, num_devices=1)
    arrays = {"in_x": np.concatenate([inputs["x_prompt"][0], inputs["x_sample"][0]])}
    for name in _NAMES:
        arrays[f"in_{name}"] = np.ascontiguousarray(inputs[name])
    arrays["in_rope"] = rope_table()
    args = [nc.dram_tensor(n, a.shape, mybir.dt.from_np(a.dtype), kind="ExternalInput").ap() for n, a in arrays.items()]
    args.append(nc.dram_tensor("out", (T, D), F32, kind="ExternalOutput").ap())
    build(nc, *args)
    got = run_bass_kernel_spmd(nc, [arrays], core_ids=[0]).results[0]["out"]
    return got[None, 0:SEQ], got[None, SEQ:T]
```

```python
from contextlib import ExitStack, contextmanager

import concourse.bass as bass
from concourse import mybir

F32 = mybir.dt.float32
F32R = mybir.dt.float32r
I32 = mybir.dt.int32
U32 = mybir.dt.uint32
ALU = mybir.AluOpType
ACT = mybir.ActivationFunctionType
AX = mybir.AxisListType.X

P = 128
D = 1024
KD = D // P
SEQS = 2
SEQ = 1024
T = SEQS * SEQ
NT = T // P
TPS = SEQ // P
CH = 256
NC = T // CH
CPS = SEQ // CH
HD = 64
NQ = 8
NKV = 2
NH = NQ + NKV
QW = NQ * HD
KVW = NKV * HD
QKVW = QW + 2 * KVW
QKW = QW + KVW
LW = 512
FT = LW // P
LHD = 64
TAPS = 4
G = 4
E_IN_G = 4
NE = G * E_IN_G
DE = 256
KE = DE // P
RW = G + NE
MT = 2 * NT + NE
SLOTS = MT * P
LN_EPS = 1e-5
QK_EPS = 1e-6
LRU_C = 8.0
ALPHA = 2.0 ** 0.25
SCALE = HD ** -0.5
NEWTON = 3


class Chain:

    def __init__(self, eng, sem, done=0):
        self.eng, self.sem, self.done, self.n = eng, sem, done, 0

    def __call__(self, ins):
        self.n += 1
        ins.then_inc(self.sem, 1)
        self.eng.wait_ge(self.sem, self.done + self.n)


def rsqrt(dve, link, x, y, t):
    link(dve.tensor_scalar(t.bitcast(I32), x.bitcast(I32), 1, None, ALU.logical_shift_right))
    link(dve.tensor_scalar(y.bitcast(I32), t.bitcast(I32), -1.0, float(0x5F3759DF), ALU.mult, ALU.add))
    link(dve.tensor_scalar(x, x, -0.5, None, ALU.mult))
    for _ in range(NEWTON):
        if x.shape[-1] == 1:
            link(dve.scalar_tensor_tensor(t, y, x, y, ALU.mult, ALU.mult))
        else:
            link(dve.tensor_tensor(t, y, y, ALU.mult))
            link(dve.tensor_tensor(t, t, x, ALU.mult))
        link(dve.scalar_tensor_tensor(y, t, 1.5, y, ALU.add, ALU.mult))


RSQRT_LINKS = 3 + 2 * NEWTON
RSQRT_LINKS_WIDE = 3 + 3 * NEWTON


def three_pass(pe, out, lhs, rhs, first, last):
    pe.matmul(out, lhs[0], rhs[0], start=first, stop=False)
    pe.matmul(out, lhs[0], rhs[1], start=False, stop=False)
    return pe.matmul(out, lhs[1], rhs[0], start=False, stop=last)


def build(nc, x, ln_in_g, ln_in_b, w_in, conv_w, conv_b, lru_wa, lru_ba, lru_wx, lru_bx, lru_lambda,
          q_norm_g, k_norm_g, attn_out_g, lru_out_g, w_out, ln1_g, ln1_b, router_wg, router_bg,
          router_we, router_be, exp_w1, exp_w3, exp_w2, ln2_g, ln2_b, rope, out):
    h_dram = nc.dram_tensor("h_dram", (T, D), F32, kind="Internal").ap()
    ht_hi_dram = nc.dram_tensor("ht_hi_dram", (NC, P, KD * CH), F32, kind="Internal").ap()
    ht_lo_dram = nc.dram_tensor("ht_lo_dram", (NC, P, KD * CH), F32, kind="Internal").ap()
    q_dram = nc.dram_tensor("q_dram", (NT, P, NQ * P), F32, kind="Internal").ap()
    h1_dram = nc.dram_tensor("h1_dram", (T, D), F32, kind="Internal").ap()
    y_dram = nc.dram_tensor("y_dram", (SLOTS, D), F32, kind="Internal").ap()

    with ExitStack() as whole:
        sb = lambda n, s, d=F32: whole.enter_context(nc.sbuf_tensor(n, s, d))
        ident = sb("ident", [P, P])
        identr = sb("identr", [P, P], F32R)
        logits = sb("logits", [P, NT, RW])
        with ExitStack() as kept:
            sb = lambda n, s, d=F32: kept.enter_context(nc.sbuf_tensor(n, s, d))
            k_hi = sb("k_hi", [P, NKV, T], F32R)
            k_lo = sb("k_lo", [P, NKV, T], F32R)
            v_all = sb("v_all", [P, NT, KVW])
            y_all = sb("y_all", [P, FT, T])
            with nc.sbuf_tensor("x_all", [P, FT, T], F32) as x_all:
                with nc.sbuf_tensor("wq_raw", [P, KD, QKVW], F32) as wq_raw:
                    project_lru(nc, x, ln_in_g, ln_in_b, w_in, ident, identr, x_all, y_all, k_hi, k_lo, v_all, wq_raw,
                                h_dram, ht_hi_dram, ht_lo_dram)
                    project_qkv(nc, wq_raw, q_norm_g, k_norm_g, rope, identr, ht_hi_dram, ht_lo_dram,
                                k_hi, k_lo, v_all, q_dram)
                lru(nc, conv_w, conv_b, lru_wa, lru_ba, lru_wx, lru_bx, lru_lambda, x_all, y_all)
            attend(nc, w_out, attn_out_g, lru_out_g, ln1_g, ln1_b, router_wg, router_bg, router_we,
                   router_be, ident, k_hi, k_lo, v_all, y_all, h_dram, q_dram, h1_dram, logits)
        sb = lambda n, s, d=F32: whole.enter_context(nc.sbuf_tensor(n, s, d))
        slots = sb("slots", [P, 2, NT], U32)
        weights = sb("weights", [P, 2, NT])
        lists = sb("lists", [P, MT + 2], U32)
        tile_expert = sb("tile_expert", [P, MT], I32)
        split_at = sb("split_at", [P, MT], I32)
        pair_live = sb("pair_live", [P, MT // 2], I32)
        last_tile = sb("last_tile", [P, 1], I32)
        tables = (lists, tile_expert, split_at, pair_live, last_tile)
        with ExitStack() as kept:
            sb = lambda n, s, d=F32: kept.enter_context(nc.sbuf_tensor(n, s, d))
            up_w = [sb(n, [P, 2, KD, 2 * DE], d) for n, d in (("up_raw", F32), ("up_hi", F32R), ("up_lo", F32R))]
            down_w = [sb(n, [P, 2, KE, D], d) for n, d in (("down_raw", F32), ("down_hi", F32R), ("down_lo", F32R))]
            route(nc, ident, logits, slots, weights, *tables, exp_w1, exp_w3, exp_w2, up_w, down_w)
            experts(nc, exp_w1, exp_w3, exp_w2, up_w, down_w, ident, *tables, h1_dram, y_dram)
        combine(nc, ln2_g[0], ln2_b[0], slots, weights, h1_dram, y_dram, out)


@contextmanager
def semaphores(nc, prefix):
    held = []

    def sem(name):
        held.append(nc.alloc_semaphore(prefix + name))
        return held[-1]

    yield sem
    nc.clear_and_free_semaphores(held)
    nc.all_engine_barrier()


def row(ap, n):
    return ap.rearrange("(o n) -> o n", o=1).broadcast_to([P, n])


def run_chunks(eng, ln, transpose, split, project):
    ln(0, 0)
    split()
    transpose(0, 0)
    ln(1, 1)
    with eng.Fori(0, (NC - 2) // 2) as n:
        for u in range(2):
            c = 2 * n + u
            project(c, u, 0)
            transpose(c + 1, 1 - u)
            ln(c + 2, u)
            project(c, u, 1)
    for u in range(2):
        project(NC - 2 + u, u, 0)
        if u == 0:
            transpose(NC - 1, 1)
        project(NC - 2 + u, u, 1)


def project_lru(nc, x, ln_g, ln_b, w_in, ident, identr, x_all, y_all, k_hi, k_lo, v_all, wq_raw, h_dram,
                ht_hi_dram, ht_lo_dram):
    with ExitStack() as ctx:
        sb = lambda n, s, d=F32: ctx.enter_context(nc.sbuf_tensor(n, s, d))
        ps = lambda n, s, d=F32: ctx.enter_context(nc.psum_tensor(n, s, d))
        sem = ctx.enter_context(semaphores(nc, "a_"))
        NF = 2 * FT
        w_hi = sb("wl_hi", [P, KD, NF * P], F32R)
        w_lo = sb("wl_lo", [P, KD, NF * P], F32R)
        raw = x_all[:].rearrange("p f t -> p (f t)").rearrange("p (k n) -> p k n", k=KD)
        g_b = sb("ln_in_g_b", [P, D])
        b_b = sb("ln_in_b_b", [P, D])
        K_LATE = 2
        xt = [sb("xt0", [P, D])[:], wq_raw[:, KD - K_LATE:, :].rearrange("p k n -> p (k n)")[:, 0:D]]
        ht = [v_all[:, j * TPS:(j + 1) * TPS, :].rearrange("p t n -> p (t n)") for j in range(2)]
        t_hi = [k_hi[:, u, :].rearrange("p (k n) -> p k n", k=KD) for u in range(2)]
        t_lo = [k_lo[:, u, :].rearrange("p (k n) -> p k n", k=KD) for u in range(2)]
        stats = sb("stats", [P, 12])
        mv = sb("mv", [P, 2])
        var = sb("var", [P, 1])
        tmp = sb("tmp", [P, 1])
        rstd = [sb(f"rstd{j}", [P, 1]) for j in range(2)]
        shift = [sb(f"shift{j}", [P, 1]) for j in range(2)]
        tps = [ps(f"tps{j}", [P, KD, P]) for j in range(2)]
        acc = [ps(f"acc{j}", [P, 512]) for j in range(4)]

        go = sem("go_a")
        w_in_sem = [sem(f"w_raw_loaded{k}") for k in range(KD)]
        wq_in = sem("wq_raw_loaded")
        ln_sem = sem("ln_rows_loaded")
        id_sem = sem("ident_made")
        hi_made = sem("w_hi_made")
        lo_made = sem("w_lo_made")
        x_in = [sem(f"x_tile_loaded{j}") for j in range(2)]
        dve_link = sem("dve_link_a")
        stats_done = sem("stats_done")
        xn_done = sem("normalised")
        hg_done = sem("gain_applied")
        h_done = sem("h_done")
        h_stored = [sem(f"h_stored{j}") for j in range(2)]
        tr_done = sem("h_transposed")
        hi_done = sem("t_hi_done")
        lo_done = sem("t_lo_done")
        t_stored = [sem(f"t_stored{c}") for c in range(2)]
        acc_done = sem("acc_done")
        acc_free = sem("acc_free")
        block = ctx.enter_context(nc.Block())

        @block.sync
        def _(sp):
            sp.sem_inc(go, 1)
            w_rows = w_in[0].rearrange("(k p) n -> p k n", p=P)[:, :, QKVW:QKVW + NF * P]
            for j in range(2):
                sp.dma_start(xt[j], x[j * P:(j + 1) * P, :]).then_inc(x_in[j], 16)
            sp.dma_start(g_b[:], row(ln_g, D)).then_inc(ln_sem, 16)
            sp.dma_start(b_b[:], row(ln_b, D)).then_inc(ln_sem, 16)
            for k in range(KD):
                sp.dma_start(raw[:, k, :], w_rows[:, k, :]).then_inc(w_in_sem[k], 16)
            wq_rows = w_in[0].rearrange("(k p) n -> p k n", p=P)[:, :, 0:QKVW]
            with sp.Fori(0, NC - 1) as c:
                for j in range(2):
                    sp.wait_ge(hg_done, 2 * c + j + 1)
                    sp.dma_start(xt[j], x[bass.ds((2 * c + j + 2) * P, P), :]).then_inc(x_in[j], 16)
            sp.dma_start(wq_raw[:, 0:KD - K_LATE], wq_rows[:, 0:KD - K_LATE]).then_inc(wq_in, 16)
            sp.wait_ge(hg_done, 2 * NC)
            sp.dma_start(wq_raw[:, KD - K_LATE:], wq_rows[:, KD - K_LATE:]).then_inc(wq_in, 16)
            sp.wait_ge(wq_in, 32)

        @block.gpsimd
        def _(pool):
            pool.memset(ident[:], 0.0).then_inc(id_sem, 1)
            pool.wait_ge(id_sem, 1)
            pool.affine_select(out=ident[:], in_=ident[:], compare_op=ALU.not_equal, fill=1.0, base=0,
                               pattern=[[-1, P]], channel_multiplier=1).then_inc(id_sem, 1)
            pool.wait_ge(ln_sem, 32)
            with pool.Fori(0, NC) as c:
                for j in range(2):
                    pool.wait_ge(hg_done, 2 * c + j + 1)
                    pool.tensor_tensor(ht[j], ht[j], b_b[:], ALU.add).then_inc(h_done, 1)

        @block.vector
        def _(dve):
            dve.wait_ge(id_sem, 2)
            dve.tensor_copy(identr[:], ident[:]).then_inc(id_sem, 1)
            links = 2 * (4 + RSQRT_LINKS)

            def ln(c, u):
                link = Chain(dve, dve_link, c * links)
                for j in range(2):
                    dve.wait_ge(x_in[j], 16 * c + 16)
                    for half in range(2):
                        link(dve.bn_stats(stats[:, 6 * half:6 * half + 6], xt[j][:, 512 * half:512 * half + 512]))
                    dve.nop(nofuse=True)
                    link(dve.bn_aggr(mv[:], stats[:]))
                    link(dve.tensor_scalar(var[:], mv[:, 1:2], LN_EPS, None, ALU.add))
                    rsqrt(dve, link, var[:], rstd[j][:], tmp[:])
                    dve.tensor_scalar(shift[j][:], mv[:, 0:1], rstd[j][:], -1.0, ALU.mult, ALU.mult)\
                       .then_inc(stats_done, 1)
                assert link.n == links
                dve.wait_ge(ln_sem, 32)
                for j in range(2):
                    dve.wait_ge(xn_done, 2 * c + j + 1)
                    dve.wait_ge(h_stored[j], 16 * c + 16)
                    dve.wait_ge(tr_done, 2 * c + j + 1)
                    dve.tensor_tensor(ht[j], xt[j], g_b[:], ALU.mult).then_inc(hg_done, 1)

            def transpose(c, u):
                for j in range(2):
                    dve.wait_ge(hi_done, 2 * c + j + 1)
                    part = slice(j * P, (j + 1) * P)
                    dve.tensor_tensor(t_lo[u][:, :, part], tps[j][:], t_hi[u][:, :, part].bitcast(F32),
                                      ALU.subtract).then_inc(lo_done, 1)

            def project(c, u, half):
                pass

            def split():
                for k in range(KD):
                    dve.wait_ge(hi_made, k + 1)
                    dve.tensor_tensor(w_lo[:, k, :], raw[:, k, :], w_hi[:, k, :].bitcast(F32), ALU.subtract)\
                       .then_inc(lo_made, 1)

            run_chunks(dve, ln, transpose, split, project)

        @block.scalar
        def _(act):
            for j in range(2):
                act.sem_inc(h_stored[j], 16)
                act.sem_inc(t_stored[j], 32)
            def ln(c, u):
                for j in range(2):
                    act.wait_ge(stats_done, 2 * c + j + 1)
                    act.activation(xt[j], xt[j], ACT.Identity, bias=shift[j][:], scale=rstd[j][:])\
                       .then_inc(xn_done, 1)

            def transpose(c, u):
                for j in range(2):
                    act.wait_ge(tr_done, 2 * c + j + 3)
                    if j == 0:
                        act.wait_ge(acc_done, NF * c + NF)
                        act.wait_ge(t_stored[u], 32 + 16 * (c - u))
                    act.activation(t_hi[u][:, :, j * P:(j + 1) * P], tps[j][:], ACT.Copy).then_inc(hi_done, 1)
                    act.wait_ge(h_done, 2 * c + j + 1)
                    act.dma_start(h_dram[bass.ds((2 * c + j) * P, P), :], ht[j]).then_inc(h_stored[j], 16)
                act.wait_ge(hi_done, 2 * c + 2)
                act.dma_start(ht_hi_dram[bass.ds(c, 1)].rearrange("o p n -> (o p) n"),
                              k_hi[:, u, :].bitcast(F32)).then_inc(t_stored[u], 16)
                act.wait_ge(lo_done, 2 * c + 4)
                act.dma_start(ht_lo_dram[bass.ds(c, 1)].rearrange("o p n -> (o p) n"),
                              k_lo[:, u, :].bitcast(F32)).then_inc(t_stored[u], 16)

            def project(c, u, half):
                for f in range(half * FT, (half + 1) * FT):
                    act.wait_ge(acc_done, 2 * NF + NF * c + f + 1)
                    act.wait_ge(go, 1)
                    dst = x_all if f < FT else y_all
                    act.activation(dst[:, f % FT, bass.ds(c * CH, CH)], acc[f % 4][:, 0:CH], ACT.Copy)\
                       .then_inc(acc_free, 1)

            def split():
                for k in range(KD):
                    act.wait_ge(w_in_sem[k], 16)
                    act.activation(w_hi[:, k, :], raw[:, k, :], ACT.Copy).then_inc(hi_made, 1)
                act.wait_ge(lo_made, KD)

            run_chunks(act, ln, transpose, split, project)
            for c in range(2):
                act.wait_ge(t_stored[c], 32 + 32 * (NC // 2))
            for j in range(2):
                act.wait_ge(h_stored[j], 16 + 16 * NC)

        @block.tensor
        def _(pe):
            pe.sem_inc(tr_done, 2)
            pe.sem_inc(lo_done, 2)
            pe.sem_inc(acc_done, 2 * NF)
            pe.sem_inc(acc_free, 4)
            pe.wait_ge(id_sem, 3)

            def ln(c, u):
                pass

            def transpose(c, u):
                for j in range(2):
                    pe.wait_ge(h_done, 2 * c + j + 1)
                    pe.wait_ge(lo_done, 2 * c + j + 1)
                    for k in range(KD):
                        last = pe.transpose(tps[j][:, k, :], ht[j][:, k * P:(k + 1) * P], ident[:])
                    last.then_inc(tr_done, 1)

            def project(c, u, half):
                if half == 0:
                    pe.wait_ge(lo_done, 2 * c + 4)
                for f in range(half * FT, (half + 1) * FT):
                    pe.wait_ge(acc_free, NF * c + f + 1)
                    cols = slice(f * P, (f + 1) * P)
                    for k in range(KD):
                        if f == 0:
                            pe.wait_ge(lo_made, k + 1)
                        last = three_pass(pe, acc[f % 4][:, 0:CH], (w_hi[:, k, cols], w_lo[:, k, cols]),
                                          (t_hi[u][:, k, :], t_lo[u][:, k, :]), k == 0, k == KD - 1)
                    last.then_inc(acc_done, 1)

            run_chunks(pe, ln, transpose, lambda: None, project)



def project_qkv(nc, raw, q_g, k_g, rope, identr, ht_hi_dram, ht_lo_dram, k_hi, k_lo, v_all, q_dram):
    with ExitStack() as ctx:
        sb = lambda n, s, d=F32: ctx.enter_context(nc.sbuf_tensor(n, s, d))
        ps = lambda n, s, d=F32: ctx.enter_context(nc.psum_tensor(n, s, d))
        sem = ctx.enter_context(semaphores(nc, "b_"))
        w_hi = sb("wq_hi", [P, KD, QKVW], F32R)
        w_lo = sb("wq_lo", [P, KD, QKVW], F32R)
        g_b = sb("qk_g_b", [P, 2, HD])
        c_hi = [sb(f"c_hi{u}", [P, KD, P], F32R) for u in range(2)]
        c_lo = [sb(f"c_lo{u}", [P, KD, P], F32R) for u in range(2)]
        flat = raw[:].rearrange("p k n -> p (k n)")
        taken = 0

        def room(n):
            nonlocal taken
            taken += n
            return flat[:, taken - n:taken]

        sq = room(QKW)
        rb = room(QKW)
        xr = [room(QKW) for u in range(2)]
        rt = [room(QKW) for u in range(2)]
        tab = room(TPS * 2 * HD).rearrange("p (t c d) -> p t c d", t=TPS, c=2)
        q_t = room(NQ * P).bitcast(F32R).rearrange("p (h t) -> p h t", h=NQ)
        ss = sb("ss", [P, NH])
        ms = sb("ms", [P, NH])
        tmp = sb("tmp_qk", [P, NH])
        rs = sb("rs", [P, NH])
        q_st = [sb(f"q_st{u}", [P, NQ, 2, HD], F32R) for u in range(2)]
        k_st = [sb(f"k_st{u}", [P, 2, NKV, 2, HD], F32R) for u in range(2)]
        pj = [ps(f"pj{u}", [P, 1024]) for u in range(2)]
        tr = ps("tr", [P, NQ + 2 * NKV, P], F32R)

        go = sem("go_b")
        rows_in = sem("qk_rows_loaded")
        hi_made = sem("wq_hi_made")
        lo_made = sem("wq_lo_made")
        c_in = [sem(f"chunk_loaded{u}") for u in range(2)]
        dve_link = sem("dve_link_b")
        pj_done = sem("pj_done")
        sq_done = sem("sq_done")
        ss_done = sem("ss_done")
        v_done = sem("v_done")
        xr_done = sem("xr_done")
        xg_done = sem("xg_done")
        a_done = sem("rope_a_done")
        b_done = sem("rope_b_done")
        rt_done = sem("rope_done")
        hi_done = sem("qk_hi_done")
        lo_done = sem("qk_lo_done")
        tr_done = sem("qk_transposed")
        qt_done = sem("q_t_done")
        kt_done = sem("k_t_done")
        q_stored = sem("q_stored")
        block = ctx.enter_context(nc.Block())

        def run_tiles(eng, front, back, stage):
            front(0, 0)
            front(1, 1)
            stage(0, 0)
            with eng.Fori(0, NT // 2 - 1) as n:
                for u in range(2):
                    front(2 * n + u + 2, u)
                    stage(2 * n + u + 1, 1 - u)
                    back(2 * n + u, u)
            stage(NT - 1, 1)
            back(NT - 2, 0)
            back(NT - 1, 1)

        def skip(t, u):
            pass

        @block.sync
        def _(sp):
            sp.sem_inc(go, 1)

            def load(n, u):
                for dst, src in ((c_hi, ht_hi_dram), (c_lo, ht_lo_dram)):
                    part = src[bass.ds(n, 1)].rearrange("o p (k t) -> (o p) k t", k=KD)[:, :, u * P:(u + 1) * P]
                    sp.dma_start(dst[u][:].bitcast(F32), part).then_inc(c_in[u], 16)

            load(0, 0)
            load(0, 1)
            sp.dma_start(g_b[:, 0, :], row(q_g[0], HD)).then_inc(rows_in, 16)
            sp.dma_start(g_b[:, 1, :], row(k_g[0], HD)).then_inc(rows_in, 16)
            sp.wait_ge(lo_made, KD)
            sp.dma_start(tab.rearrange("p t c d -> p (t c d)"), rope).then_inc(rows_in, 16)
            with sp.Fori(1, NT // 2) as n:
                for u in range(2):
                    sp.wait_ge(pj_done, 2 * n + u - 1)
                    load(n, u)

        @block.scalar
        def _(act):
            act.sem_inc(q_stored, 16)
            act.sem_inc(v_done, 2)
            act.sem_inc(qt_done, 1)
            for k in range(KD):
                act.activation(w_hi[:, k, :], raw[:, k, :], ACT.Copy).then_inc(hi_made, 1)
            act.wait_ge(lo_made, KD)

            def front(t, u):
                act.wait_ge(pj_done, t + 1)
                act.wait_ge(ss_done, t + 1)
                act.activation(sq, pj[u][:, 0:QKW], ACT.Square).then_inc(sq_done, 1)
                act.activation(v_all[:, bass.ds(t, 1), :].rearrange("p o n -> p (o n)"), pj[u][:, QKW:QKVW],
                               ACT.Copy).then_inc(v_done, 1)

            def stage(t, u):
                act.wait_ge(rt_done, t + 2)
                act.wait_ge(tr_done, t + 1)
                rows = rt[u].rearrange("p (h d) -> p h d", h=NH)
                act.activation(q_st[u][:, :, 0, :], rows[:, 0:NQ, :], ACT.Copy)
                act.activation(k_st[u][:, 0], rows[:, NQ:NH, :].unsqueeze(2).broadcast_to([P, NKV, 2, HD]), ACT.Copy)\
                   .then_inc(hi_done, 1)

            def back(t, u):
                act.wait_ge(tr_done, t + 3)
                act.wait_ge(q_stored, 16 * t + 16)
                act.activation(q_t, tr[:, 0:NQ, :].bitcast(F32), ACT.Copy).then_inc(qt_done, 1)
                act.wait_ge(qt_done, t + 2)
                act.dma_start(q_dram[bass.ds(t, 1)].rearrange("o p n -> (o p) n"),
                              q_t.rearrange("p h t -> p (h t)").bitcast(F32)).then_inc(q_stored, 16)

            run_tiles(act, front, back, stage)
            act.wait_ge(q_stored, 16 + 16 * NT)

        @block.vector
        def _(dve):
            dve.sem_inc(ss_done, 1)
            dve.sem_inc(xr_done, 2)
            dve.sem_inc(rt_done, 1)
            dve.sem_inc(kt_done, 1)
            for k in range(KD):
                dve.wait_ge(hi_made, k + 1)
                dve.tensor_tensor(w_lo[:, k, :], raw[:, k, :], w_hi[:, k, :].bitcast(F32), ALU.subtract)\
                   .then_inc(lo_made, 1)
            dve.wait_ge(rows_in, 48)
            links = 1 + RSQRT_LINKS_WIDE

            def front(t, u):
                link = Chain(dve, dve_link, t * links)
                dve.wait_ge(sq_done, t + 1)
                dve.tensor_reduce(ss[:], sq.rearrange("p (h d) -> p h d", h=NH), AX, ALU.add).then_inc(ss_done, 1)
                dve.wait_ge(ss_done, t + 2)
                link(dve.tensor_scalar(ms[:], ss[:], 1.0 / HD, QK_EPS, ALU.mult, ALU.add))
                rsqrt(dve, link, ms[:], rs[:], tmp[:])
                assert link.n == links
                dve.wait_ge(b_done, t + 1)
                dve.wait_ge(v_done, t + 3)
                dve.tensor_tensor(xr[u].rearrange("p (h d) -> p h d", h=NH),
                                  pj[u][:, 0:QKW].rearrange("p (h d) -> p h d", h=NH),
                                  rs[:].unsqueeze(2).broadcast_to([P, NH, HD]), ALU.mult).then_inc(xr_done, 1)

            def stage(t, u):
                dve.wait_ge(xg_done, t + 1)
                dve.wait_ge(lo_done, t + 1)
                dve.tensor_tensor(rt[u].rearrange("p (h d) -> p h d", h=NH),
                                  xr[u].rearrange("p (h d) -> p h d", h=NH),
                                  tab[:, bass.ds(t % TPS, 1), 0, :].broadcast_to([P, NH, HD]), ALU.mult).then_inc(a_done, 1)
                dve.wait_ge(a_done, t + 1)
                dve.wait_ge(b_done, t + 3)
                dve.tensor_tensor(rt[u], rt[u], rb, ALU.add).then_inc(rt_done, 1)

            def back(t, u):
                dve.wait_ge(tr_done, t + 3)
                dve.wait_ge(go, 1)
                dve.tensor_copy(k_hi[:, :, bass.ds(t * P, P)], tr[:, NQ:NQ + NKV, :].bitcast(F32))
                dve.tensor_copy(k_lo[:, :, bass.ds(t * P, P)], tr[:, NQ + NKV:, :].bitcast(F32)).then_inc(kt_done, 1)

            run_tiles(dve, front, back, stage)

        @block.gpsimd
        def _(pool):
            pool.sem_inc(b_done, 2)
            pool.sem_inc(lo_done, 2)
            pool.wait_ge(lo_made, KD)
            pool.wait_ge(rows_in, 48)

            def front(t, u):
                x5 = xr[u].rearrange("p (h s f d) -> p h s f d", h=NH, s=2, f=2)
                b5 = rb.rearrange("p (h s f d) -> p h s f d", h=NH, s=2, f=2)
                s5 = tab[:, bass.ds(t % TPS, 1), 1, :].rearrange("p o (s f d) -> p o s f d", s=2, f=2)
                pool.wait_ge(xr_done, t + 3)
                heads = xr[u].rearrange("p (h d) -> p h d", h=NH)
                for c, a, b in ((0, 0, NQ), (1, NQ, NH)):
                    last = pool.tensor_tensor(heads[:, a:b], heads[:, a:b],
                                              g_b[:, c:c + 1, :].broadcast_to([P, b - a, HD]), ALU.mult)
                last.then_inc(xg_done, 1)
                pool.wait_ge(xg_done, t + 1)
                pool.wait_ge(rt_done, t + 1)
                pool.wait_ge(go, 1)
                for f in range(2):
                    last = pool.tensor_tensor(b5[:, :, :, f, :], x5[:, :, :, 1 - f, :],
                                              s5[:, :, :, f, :].broadcast_to([P, NH, 2, HD // 4]), ALU.mult)
                last.then_inc(b_done, 1)

            def stage(t, u):
                rows = rt[u].rearrange("p (h d) -> p h d", h=NH)
                pool.wait_ge(hi_done, t + 1)
                pool.tensor_tensor(q_st[u][:, :, 1, :], rows[:, 0:NQ, :], q_st[u][:, :, 0, :].bitcast(F32), ALU.subtract)
                pool.tensor_tensor(k_st[u][:, 1], rows[:, NQ:NH, :].unsqueeze(2).broadcast_to([P, NKV, 2, HD]),
                                   k_st[u][:, 0].bitcast(F32), ALU.subtract).then_inc(lo_done, 1)

            run_tiles(pool, front, skip, stage)

        @block.tensor
        def _(pe):
            pe.sem_inc(tr_done, 2)

            def front(t, u):
                pe.wait_ge(c_in[u], 16 * (t - u) + 32)
                pe.wait_ge(v_done, t + 1)
                pe.wait_ge(xr_done, t + 1)
                for a, b in ((0, QW), (QW, QKVW)):
                    for k in range(KD):
                        if a == 0:
                            pe.wait_ge(lo_made, k + 1)
                        last = three_pass(pe, pj[u][:, a:b], (c_hi[u][:, k, :], c_lo[u][:, k, :]),
                                          (w_hi[:, k, a:b], w_lo[:, k, a:b]), k == 0, k == KD - 1)
                last.then_inc(pj_done, 1)

            def back(t, u):
                pe.wait_ge(lo_done, t + 3)
                pe.wait_ge(qt_done, t + 1)
                pe.wait_ge(kt_done, t + 1)
                for h in range(NQ):
                    pe.transpose(tr[:, h, :], q_st[u][:, h].rearrange("p c d -> p (c d)"), identr[:])
                for c in range(2):
                    for h in range(NKV):
                        last = pe.transpose(tr[:, NQ + NKV * c + h, :], k_st[u][:, c, h].rearrange("p c d -> p (c d)"),
                                            identr[:])
                last.then_inc(tr_done, 1)

            run_tiles(pe, front, back, skip)


def lru(nc, conv_w, conv_b, lru_wa, lru_ba, lru_wx, lru_bx, lru_lambda, x_all, y_all):
    with ExitStack() as ctx:
        sb = lambda n, s, d=F32: ctx.enter_context(nc.sbuf_tensor(n, s, d))
        sem = ctx.enter_context(semaphores(nc, "c_"))
        UNITS = [(s, f) for s in range(SEQS) for f in range(FT)]
        NG = 4
        gw = sb("gate_w", [P, FT, NG, P])
        gb = sb("gate_b", [P, NG, FT])
        cw = sb("conv_w_t", [P, TAPS, FT])
        cb = sb("conv_b_t", [P, FT])
        lam = sb("lam_t", [P, 2, FT])
        neg = sb("neg_lam", [P, 2, FT])
        mag = sb("abs_lam", [P, 2, FT])
        e = sb("exp_lam", [P, 2, FT])
        z = sb("z_lam", [P, 2, FT])
        z2 = sb("z2_lam", [P, 2, FT])
        ser = sb("series", [P, 2, FT])
        decay = sb("decay", [P, 2, FT])
        ndecay = sb("ndecay", [P, 2, FT])
        xc = [sb(f"xc{u}", [P, SEQ]) for u in range(2)]
        r = [sb(f"r{u}", [P, 2, SEQ]) for u in range(3)]
        i = [sb(f"i{u}", [P, 2, SEQ]) for u in range(3)]
        th = [sb(f"th{u}", [P, 2, SEQ]) for u in range(3)]
        a2 = sb("a2", [P, 2, SEQ])
        gp = ctx.enter_context(nc.psum_tensor("gp", [P, NG, SEQ], F32))

        gw_zero = sem("gate_w_zeroed")
        rows_in = sem("lru_rows_loaded")
        gw_in = sem("gate_w_loaded")
        dve_link = sem("dve_link_c")
        act_link = sem("act_link_c")
        mag_done = sem("abs_lam_done")
        e_done = sem("exp_lam_done")
        decay_done = sem("decay_done")
        xc_done = sem("conv_done")
        gates_done = sem("gates_done")
        sig_done = sem("sigmoids_done")
        th_done = sem("tanh_done")
        a_done = sem("a_done")
        ix_done = sem("ix_done")
        a2_done = sem("a2_done")
        w_done = sem("one_minus_a2_done")
        root_done = sem("root_done")
        scans_done = sem("scans_done")
        sum_done = sem("sum_done")
        gelu_done = sem("gelu_done")
        out_done = sem("lru_done")
        block = ctx.enter_context(nc.Block())

        @block.sync
        def _(sp):
            with nc.allow_non_contiguous_dma("small per-feature vectors"):
                sp.dma_start(lam[:], lru_lambda[0].rearrange("d (f p) -> p d f", p=P)).then_inc(rows_in, 16)
                for w in range(TAPS):
                    sp.dma_start(cw[:, w], conv_w[0, w].rearrange("(f p) -> p f", p=P)).then_inc(rows_in, 16)
                sp.dma_start(cb[:], conv_b[0].rearrange("(f p) -> p f", p=P)).then_inc(rows_in, 16)
                for n, src in enumerate((lru_ba, lru_bx)):
                    for d in range(2):
                        sp.dma_start(gb[:, 2 * d + n], src[0, d].rearrange("h i -> (h i)").rearrange("(f p) -> p f", p=P))\
                          .then_inc(rows_in, 16)
            sp.wait_ge(gw_zero, 1)
            for n, src in enumerate((lru_wa, lru_wx)):
                for d in range(2):
                    for c in range(2):
                        part = src[0, d].rearrange("(f c) i j -> c i f j", c=2)[c]
                        sp.dma_start(gw[c * LHD:(c + 1) * LHD, :, 2 * d + n, c * LHD:(c + 1) * LHD], part)\
                          .then_inc(gw_in, 16)

        def run_units(conv, front, w, back, out):
            conv(0)
            conv(1)
            front(0)
            for n in range(len(UNITS)):
                w(n)
                if n:
                    out(n - 1)
                if n + 1 < len(UNITS):
                    front(n + 1)
                if n + 2 < len(UNITS):
                    conv(n + 2)
                back(n)
            out(len(UNITS) - 1)

        def skip(n):
            pass

        @block.vector
        def _(dve):
            link = Chain(dve, dve_link)
            dve.wait_ge(rows_in, 160)
            link(dve.tensor_scalar(neg[:], lam[:], -1.0, None, ALU.mult))
            dve.tensor_tensor(mag[:], lam[:], neg[:], ALU.max).then_inc(mag_done, 1)
            dve.wait_ge(e_done, 1)
            link(dve.tensor_scalar(z2[:], e[:], 2.0, None, ALU.add))
            link(dve.reciprocal(z2[:], z2[:]))
            link(dve.tensor_tensor(z[:], e[:], z2[:], ALU.mult))
            link(dve.tensor_tensor(z2[:], z[:], z[:], ALU.mult))
            link(dve.tensor_scalar(ser[:], z2[:], 1 / 19, 1 / 17, ALU.mult, ALU.add))
            for odd in range(15, 0, -2):
                link(dve.tensor_tensor(ser[:], ser[:], z2[:], ALU.mult))
                link(dve.tensor_scalar(ser[:], ser[:], 1 / odd, None, ALU.add))
            link(dve.tensor_tensor(ser[:], ser[:], z[:], ALU.mult))
            link(dve.tensor_scalar(neg[:], neg[:], 0.0, LRU_C, ALU.max, ALU.mult))
            link(dve.scalar_tensor_tensor(decay[:], ser[:], 2.0 * LRU_C, neg[:], ALU.mult, ALU.add))
            dve.tensor_scalar(ndecay[:], decay[:], -1.0, None, ALU.mult).then_inc(decay_done, 1)

            def conv(n):
                s, f = UNITS[n]
                c = xc[n % 2]
                xs = x_all[:, f, s * SEQ:(s + 1) * SEQ]
                if n >= 2:
                    dve.wait_ge(ix_done, n - 1)
                    dve.wait_ge(gates_done, NG * (n - 1))
                link(dve.tensor_scalar(c[:], xs, cw[:, 2, f:f + 1], cb[:, f:f + 1], ALU.mult, ALU.add))
                link(dve.scalar_tensor_tensor(c[:, 2:], xs[:, :SEQ - 2], cw[:, 0, f:f + 1], c[:, 2:],
                                              ALU.mult, ALU.add))
                link(dve.scalar_tensor_tensor(c[:, 1:], xs[:, :SEQ - 1], cw[:, 1, f:f + 1], c[:, 1:],
                                              ALU.mult, ALU.add))
                dve.scalar_tensor_tensor(c[:, :SEQ - 1], xs[:, 1:], cw[:, 3, f:f + 1], c[:, :SEQ - 1],
                                         ALU.mult, ALU.add).then_inc(xc_done, 1)

            def w(n):
                u = n % 3
                dve.wait_ge(a2_done, n + 1)
                dve.wait_ge(th_done, 2 * n + 2)
                dve.scalar_tensor_tensor(th[u][:], a2[:], 1.0, th[u][:], ALU.add, ALU.mult).then_inc(w_done, 1)

            def back(n):
                u = n % 3
                dve.wait_ge(root_done, n + 1)
                dve.wait_ge(ix_done, n + 1)
                link(dve.tensor_tensor(i[u][:], i[u][:], th[u][:], ALU.mult))
                dve.tensor_tensor_scan(i[u][:, 0], r[u][:, 0], i[u][:, 0], 0.0, ALU.mult, ALU.add)
                dve.tensor_tensor_scan(i[u][:, 1, ::-1], r[u][:, 1, ::-1], i[u][:, 1, ::-1], 0.0, ALU.mult, ALU.add)\
                   .then_inc(scans_done, 1)

            def out(n):
                s, f = UNITS[n]
                ys = y_all[:, f, s * SEQ:(s + 1) * SEQ]
                dve.wait_ge(sum_done, n + 1)
                dve.wait_ge(gelu_done, 1)
                dve.tensor_tensor(ys, ys, i[n % 3][:, 0], ALU.mult).then_inc(out_done, 1)

            run_units(conv, skip, w, back, out)

        @block.gpsimd
        def _(pool):
            pool.memset(gw[:], 0.0).then_inc(gw_zero, 1)

            def front(n):
                u = n % 3
                pool.wait_ge(a_done, n + 1)
                if n:
                    pool.wait_ge(w_done, n)
                pool.tensor_tensor(a2[:], r[u][:], r[u][:], ALU.mult).then_inc(a2_done, 1)
                pool.wait_ge(sig_done, NG * n + NG)
                pool.wait_ge(xc_done, n + 1)
                for d in range(2):
                    last = pool.tensor_tensor(i[u][:, d], i[u][:, d], xc[n % 2][:], ALU.mult)
                last.then_inc(ix_done, 1)

            def back(n):
                u = n % 3
                pool.wait_ge(scans_done, n + 1)
                pool.tensor_tensor(i[u][:, 0], i[u][:, 0], i[u][:, 1], ALU.add).then_inc(sum_done, 1)

            run_units(skip, front, skip, back, skip)

        @block.scalar
        def _(act):
            act.wait_ge(mag_done, 1)
            act.activation(e[:], mag[:], ACT.Exp, scale=-1.0).then_inc(e_done, 1)
            act.activation(y_all[:], y_all[:], ACT.Gelu_apprx_tanh).then_inc(gelu_done, 1)
            act.wait_ge(decay_done, 1)

            def front(n):
                s, f = UNITS[n]
                u = n % 3
                if n >= 3:
                    act.wait_ge(out_done, n - 2)
                for g in range(NG):
                    act.wait_ge(gates_done, NG * n + g + 1)
                    dst = (r, i)[g % 2][u][:, g // 2]
                    act.activation(dst, gp[:, g], ACT.Sigmoid, bias=gb[:, g, f:f + 1]).then_inc(sig_done, 1)
                act.wait_ge(sig_done, NG * n + NG)
                for d in range(2):
                    act.activation(th[u][:, d], r[u][:, d], ACT.Tanh, scale=decay[:, d, f:f + 1]).then_inc(th_done, 1)
                act.wait_ge(th_done, 2 * n + 2)
                for d in range(2):
                    last = act.activation(r[u][:, d], r[u][:, d], ACT.Exp, scale=ndecay[:, d, f:f + 1])
                last.then_inc(a_done, 1)

            def back(n):
                act.wait_ge(w_done, n + 1)
                act.activation(th[n % 3][:], th[n % 3][:], ACT.Sqrt).then_inc(root_done, 1)

            run_units(skip, front, skip, back, skip)

        @block.tensor
        def _(pe):
            pe.wait_ge(gw_in, 128)

            def front(n):
                s, f = UNITS[n]
                u = n % 2
                pe.wait_ge(xc_done, n + 1)
                for g in range(NG):
                    if n:
                        pe.wait_ge(sig_done, NG * (n - 1) + g + 1)
                    for c in range(2):
                        last = pe.matmul(gp[:, g, c * 512:(c + 1) * 512], gw[:, f, g, :], xc[u][:, c * 512:(c + 1) * 512],
                                         start=True, stop=True)
                    last.then_inc(gates_done, 1)

            run_units(skip, front, skip, skip, skip)


def need(eng, sem, value):
    if not (isinstance(value, int) and value < 1):
        eng.wait_ge(sem, value)


def attend(nc, w_out, attn_g, lru_g, ln_g, ln_b, router_wg, router_bg, router_we, router_be, ident,
           k_hi, k_lo, v_all, y_all, h_dram, q_dram, h1_dram, logits):
    with ExitStack() as ctx:
        sb = lambda n, s, d=F32: ctx.enter_context(nc.sbuf_tensor("d_" + n, s, d))
        ps = lambda n, s, d=F32: ctx.enter_context(nc.psum_tensor("d_" + n, s, d))
        sem = ctx.enter_context(semaphores(nc, "d_"))
        GQ = NQ // NKV
        HALF = TPS // 2
        w_hi = sb("wo_hi", [P, KD, D], F32R)
        w_lo = sb("wo_lo", [P, KD, D], F32R)
        out_g = sb("out_g", [P, KD])
        g_b = sb("ln1_g_b", [P, D])
        b_b = sb("ln1_b_b", [P, D])
        wr = sb("router_w", [P, KD, RW])
        rb_b = sb("router_b", [P, RW])
        ones = sb("ones", [P, 2])
        q_t = [sb(f"q_tile{u}", [P, NQ, P], F32R) for u in range(2)]
        pr = [sb(f"probs{j}", [P, SEQ]) for j in range(2)]
        pt = [sb(f"probs_t{j}", [P, TPS, P]) for j in range(2)]
        mx = sb("mx", [P, 2, NQ])
        nm = sb("neg_max", [P, 2, NQ])
        rsum = sb("rsum", [P, 2, NQ])
        rinv = sb("rinv", [P, NQ])
        o_n = sb("o_n", [P, QW])
        junk = sb("junk", [P, QW])
        m_hi = sb("m_hi", [P, KD, P], F32R)
        m_lo = sb("m_lo", [P, KD, P], F32R)
        lsq = [sb(f"lru_sq{u}", [P, FT, P]) for u in range(2)]
        lvar = sb("lru_var", [P, NT])
        lrstd = sb("lru_rstd", [P, NT])
        ltmp = sb("lru_tmp", [P, NT])
        ssa = sb("ssa", [P, 1])
        var = sb("var_a", [P, 1])
        rr = sb("rstds", [P, 2])
        tmp2 = sb("tmp_a", [P, 1])
        hb = sb("h_tile", [P, D])
        s_t = sb("s_tile", [P, D])
        h1 = sb("h1_tile", [P, D])
        h1t = sb("h1_t", [P, KD, P])
        stats = sb("stats1", [P, 12])
        mv = sb("mv1", [P, 2])
        var1 = sb("var1", [P, 1])
        tmp1 = sb("tmp1", [P, 1])
        rstd1 = sb("rstd1", [P, 1])
        shift1 = sb("shift1", [P, 1])
        raw = [s_t, h1]
        s_ps = [ps(f"s_ps{j}", [P, SEQ]) for j in range(2)]
        pt_ps = [ps(f"pt_ps{c}", [P, HALF, P]) for c in range(2)]
        o_ps = ps("o_ps", [P, QW])
        m_ps = ps("m_ps", [P, 512])

        rows_in = sem("rows_loaded_d")
        raw_in = [sem(f"wo_raw_loaded{j}") for j in range(2)]
        ones_made = sem("ones_made")
        act_link = sem("act_link_d")
        dve_link = sem("dve_link_d")
        hi_made = sem("wo_hi_made")
        lo_made = sem("wo_lo_made")
        q_in = [sem(f"q_loaded{u}") for u in range(2)]
        s_done = sem("scores_done")
        mx_done = sem("max_done")
        nm_done = sem("neg_max_done")
        p_done = sem("probs_done")
        tr_done = [sem(f"probs_transposed{c}") for c in range(2)]
        pt_done = [sem(f"probs_t_done{c}") for c in range(2)]
        o_done = sem("o_done")
        rinv_done = sem("rinv_done")
        on_done = sem("o_norm_done")
        ssa_done = sem("ssa_done")
        m_done = sem("m_bank_written")
        m_free = sem("m_bank_read")
        late_done = sem("m_bank_written_late")
        late_free = sem("m_bank_read_late")
        mh_done = sem("m_hi_done")
        lh_done = sem("lru_hi_done")
        lsq_done = sem("lru_sq_done")
        lss_done = sem("lru_sq_summed")
        lr_link = sem("lru_rstd_link")
        h_in = sem("h_loaded")
        ah_done = sem("alpha_h_done")
        ln_done = sem("ln1_stats_done")
        xn_done = sem("ln1_normalised")
        hg_done = sem("ln1_gain_done")
        h1_done = sem("h1_done")
        h1_stored = sem("h1_stored")
        USES = 5
        LATE = 3
        block = ctx.enter_context(nc.Block())

        def run_heads(eng, first, head, post, late):
            def tile(t, u, stage=2, is_last=False):
                for h in range(NQ):
                    nxt = [(t, u, i) if i < NQ else None if is_last else (t + 1, 1 - u, i - NQ) for i in (h + 1, h + 2)]
                    head(t, u, h, nxt, stage)
                    if stage == 2 and h in range(1, LATE + 1):
                        late(t - 2, h - 1, False)

            first()
            tile(0, 0, stage=0)
            tile(1, 1, stage=1)
            with eng.Fori(1, NT // 2 - 1) as n:
                tile(2 * n, 0)
                tile(2 * n + 1, 1)
            tile(NT - 2, 0)
            tile(NT - 1, 1, is_last=True)
            for step in range(-1, NQ):
                post(NT - 1, 1, step)
                if step in range(1, LATE + 1):
                    late(NT - 2, step - 1, False)
            for step in range(LATE):
                late(NT - 1, step, True)

        @block.sync
        def _(sp):
            def load_q(t, u):
                sp.dma_start(q_t[u][:].rearrange("p h t -> p (h t)").bitcast(F32),
                             q_dram[bass.ds(t, 1)].rearrange("o p n -> (o p) n")).then_inc(q_in[u], 16)

            def load_h(t):
                sp.dma_start(hb[:], h_dram[bass.ds(t * P, P), :]).then_inc(h_in, 16)

            def store_h1(t):
                sp.wait_ge(h1_done, 2 * t + 2)
                sp.dma_start(h1_dram[bass.ds(t * P, P), :], h1[:]).then_inc(h1_stored, 16)

            sp.sem_inc(h1_stored, 16)
            load_q(0, 0)
            load_q(1, 1)
            load_h(0)
            with nc.allow_non_contiguous_dma("small per-feature vectors and router columns"):
                sp.dma_start(out_g[:, 0:FT], attn_g[0].rearrange("(f p) -> p f", p=P)).then_inc(rows_in, 16)
                sp.dma_start(out_g[:, FT:KD], lru_g[0].rearrange("(f p) -> p f", p=P)).then_inc(rows_in, 16)
                sp.dma_start(wr[:, :, 0:G], router_wg[0].rearrange("(k p) g -> p k g", p=P)).then_inc(rows_in, 16)
                sp.dma_start(wr[:, :, G:RW], router_we[0].rearrange("(k p) g e -> p k (g e)", p=P)).then_inc(rows_in, 16)
            sp.dma_start(rb_b[:, 0:G], row(router_bg[0], G)).then_inc(rows_in, 16)
            sp.dma_start(rb_b[:, G:RW], row(router_be[0].rearrange("g e -> (g e)"), NE)).then_inc(rows_in, 16)
            sp.dma_start(g_b[:], row(ln_g[0], D)).then_inc(rows_in, 16)
            sp.dma_start(b_b[:], row(ln_b[0], D)).then_inc(rows_in, 16)
            for k in range(KD):
                need(sp, lo_made, k - 1)
                sp.dma_start(raw[k % 2][:], w_out[0, k * P:(k + 1) * P, :]).then_inc(raw_in[k % 2], 16)

            def during(t, u):
                if u is not None:
                    sp.wait_ge(s_done, NQ * t)
                    load_q(t + 1, u)
                sp.wait_ge(m_free, USES * (t - 1) + 5)
                load_h(t)
                store_h1(t - 1)

            with sp.Fori(0, NT // 2 - 1) as n:
                during(2 * n + 1, 0)
                during(2 * n + 2, 1)
            during(NT - 1, None)
            store_h1(NT - 1)
            sp.wait_ge(h1_stored, 16 * NT + 16)

        @block.tensor
        def _(pe):
            pe.wait_ge(ones_made, 1)
            pe.sem_inc(m_done, 1)

            def scores(t, u, h):
                n = NQ * t + h
                if h == 0:
                    pe.wait_ge(q_in[u], 8 * (t - u) + 16)
                for c in range(2):
                    out = s_ps[h % 2][:, c * 512:(c + 1) * 512]
                    keys = bass.ds((t // TPS) * SEQ + c * 512, 512)
                    pe.matmul(out, q_t[u][:, h, :], k_hi[:, h // GQ, keys], start=True, stop=False)
                    last = pe.matmul(out, q_t[u][:, h, :], k_lo[:, h // GQ, keys], start=False, stop=True)
                last.then_inc(s_done, 1)

            def head(t, u, h, nxt, stage):
                n = NQ * t + h
                pe.wait_ge(p_done, n + 1)
                for c in range(2):
                    need(pe, pt_done[c], n)
                    for j in range(HALF):
                        k = c * HALF + j
                        last = pe.transpose(pt_ps[c][:, j, :], pr[h % 2][:, k * P:(k + 1) * P], ident[:])
                    last.then_inc(tr_done[c], 1)
                if nxt[1]:
                    scores(*nxt[1])
                if stage == 0:
                    for tt in (2 * h, 2 * h + 1):
                        pe.wait_ge(lsq_done, tt + 1)
                        for k in range(FT):
                            last = pe.matmul(m_ps[:, tt:tt + 1], lsq[tt % 2][:, k, :], ones[:, 0:1], start=k == 0, stop=k == FT - 1)
                        last.then_inc(lss_done, 1)
                else:
                    post(t - 1, 1 - u, h)
                if h == 0:
                    need(pe, on_done, t)
                for k in range(TPS):
                    if k % HALF == 0:
                        pe.wait_ge(pt_done[k // HALF], n + 1)
                    v_rows = v_all[:, bass.ds((t // TPS) * TPS + k, 1), (h // GQ) * HD:(h // GQ + 1) * HD]
                    last = pe.matmul(o_ps[:, h * HD:(h + 1) * HD], pt[h % 2][:, k, :],
                                     v_rows.rearrange("p o d -> p (o d)"), start=k == 0, stop=k == TPS - 1)
                last.then_inc(o_done, 1)

            def project(first_k, half):
                for k in range(FT):
                    kk = first_k + k
                    cols = slice(half * 512, (half + 1) * 512)
                    last = three_pass(pe, m_ps[:], (m_hi[:, kk, :], m_lo[:, kk, :]),
                                      (w_hi[:, kk, cols], w_lo[:, kk, cols]), k == 0, k == FT - 1)
                last.then_inc(m_done, 1)

            def post(t, u, step):
                use = USES * t + 1
                if step == 0:
                    pe.wait_ge(on_done, t + 1)
                    for k in range(FT):
                        last = pe.transpose(m_ps[:, k * P:(k + 1) * P], o_n[:, k * P:(k + 1) * P], ident[:])
                    last.then_inc(m_done, 1)
                if step in (2, 3, 4) and not (isinstance(t, int) and t == 0):
                    pe.wait_ge(late_free, LATE * (t - 1) + step - 1)
                if step == 1:
                    pe.wait_ge(lo_made, KD)
                    pe.wait_ge(m_free, use + 1)
                    project(FT, 0)
                if step == 2:
                    pe.wait_ge(m_free, use + 2)
                    project(0, 0)
                if step == 3:
                    pe.wait_ge(m_free, use + 3)
                    project(FT, 1)
                if step == 4:
                    pe.wait_ge(m_free, use + 4)
                    project(0, 1)
            def late(t, step, alone):
                pe.wait_ge(m_free, USES * (t + 1) + 1 + (0 if alone else step + 2))
                if step > 0:
                    pe.wait_ge(late_free, LATE * t + step)
                if step < 2:
                    pe.wait_ge(h1_done, 2 * t + step + 1)
                    for j in range(FT):
                        k = step * FT + j
                        last = pe.transpose(m_ps[:, j * P:(j + 1) * P], h1[:, k * P:(k + 1) * P], ident[:])
                else:
                    pe.wait_ge(rows_in, 128)
                    for k in range(KD):
                        last = pe.matmul(m_ps[:, 0:RW], h1t[:, k, :], wr[:, k, :], start=k == 0, stop=k == KD - 1)
                last.then_inc(late_done, 1)

            run_heads(pe, lambda: (scores(0, 0, 0), scores(0, 0, 1)), head, post, late)

        @block.scalar
        def _(act):
            def exp(t, u, h):
                n = NQ * t + h
                act.wait_ge(nm_done, n + 1)
                need(act, tr_done[1], n - 1)
                act.activation(pr[h % 2][:], s_ps[h % 2][:], ACT.Exp, bias=nm[:, u, h:h + 1], scale=SCALE,
                               accum_out=rsum[:, u, h:h + 1]).then_inc(p_done, 1)

            def head(t, u, h, nxt, stage):
                n = NQ * t + h
                act.wait_ge(tr_done[0], n + 1)
                need(act, o_done, n - 1)
                act.activation(pt[h % 2][:, 0:HALF], pt_ps[0][:], ACT.Copy).then_inc(pt_done[0], 1)
                if nxt[0]:
                    exp(*nxt[0])
                if stage == 0:
                    act.wait_ge(raw_in[h % 2], 16 * (h // 2 + 1))
                    act.wait_ge(rows_in, 128)
                    act.activation(raw[h % 2][:], raw[h % 2][:], ACT.Copy, scale=out_g[:, h:h + 1]).then_inc(act_link, 1)
                    act.wait_ge(act_link, h + 1)
                    act.activation(w_hi[:, h, :], raw[h % 2][:], ACT.Copy).then_inc(hi_made, 1)
                else:
                    post(t - 1, 1 - u, h)

            def post(t, u, step):
                use = USES * t + 1
                if step == 0:
                    act.wait_ge(on_done, t + 1)
                    act.activation(junk[:], o_n[:], ACT.Square, accum_out=ssa[:]).then_inc(ssa_done, 1)
                    act.wait_ge(m_done, use + 1)
                    act.activation(m_hi[:, 0:FT], m_ps[:].rearrange("p (k t) -> p k t", k=FT), ACT.Copy)\
                       .then_inc(mh_done, 1)
                    act.activation(m_hi[:, FT:KD], y_all[:, :, bass.ds(t * P, P)], ACT.Copy).then_inc(lh_done, 1)
                    act.wait_ge(h_in, 16 * t + 16)
                    act.activation(hb[:], hb[:], ACT.Copy, scale=ALPHA).then_inc(ah_done, 1)
                if step == 6:
                    act.wait_ge(ln_done, t + 1)
                    act.activation(s_t[:], s_t[:], ACT.Identity, bias=shift1[:], scale=rstd1[:]).then_inc(xn_done, 1)

            def late(t, step, alone):
                if step < 2:
                    act.wait_ge(late_done, LATE * t + step + 1)
                    act.activation(h1t[:, step * FT:(step + 1) * FT], m_ps[:].rearrange("p (k t) -> p k t", k=FT),
                                   ACT.Copy).then_inc(late_free, 1)

            run_heads(act, lambda: exp(0, 0, 0), head, post, late)

        @block.vector
        def _(dve):
            dve.memset(ones[:], 1.0).then_inc(ones_made, 1)
            links = (2 + RSQRT_LINKS) + (4 + RSQRT_LINKS)

            def neg_max(t, u, h):
                n = NQ * t + h
                dve.wait_ge(s_done, n + 1)
                dve.tensor_reduce(mx[:, u, h:h + 1], s_ps[h % 2][:], AX, ALU.max).then_inc(mx_done, 1)
                dve.wait_ge(mx_done, n + 1)
                dve.tensor_scalar(nm[:, u, h:h + 1], mx[:, u, h:h + 1], -SCALE, None, ALU.mult).then_inc(nm_done, 1)

            def head(t, u, h, nxt, stage):
                n = NQ * t + h
                if h == 0 and stage > 0:
                    post(t - 1, 1 - u, -1)
                dve.wait_ge(tr_done[1], n + 1)
                need(dve, o_done, n - 1)
                dve.tensor_copy(pt[h % 2][:, HALF:], pt_ps[1][:]).then_inc(pt_done[1], 1)
                if nxt[1]:
                    neg_max(*nxt[1])
                if stage == 0:
                    dve.wait_ge(hi_made, h + 1)
                    dve.tensor_tensor(w_lo[:, h, :], raw[h % 2][:], w_hi[:, h, :].bitcast(F32), ALU.subtract)\
                       .then_inc(lo_made, 1)
                    if h == NQ - 1:
                        link = Chain(dve, lr_link)
                        dve.wait_ge(lss_done, NT)
                        dve.tensor_scalar(lvar[:], m_ps[:, 0:NT], 1.0 / LW, LN_EPS, ALU.mult, ALU.add).then_inc(m_free, 1)
                        dve.wait_ge(m_free, 1)
                        rsqrt(dve, link, lvar[:], lrstd[:], ltmp[:])
                else:
                    post(t - 1, 1 - u, h)

            def post(t, u, step):
                use = USES * t + 1
                if step == -1:
                    dve.wait_ge(o_done, NQ * t + NQ)
                    dve.wait_ge(p_done, NQ * t + NQ)
                    dve.reciprocal(rinv[:], rsum[:, u]).then_inc(rinv_done, 1)
                    dve.wait_ge(rinv_done, t + 1)
                    dve.tensor_tensor(o_n[:].rearrange("p (h d) -> p h d", h=NQ),
                                      o_ps[:].rearrange("p (h d) -> p h d", h=NQ),
                                      rinv[:].unsqueeze(2).broadcast_to([P, NQ, HD]), ALU.mult).then_inc(on_done, 1)
                if step == 0:
                    dve.wait_ge(lh_done, t + 1)
                    dve.nop(nofuse=True)
                    dve.tensor_tensor(m_lo[:, FT:KD], y_all[:, :, bass.ds(t * P, P)], m_hi[:, FT:KD].bitcast(F32),
                                      ALU.subtract)
                    dve.wait_ge(mh_done, t + 1)
                    dve.tensor_tensor(m_lo[:, 0:FT], m_ps[:].rearrange("p (k t) -> p k t", k=FT),
                                      m_hi[:, 0:FT].bitcast(F32), ALU.subtract).then_inc(m_free, 1)
                if step == 1:
                    link = Chain(dve, dve_link, links * t)
                    dve.nop(nofuse=True)
                    link(dve.tensor_copy(rr[:, 1:2], lrstd[:, bass.ds(t, 1)]))
                    dve.wait_ge(m_done, use + 2)
                    dve.wait_ge(ah_done, t + 1)
                    dve.scalar_tensor_tensor(s_t[:, 0:512], m_ps[:], rr[:, 1:2], hb[:, 0:512], ALU.mult, ALU.add)\
                       .then_inc(m_free, 1)
                    dve.wait_ge(ssa_done, t + 1)
                    link(dve.tensor_scalar(var[:], ssa[:], 1.0 / QW, LN_EPS, ALU.mult, ALU.add))
                    rsqrt(dve, link, var[:], rr[:, 0:1], tmp2[:])
                if step == 2:
                    dve.wait_ge(m_done, use + 3)
                    dve.wait_ge(m_free, use + 2)
                    dve.scalar_tensor_tensor(s_t[:, 0:512], m_ps[:], rr[:, 0:1], s_t[:, 0:512], ALU.mult, ALU.add)\
                       .then_inc(m_free, 1)
                if step == 3:
                    dve.wait_ge(m_done, use + 4)
                    dve.scalar_tensor_tensor(s_t[:, 512:], m_ps[:], rr[:, 1:2], hb[:, 512:], ALU.mult, ALU.add)\
                       .then_inc(m_free, 1)
                if step == 4:
                    link = Chain(dve, dve_link, links * t + 2 + RSQRT_LINKS)
                    dve.wait_ge(m_done, use + 5)
                    dve.wait_ge(m_free, use + 4)
                    dve.scalar_tensor_tensor(s_t[:, 512:], m_ps[:], rr[:, 0:1], s_t[:, 512:], ALU.mult, ALU.add)\
                       .then_inc(m_free, 1)
                    dve.wait_ge(m_free, use + 5)
                    for half in range(2):
                        link(dve.bn_stats(stats[:, 6 * half:6 * half + 6], s_t[:, 512 * half:512 * half + 512]))
                if step == 5:
                    link = Chain(dve, dve_link, links * t + 4 + RSQRT_LINKS)
                    dve.nop(nofuse=True)
                    link(dve.bn_aggr(mv[:], stats[:]))
                    link(dve.tensor_scalar(var1[:], mv[:, 1:2], LN_EPS, None, ALU.add))
                    rsqrt(dve, link, var1[:], rstd1[:], tmp1[:])
                    dve.tensor_scalar(shift1[:], mv[:, 0:1], rstd1[:], -1.0, ALU.mult, ALU.mult).then_inc(ln_done, 1)
                if step == 7:
                    dve.wait_ge(xn_done, t + 1)
                    dve.wait_ge(h1_stored, 16 * t + 16)
                    if not (isinstance(t, int) and t == 0):
                        dve.wait_ge(late_done, LATE * (t - 1) + 2)
                    for half in range(2):
                        part = slice(half * 512, (half + 1) * 512)
                        dve.tensor_tensor(h1[:, part], s_t[:, part], g_b[:, part], ALU.mult).then_inc(hg_done, 1)

            def late(t, step, alone):
                if step == 2:
                    dve.wait_ge(late_done, LATE * t + 3)
                    dve.nop(nofuse=True)
                    dve.tensor_tensor(logits[:, bass.ds(t, 1), :].rearrange("p o n -> p (o n)"), m_ps[:, 0:RW], rb_b[:],
                                      ALU.add).then_inc(late_free, 1)

            run_heads(dve, lambda: (neg_max(0, 0, 0), neg_max(0, 0, 1)), head, post, late)

        @block.gpsimd
        def _(pool):
            for t in range(NT):
                need(pool, lss_done, t - 1)
                part = y_all[:, :, t * P:(t + 1) * P]
                pool.tensor_tensor(lsq[t % 2][:], part, part, ALU.mult).then_inc(lsq_done, 1)
            pool.wait_ge(rows_in, 128)
            with pool.Fori(0, NT) as t:
                for half in range(2):
                    part = slice(half * 512, (half + 1) * 512)
                    pool.wait_ge(hg_done, 2 * t + half + 1)
                    pool.tensor_tensor(h1[:, part], h1[:, part], b_b[:, part], ALU.add).then_inc(h1_done, 1)


def load_expert(sp, exp_w1, exp_w3, exp_w2, up_raw, down_raw, e, b, loaded):
    part = lambda w: w[0][bass.ds(e, 1)].rearrange("o (k p) n -> p (o k) n", p=P)
    sp.dma_start(up_raw[:, b, :, 0:DE], part(exp_w1)).then_inc(loaded, 16)
    sp.dma_start(up_raw[:, b, :, DE:2 * DE], part(exp_w3)).then_inc(loaded, 16)
    sp.dma_start(down_raw[:, b], part(exp_w2)).then_inc(loaded, 16)


def route(nc, ident, logits, slots, weights, lists, tile_expert, split_at, pair_live, last_tile,
          exp_w1, exp_w3, exp_w2, up_w, down_w):
    with ExitStack() as ctx:
        sb = lambda n, s, d=F32: ctx.enter_context(nc.sbuf_tensor("r_" + n, s, d))
        sem = ctx.enter_context(semaphores(nc, "r_"))
        gl = logits[:, :, 0:G]
        el = logits[:, :, G:RW].rearrange("p t (g e) -> p t g e", g=G)
        top = sb("top", [P, NT])
        gd = sb("gd", [P, NT, G])
        ge = sb("ge", [P, NT, G])
        gsum = sb("gsum", [P, NT])
        gprob = sb("gprob", [P, NT])
        eq = sb("eq", [P, NT, G])
        seen = sb("seen", [P, NT])
        oh_g = sb("oh_g", [P, NT, G])
        oh_e = [sb(f"oh_e{c}", [P, NT, E_IN_G]) for c in range(2)]
        prod = sb("prod", [P, NT, G, E_IN_G])
        es = sb("es", [P, NT, E_IN_G])
        m1 = sb("m1", [P, NT])
        m2 = sb("m2", [P, NT])
        gap = sb("gap", [P, NT])
        x2 = sb("x2", [P, NT])
        hot = [sb(f"hot{c}", [P, NT, G, E_IN_G]) for c in range(2)]
        both = sb("both", [P, NT, NE])
        tri = sb("tri", [P, P])
        ones = sb("ones", [P, P])
        offs = sb("offs", [P, NT + 1, NE])
        thr_i = sb("thr_i", [P, NT], I32)
        thr = sb("thr", [P, NT])
        over = sb("over", [P, NE, NT])
        n_tiles = sb("n_tiles", [P, NE])
        upto = sb("upto", [P, NE])
        first_tile = sb("first_tile", [P, NE])
        start = sb("start", [P, NE])
        base = sb("base", [P, NT, NE])
        slot_f = sb("slot_f", [P, 2, NT])
        tile_i = sb("tile_i", [P, MT], I32)
        tile_f = sb("tile_f", [P, MT])
        past = sb("past", [P, MT, NE])
        splits = sb("splits", [P, MT])
        live = sb("live", [P, MT // 2])
        last_f = sb("last_f", [P, 1])
        exp_f = sb("exp_f", [P, MT])
        tok_i = sb("tok_i", [P, NT], I32)
        tok = sb("tok", [P, NT])
        lane_i = sb("lane_i", [P, P], I32)
        lane = sb("lane", [P, P])
        PAIRS = 2 * NT
        PARTS = 4
        part_i = [sb(f"part_i{c}", [P, PAIRS], I32) for c in range(2)]
        part_f = [sb(f"part_f{c}", [P, PAIRS]) for c in range(2)]
        hot_lane = sb("hot_lane", [P, PAIRS, P], F32R)
        hot_tile = sb("hot_tile", [P, PAIRS, MT])
        tok_tile = sb("tok_tile", [P, PAIRS, MT], F32R)
        rank_ps = ctx.enter_context(nc.psum_tensor("rank_ps", [P, NT * NE], F32))
        tot_ps = ctx.enter_context(nc.psum_tensor("tot_ps", [P, NT * NE], F32))
        list_ps = ctx.enter_context(nc.psum_tensor("list_ps", [P, MT], F32))

        dve_link = sem("dve_link")
        pool_link = sem("pool_link")
        made = sem("constants_made")
        gd_done = sem("gd_done")
        ge_done = sem("ge_done")
        gap_done = sem("gap_done")
        x2_done = sem("x2_done")
        both_done = sem("both_done")
        counted = sem("counted")
        tok_tile_done = sem("tok_tile_done")
        hot_lane_done = sem("hot_lane_done")
        listed = sem("lists_done")
        w_in = [sem(f"expert_loaded{b}") for b in range(2)]
        hi_made = sem("expert_hi_made")
        lo_made = sem("expert_lo_made")
        block = ctx.enter_context(nc.Block())

        @block.gpsimd
        def _(pool):
            link = Chain(pool, pool_link)
            pool.iota(lane_i[:], [[1, P]], base=0, channel_multiplier=0).then_inc(made, 1)
            pool.memset(ones[:], 1.0).then_inc(made, 1)
            pool.iota(thr_i[:], [[P, NT]], base=0, channel_multiplier=0).then_inc(made, 1)
            pool.iota(tile_i[:], [[1, MT]], base=0, channel_multiplier=0).then_inc(made, 1)
            pool.iota(tok_i[:], [[P, NT]], base=0, channel_multiplier=1).then_inc(made, 1)
            link(pool.memset(tri[:], 1.0))
            pool.affine_select(out=tri[:], in_=tri[:], compare_op=ALU.is_gt, fill=0.0, base=0,
                               pattern=[[1, P]], channel_multiplier=-1).then_inc(made, 1)

        @block.sync
        def _(sp):
            for e in range(2):
                load_expert(sp, exp_w1, exp_w3, exp_w2, up_w[0], down_w[0], e, e, w_in[e])
            for e in range(2):
                sp.wait_ge(w_in[e], 48)

        pieces = [[w[:, 0, k] for w in up_w] for k in range(KD)] + [[w[:, 0, k] for w in down_w] for k in range(KE)]

        @block.scalar
        def _(act):
            act.wait_ge(gd_done, 1)
            act.activation(ge[:], gd[:], ACT.Exp).then_inc(ge_done, 1)
            act.wait_ge(gap_done, 1)
            act.activation(x2[:], gap[:], ACT.Exp).then_inc(x2_done, 1)
            act.wait_ge(w_in[0], 48)
            for raw, hi, lo in pieces:
                act.activation(hi, raw, ACT.Copy).then_inc(hi_made, 1)

        @block.vector
        def _(dve):
            link = Chain(dve, dve_link)
            over_g = lambda v: v[:].unsqueeze(2).broadcast_to([P, NT, G])

            def first_hot(out):
                link(dve.tensor_copy(out[:, :, 0], eq[:, :, 0]))
                link(dve.tensor_copy(seen[:], eq[:, :, 0]))
                for j in range(1, G):
                    link(dve.scalar_tensor_tensor(out[:, :, j], seen[:], 0.5, eq[:, :, j], ALU.is_lt, ALU.mult))
                    link(dve.tensor_tensor(seen[:], seen[:], eq[:, :, j], ALU.max))

            link(dve.tensor_reduce(top[:], gl, AX, ALU.max))
            dve.tensor_tensor(gd[:], gl, over_g(top), ALU.subtract).then_inc(gd_done, 1)
            link(dve.tensor_tensor(eq[:], gl, over_g(top), ALU.is_equal))
            first_hot(oh_g)
            dve.wait_ge(ge_done, 1)
            link(dve.tensor_reduce(gsum[:], ge[:], AX, ALU.add))
            link(dve.reciprocal(gprob[:], gsum[:]))
            group_hot = oh_g[:].unsqueeze(3).broadcast_to([P, NT, G, E_IN_G])
            link(dve.tensor_tensor(prod[:], el, group_hot, ALU.mult))
            link(dve.tensor_reduce(es[:], prod[:].rearrange("p t g e -> p t e g"), AX, ALU.add))
            link(dve.tensor_reduce(m1[:], es[:], AX, ALU.max))
            link(dve.tensor_tensor(eq[:], es[:], over_g(m1), ALU.is_equal))
            first_hot(oh_e[0])
            link(dve.scalar_tensor_tensor(es[:], oh_e[0][:], -3e38, es[:], ALU.mult, ALU.add))
            link(dve.tensor_reduce(m2[:], es[:], AX, ALU.max))
            link(dve.tensor_tensor(eq[:], es[:], over_g(m2), ALU.is_equal))
            first_hot(oh_e[1])
            dve.tensor_tensor(gap[:], m2[:], m1[:], ALU.subtract).then_inc(gap_done, 1)
            for c in range(2):
                link(dve.tensor_tensor(hot[c][:], group_hot, oh_e[c][:].unsqueeze(2).broadcast_to([P, NT, G, E_IN_G]),
                                       ALU.mult))
            dve.tensor_tensor(both[:], hot[0][:].rearrange("p t g e -> p t (g e)"),
                              hot[1][:].rearrange("p t g e -> p t (g e)"), ALU.add).then_inc(both_done, 1)
            dve.wait_ge(x2_done, 1)
            link(dve.tensor_scalar(m1[:], x2[:], 1.0, None, ALU.add))
            link(dve.reciprocal(m2[:], m1[:]))
            link(dve.tensor_tensor(weights[:, 0], m2[:], gprob[:], ALU.mult))
            link(dve.tensor_tensor(weights[:, 1], weights[:, 0], x2[:], ALU.mult))
            dve.wait_ge(made, 6)
            link(dve.tensor_copy(thr[:], thr_i[:]))
            link(dve.tensor_copy(tile_f[:], tile_i[:]))
            link(dve.tensor_copy(tok[:], tok_i[:]))
            link(dve.tensor_copy(lane[:], lane_i[:]))
            dve.wait_ge(counted, 2)
            link(dve.memset(offs[:, 0], 0.0))
            for t in range(NT):
                link(dve.tensor_tensor(offs[:, t + 1], offs[:, t], tot_ps[:, t * NE:(t + 1) * NE], ALU.add))
            link(dve.tensor_tensor(over[:], offs[:, NT].unsqueeze(2).broadcast_to([P, NE, NT]),
                                   thr[:].unsqueeze(1).broadcast_to([P, NE, NT]), ALU.is_gt))
            link(dve.tensor_reduce(n_tiles[:], over[:], AX, ALU.add))
            link(dve.tensor_scalar(n_tiles[:], n_tiles[:], 1.0, None, ALU.max))
            link(dve.tensor_tensor_scan(upto[:], ones[:, 0:NE], n_tiles[:], 0.0, ALU.mult, ALU.add))
            link(dve.tensor_tensor(first_tile[:], upto[:], n_tiles[:], ALU.subtract))
            link(dve.tensor_scalar(start[:], first_tile[:], float(P), None, ALU.mult))
            link(dve.tensor_tensor(base[:], rank_ps[:].rearrange("p (t e) -> p t e", t=NT), offs[:, 0:NT], ALU.add))
            link(dve.tensor_tensor(base[:], base[:], start[:].unsqueeze(1).broadcast_to([P, NT, NE]), ALU.add))
            for c in range(2):
                pick = hot[c][:].rearrange("p t g e -> p t (g e)")
                link(dve.tensor_tensor(both[:], base[:], pick, ALU.mult))
                link(dve.tensor_reduce(slot_f[:, c], both[:], AX, ALU.add))
            link(dve.tensor_copy(slots[:], slot_f[:]))
            flat = slots[:].rearrange("p c t -> p (c t)").bitcast(I32)
            for part, (number, op) in enumerate(((P - 1, ALU.bitwise_and), (P.bit_length() - 1, ALU.logical_shift_right))):
                link(dve.tensor_scalar(part_i[part][:], flat, number, None, op))
                link(dve.tensor_copy(part_f[part][:], part_i[part][:]))
            over_tiles = lambda v: v.unsqueeze(2).broadcast_to([P, PAIRS, MT])
            link(dve.tensor_tensor(hot_tile[:], over_tiles(part_f[1][:]), tile_f[:].unsqueeze(1).broadcast_to([P, PAIRS, MT]),
                                   ALU.is_equal))
            for c in range(2):
                half = slice(c * NT, (c + 1) * NT)
                dve.tensor_tensor(tok_tile[:, half], hot_tile[:, half], tok[:].unsqueeze(2).broadcast_to([P, NT, MT]),
                                  ALU.mult).then_inc(tok_tile_done, 1)
            for n in range(PARTS):
                some = slice(n * PAIRS // PARTS, (n + 1) * PAIRS // PARTS)
                shape = [P, PAIRS // PARTS, P]
                dve.tensor_tensor(hot_lane[:, some], part_f[0][:, some].unsqueeze(2).broadcast_to(shape),
                                  lane[:].unsqueeze(1).broadcast_to(shape), ALU.is_equal).then_inc(hot_lane_done, 1)
            link(dve.tensor_tensor(past[:], upto[:].unsqueeze(1).broadcast_to([P, MT, NE]),
                                   tile_f[:].unsqueeze(2).broadcast_to([P, MT, NE]), ALU.is_le))
            link(dve.tensor_reduce(exp_f[:], past[:], AX, ALU.add))
            link(dve.tensor_scalar(exp_f[:], exp_f[:], float(NE - 1), None, ALU.min))
            link(dve.tensor_copy(tile_expert[:], exp_f[:]))
            link(dve.tensor_tensor(past[:, :, 0:NE - 1], first_tile[:, 0:NE - 1].unsqueeze(1).broadcast_to([P, MT, NE - 1]),
                                   tile_f[:].unsqueeze(2).broadcast_to([P, MT, NE - 1]), ALU.is_equal))
            link(dve.tensor_reduce(splits[:], past[:, :, 0:NE - 1], AX, ALU.add))
            link(dve.tensor_copy(split_at[:], splits[:]))
            evens = tile_f[:].rearrange("p (n u) -> p n u", u=2)[:, :, 0]
            link(dve.tensor_tensor(live[:], evens, upto[:, NE - 1:NE].broadcast_to([P, MT // 2]), ALU.is_lt))
            link(dve.tensor_copy(pair_live[:], live[:]))
            link(dve.tensor_reduce(last_f[:], live[:], AX, ALU.add))
            link(dve.tensor_scalar(last_f[:], last_f[:], 2.0, -1.0, ALU.mult, ALU.add))
            link(dve.tensor_copy(last_tile[:], last_f[:]))
            link(dve.memset(lists[:, MT:], 0))
            for n, (raw, hi, lo) in enumerate(pieces):
                dve.wait_ge(hi_made, n + 1)
                dve.tensor_tensor(lo, raw, hi.bitcast(F32), ALU.subtract).then_inc(lo_made, 1)
            dve.wait_ge(listed, 1)
            link(dve.tensor_copy(lists[:, 0:MT], list_ps[:]))

        @block.tensor
        def _(pe):
            pe.wait_ge(both_done, 1)
            pe.wait_ge(made, 6)
            m = both[:].rearrange("p t e -> p (t e)")
            pe.matmul(rank_ps[:], tri[:], m, start=True, stop=True).then_inc(counted, 1)
            pe.matmul(tot_ps[:], ones[:], m, start=True, stop=True).then_inc(counted, 1)
            pe.wait_ge(tok_tile_done, 2)
            for n in range(PAIRS):
                pe.wait_ge(hot_lane_done, n * PARTS // PAIRS + 1)
                last = pe.matmul(list_ps[:], hot_lane[:, n, :], tok_tile[:, n, :], start=n == 0, stop=n == PAIRS - 1)
            last.then_inc(listed, 1)


def experts(nc, exp_w1, exp_w3, exp_w2, up_w, down_w, ident, lists, tile_expert, split_at, pair_live, last_tile,
            h1_dram, y_dram):
    with ExitStack() as ctx:
        sb = lambda n, s, d=F32: ctx.enter_context(nc.sbuf_tensor("e_" + n, s, d))
        ps = lambda n, s, d=F32: ctx.enter_context(nc.psum_tensor("e_" + n, s, d))
        sem = ctx.enter_context(semaphores(nc, "e_"))
        HALF = KD // 2
        UP_PARTS = 4
        UP_FIRST = 3
        DOWN_PARTS = KE
        up_raw, up_hi, up_lo = up_w
        down_raw, down_hi, down_lo = down_w
        ix = [sb(f"ix{u}", [P, 1], U32) for u in range(2)]
        xg = [sb(f"xg{u}", [P, D]) for u in range(2)]
        xt_hi = [sb(f"xt_hi{u}", [P, KD, P], F32R) for u in range(2)]
        xt_lo = [sb(f"xt_lo{u}", [P, KD, P], F32R) for u in range(2)]
        sg = sb("sg", [P, DE])
        hid = sb("hid", [P, DE])
        ht_hi = sb("ht_hi", [P, KE, P], F32R)
        ht_lo = sb("ht_lo", [P, KE, P], F32R)
        yt = [sb(f"yt{u}", [P, D]) for u in range(2)]
        t_ps = [ps(f"t_ps{c}", [P, HALF, P]) for c in range(2)]
        a_ps = ps("a_ps", [P, 2 * DE])
        h_ps = ps("h_ps", [P, KE, P])
        y_ps = [ps(f"y_ps{c}", [P, 512]) for c in range(2)]

        go = sem("go")
        ix_done = sem("index_ready")
        x_in = [sem(f"rows_gathered{u}") for u in range(2)]
        w_in = [sem(f"weights_loaded{b}") for b in range(2)]
        w_ready = sem("raw_weights_ready")
        up_hi_made = sem("up_hi_made")
        up_lo_made = sem("up_lo_made")
        down_hi_made = sem("down_hi_made")
        down_lo_made = sem("down_lo_made")
        t_done = [sem(f"x_transposed{c}") for c in range(2)]
        xh_done = [sem(f"xt_hi_done{c}") for c in range(2)]
        xl_done = [sem(f"xt_lo_done{c}") for c in range(2)]
        a_done = sem("a_done")
        sg_done = sem("silu_done")
        hid_done = sem("hid_done")
        h_done = sem("hid_transposed")
        hh_done = sem("ht_hi_done")
        hl_done = sem("ht_lo_done")
        y_done = [sem(f"y_done{c}") for c in range(2)]
        yt_done = [sem(f"yt_done{c}") for c in range(2)]
        y_stored = [sem(f"y_stored{u}") for u in range(2)]
        filled = sem("unused_rows_filled")
        block = ctx.enter_context(nc.Block())

        def buffer(w, e, rows):
            return w[:, bass.ds(e % 2, 1), rows, :].rearrange("p o k n -> p (o k) n")

        def expert_of(eng, j):
            return eng.value_load(tile_expert[0:1, bass.ds(j, 1)], min_val=0, max_val=NE - 1)

        def beside_first_tile(eng, j, split):
            flag = eng.value_load(split_at[0:1, bass.ds(j, 1)], min_val=0, max_val=1)
            with eng.If(flag > 0):
                split(eng.value_load(tile_expert[0:1, bass.ds(j, 1)], min_val=0, max_val=NE - 2) + 1)

        def run_tiles(eng, ahead, split_first, up, turn, down, turn_hid, split_rest, fill=None):
            def tile(j, u, is_first=False):
                ahead(j + 2, u)
                if split_first:
                    beside_first_tile(eng, j, split_first)
                up(j, u)
                turn(j + 1, 1 - u)
                if not is_first:
                    down(j - 1, 1 - u)
                turn_hid(j, u)
                if split_rest:
                    beside_first_tile(eng, j, split_rest)

            turn(0, 0)
            tile(0, 0, is_first=True)
            tile(1, 1)
            with eng.Fori(1, MT // 2) as n:
                flag = eng.value_load(pair_live[0:1, bass.ds(n, 1)], min_val=0, max_val=1)
                with eng.If(flag > 0):
                    for u in range(2):
                        tile(2 * n + u, u)
                    if fill:
                        eng.sem_inc(filled, 32)
                if fill:
                    with eng.Else():
                        fill(n)
            last = eng.value_load(last_tile[0:1, 0:1], min_val=1, max_val=MT - 1)
            down(last, 1)
            return last

        def skip(j, u):
            pass

        @block.sync
        def _(sp):
            for b in range(2):
                sp.sem_inc(w_in[b], 48)
            with sp.Fori(0, NE // 2 - 1) as n:
                for b in range(2):
                    sp.wait_ge(w_in[b], 48 * n + 48)
                    sp.sem_inc(w_ready, 1)
                    sp.wait_ge(up_lo_made, UP_PARTS * (2 * n + b + 1))
                    sp.nop(nofuse=True)
                    sp.wait_ge(down_lo_made, DOWN_PARTS * (2 * n + b + 1))
                    sp.nop(nofuse=True)
                    load_expert(sp, exp_w1, exp_w3, exp_w2, up_raw, down_raw, 2 * n + 2 + b, b, w_in[b])
            for b in range(2):
                sp.wait_ge(w_in[b], 48 * (NE // 2))
                sp.sem_inc(w_ready, 1)

        @block.gpsimd
        def _(pool):
            def ahead(j, u):
                pool.wait_ge(ix_done, j + 1)
                pool.nop(nofuse=True)
                pool.indirect_dma_start(xg[u][:], None, h1_dram, bass.IndirectOffsetOnAxis(ix[u][:, 0:1], 0))\
                    .then_inc(x_in[u], 16)

            ahead(0, 0)
            ahead(1, 1)
            last = run_tiles(pool, ahead, None, skip, skip, skip, skip, None)
            pool.wait_ge(x_in[1], 8 * (last - 1) + 32)

        @block.tensor
        def _(pe):
            def turn(j, u):
                pe.wait_ge(x_in[u], 8 * (j - u) + 16)
                for c in range(2):
                    pe.wait_ge(xl_done[c], j + 1)
                    for i in range(HALF):
                        k = c * HALF + i
                        last = pe.transpose(t_ps[c][:, i, :], xg[u][:, k * P:(k + 1) * P], ident[:])
                    last.then_inc(t_done[c], 1)

            def up(j, u):
                e = expert_of(pe, j)
                pe.wait_ge(up_lo_made, UP_PARTS * e + UP_PARTS)
                for k in range(KD):
                    if k % HALF == 0:
                        pe.wait_ge(xl_done[k // HALF], j + 2)
                    w = [buffer(part, e, slice(k, k + 1)).rearrange("p o n -> p (o n)") for part in (up_hi, up_lo)]
                    last = three_pass(pe, a_ps[:], (xt_hi[u][:, k, :], xt_lo[u][:, k, :]), w, k == 0, k == KD - 1)
                last.then_inc(a_done, 1)

            def turn_hid(j, u):
                pe.wait_ge(hid_done, j + 2)
                pe.wait_ge(hl_done, j + 1)
                for k in range(KE):
                    last = pe.transpose(h_ps[:, k, :], hid[:, k * P:(k + 1) * P], ident[:])
                last.then_inc(h_done, 1)

            def down(j, u):
                e = expert_of(pe, j)
                pe.wait_ge(down_lo_made, DOWN_PARTS * e + DOWN_PARTS)
                pe.wait_ge(hl_done, j + 2)
                for c in range(2):
                    pe.wait_ge(yt_done[c], j + 1)
                    for k in range(KE):
                        w = [buffer(part, e, slice(k, k + 1)).rearrange("p o n -> p (o n)")[:, c * 512:(c + 1) * 512]
                             for part in (down_hi, down_lo)]
                        last = three_pass(pe, y_ps[c][:], (ht_hi[:, k, :], ht_lo[:, k, :]), w, k == 0, k == KE - 1)
                    last.then_inc(y_done[c], 1)

            run_tiles(pe, skip, None, up, turn, down, turn_hid, None)

        @block.scalar
        def _(act):
            act.sem_inc(go, 1)
            act.sem_inc(up_hi_made, UP_PARTS)
            act.sem_inc(down_hi_made, DOWN_PARTS)
            for c in range(2):
                act.sem_inc(yt_done[c], 1)
            for u in range(2):
                act.sem_inc(y_stored[u], 16)

            def split_up(e, parts):
                for i in parts:
                    rows = slice(i * (KD // UP_PARTS), (i + 1) * (KD // UP_PARTS))
                    act.wait_ge(go, 1)
                    act.activation(buffer(up_hi, e, rows), buffer(up_raw, e, rows), ACT.Copy).then_inc(up_hi_made, 1)

            def split_first(e):
                act.wait_ge(w_ready, e + 1)
                split_up(e, range(UP_FIRST))

            def split_rest(e):
                split_up(e, range(UP_FIRST, UP_PARTS))
                for k in range(DOWN_PARTS):
                    act.wait_ge(go, 1)
                    act.activation(buffer(down_hi, e, slice(k, k + 1)), buffer(down_raw, e, slice(k, k + 1)), ACT.Copy)\
                       .then_inc(down_hi_made, 1)

            def ahead(j, u):
                act.wait_ge(a_done, j - 1)
                act.wait_ge(go, 1)

            def up(j, u):
                act.wait_ge(a_done, j + 2)
                act.wait_ge(hid_done, j + 1)
                act.activation(sg[:], a_ps[:, 0:DE], ACT.Silu).then_inc(sg_done, 1)

            def turn(j, u):
                for c in range(2):
                    act.wait_ge(t_done[c], j + 1)
                    act.activation(xt_hi[u][:, c * HALF:(c + 1) * HALF], t_ps[c][:], ACT.Copy).then_inc(xh_done[c], 1)

            def down(j, u):
                act.wait_ge(y_stored[u], 8 * (j - u) + 16)
                for c in range(2):
                    act.wait_ge(y_done[c], j + 1)
                    act.activation(yt[u][:, c * 512:(c + 1) * 512], y_ps[c][:], ACT.Copy).then_inc(yt_done[c], 1)
                act.wait_ge(yt_done[0], j + 2)
                act.wait_ge(yt_done[1], j + 2)
                act.dma_start(y_dram[bass.ds(j * P, P), :], yt[u][:]).then_inc(y_stored[u], 16)

            def turn_hid(j, u):
                act.wait_ge(h_done, j + 1)
                act.activation(ht_hi[:], h_ps[:], ACT.Copy).then_inc(hh_done, 1)

            def fill(n):
                for u in range(2):
                    act.dma_start(y_dram[bass.ds((2 * n + u) * P, P), :], yt[0][:]).then_inc(filled, 16)

            last = run_tiles(act, ahead, split_first, up, turn, down, turn_hid, split_rest, fill)
            stores = 8 * last + 24
            for u in range(2):
                act.wait_ge(y_stored[u], stores)
                act.nop(nofuse=True)
            act.wait_ge(filled, 16 * (MT - 2))

        @block.vector
        def _(dve):
            dve.sem_inc(up_lo_made, UP_PARTS)
            dve.sem_inc(down_lo_made, DOWN_PARTS)
            dve.sem_inc(a_done, 1)
            dve.sem_inc(hid_done, 1)
            dve.sem_inc(hl_done, 1)
            for c in range(2):
                dve.sem_inc(xl_done[c], 1)

            def index(j, u):
                dve.nop(nofuse=True)
                dve.tensor_copy(ix[u][:], lists[:, bass.ds(j, 1)]).then_inc(ix_done, 1)

            def ahead(j, u):
                dve.wait_ge(t_done[1], j - 1)
                index(j, u)

            def split_up(e, parts):
                for i in parts:
                    rows = slice(i * (KD // UP_PARTS), (i + 1) * (KD // UP_PARTS))
                    dve.wait_ge(up_hi_made, UP_PARTS * e + i + 1)
                    dve.nop(nofuse=True)
                    dve.tensor_tensor(buffer(up_lo, e, rows), buffer(up_raw, e, rows), buffer(up_hi, e, rows).bitcast(F32),
                                      ALU.subtract).then_inc(up_lo_made, 1)

            def split_first(e):
                split_up(e, range(UP_FIRST))

            def split_rest(e):
                split_up(e, range(UP_FIRST, UP_PARTS))
                for k in range(DOWN_PARTS):
                    row_k = slice(k, k + 1)
                    dve.wait_ge(down_hi_made, DOWN_PARTS * e + k + 1)
                    dve.nop(nofuse=True)
                    dve.tensor_tensor(buffer(down_lo, e, row_k), buffer(down_raw, e, row_k),
                                      buffer(down_hi, e, row_k).bitcast(F32), ALU.subtract).then_inc(down_lo_made, 1)

            def up(j, u):
                dve.wait_ge(sg_done, j + 1)
                dve.tensor_tensor(hid[:], sg[:], a_ps[:, DE:2 * DE], ALU.mult).then_inc(hid_done, 1)

            def turn(j, u):
                for c in range(2):
                    part = slice(c * HALF, (c + 1) * HALF)
                    dve.wait_ge(xh_done[c], j + 1)
                    dve.tensor_tensor(xt_lo[u][:, part], t_ps[c][:], xt_hi[u][:, part].bitcast(F32), ALU.subtract)\
                       .then_inc(xl_done[c], 1)

            def turn_hid(j, u):
                dve.wait_ge(hh_done, j + 1)
                dve.tensor_tensor(ht_lo[:], h_ps[:], ht_hi[:].bitcast(F32), ALU.subtract).then_inc(hl_done, 1)

            index(0, 0)
            index(1, 1)
            run_tiles(dve, ahead, split_first, up, turn, skip, turn_hid, split_rest)


def combine(nc, ln_g, ln_b, slots, weights, h1_dram, y_dram, out):
    with ExitStack() as ctx:
        sb = lambda n, s, d=F32: ctx.enter_context(nc.sbuf_tensor("c_" + n, s, d))
        sem = ctx.enter_context(semaphores(nc, "c_"))
        GT = 2
        NB = 4
        NG = NT // GT
        g_b = sb("g_b", [P, D])
        b_b = sb("b_b", [P, D])
        ix = [sb(f"ix{u}", [P, 2, GT], U32) for u in range(NB)]
        h1 = [sb(f"h1{u}", [P, GT, D]) for u in range(NB)]
        y1 = [sb(f"y1{u}", [P, GT, D]) for u in range(NB)]
        y2 = [sb(f"y2{u}", [P, GT, D]) for u in range(NB)]
        wt = [sb(f"wt{u}", [P, 2, GT]) for u in range(NB)]
        stats = sb("stats", [P, GT, 12])
        mv = sb("mv", [P, GT, 2])
        var = sb("var", [P, GT])
        tmp = sb("tmp", [P, GT])
        rstd = [sb(f"rstd{u}", [P, GT]) for u in range(NB)]
        shift = [sb(f"shift{u}", [P, GT]) for u in range(NB)]
        rows_in = sem("rows_loaded")
        ix_done = sem("index_ready")
        h_in = [sem(f"h1_loaded{u}") for u in range(NB)]
        y_in = [sem(f"y_gathered{u}") for u in range(NB)]
        dve_link = sem("dve_link")
        ah_done = sem("alpha_h_done")
        ln_done = sem("stats_done")
        xn_done = sem("normalised")
        hg_done = sem("gain_done")
        o_done = sem("out_done")
        stored = [sem(f"stored{u}") for u in range(NB)]
        block = ctx.enter_context(nc.Block())

        @block.sync
        def _(sp):
            for u in range(NB):
                sp.sem_inc(stored[u], 16 * GT)
            for g in range(NG):
                n, u = divmod(g, NB)
                sp.wait_ge(stored[u], 16 * GT * n + 16 * GT)
                if g:
                    sp.wait_ge(y_in[(g - 1) % NB], 32 * GT * ((g - 1) // NB + 1))
                for i in range(GT):
                    t = g * GT + i
                    sp.dma_start(h1[u][:, i], h1_dram[t * P:(t + 1) * P, :]).then_inc(h_in[u], 16)
                if g == 0:
                    sp.dma_start(g_b[:], row(ln_g, D)).then_inc(rows_in, 16)
                    sp.dma_start(b_b[:], row(ln_b, D)).then_inc(rows_in, 16)
            for u in range(NB):
                sp.wait_ge(stored[u], 16 * GT * (1 + NG // NB))

        def run_groups(eng, load, norm, finish):
            for u in range(NB - 1):
                load(u, u)
            norm(0, 0)
            with eng.Fori(0, NG // NB - 1) as n:
                for u in range(NB):
                    g = NB * n + u
                    load(g + NB - 1, (u + NB - 1) % NB)
                    norm(g + 1, (u + 1) % NB)
                    finish(g, u)
            for u in range(NB):
                g = NG - NB + u
                if u == 0:
                    load(NG - 1, NB - 1)
                if u < NB - 1:
                    norm(g + 1, u + 1)
                finish(g, u)

        @block.gpsimd
        def _(pool):
            def load(g, u):
                pool.wait_ge(ln_done, g + 1)
                pool.wait_ge(ix_done, g + 1)
                pool.nop(nofuse=True)
                for i in range(GT):
                    for c, y in enumerate((y1, y2)):
                        pool.indirect_dma_start(y[u][:, i], None, y_dram, bass.IndirectOffsetOnAxis(ix[u][:, c, i:i + 1], 0))\
                            .then_inc(y_in[u], 16)

            def finish(g, u):
                pool.wait_ge(rows_in, 32)
                for i in range(GT):
                    pool.wait_ge(hg_done, GT * g + i + 1)
                    pool.tensor_tensor(h1[u][:, i], h1[u][:, i], b_b[:], ALU.add).then_inc(o_done, 1)

            run_groups(pool, load, lambda g, u: None, finish)

        @block.vector
        def _(dve):
            dve.sem_inc(ln_done, NB)
            links = 5 + RSQRT_LINKS_WIDE + 1

            def load(g, u):
                dve.wait_ge(ln_done, g + 1)
                dve.nop(nofuse=True)
                dve.tensor_copy(wt[u][:], weights[:, :, bass.ds(g * GT, GT)])
                dve.tensor_copy(ix[u][:], slots[:, :, bass.ds(g * GT, GT)]).then_inc(ix_done, 1)

            def norm(g, u):
                link = Chain(dve, dve_link, links * g)
                dve.wait_ge(ah_done, GT * g + GT)
                dve.wait_ge(ix_done, g + 1)
                dve.wait_ge(y_in[u], (32 * GT // NB) * (g - u) + 32 * GT)
                for c, y in enumerate((y1, y2)):
                    for i in range(GT):
                        last = dve.scalar_tensor_tensor(h1[u][:, i], y[u][:, i], wt[u][:, c, i:i + 1], h1[u][:, i],
                                                        ALU.mult, ALU.add)
                    link(last)
                for i in range(GT):
                    for half in range(2):
                        last = dve.bn_stats(stats[:, i, 6 * half:6 * half + 6], h1[u][:, i, 512 * half:512 * half + 512])
                link(last)
                dve.nop(nofuse=True)
                for i in range(GT):
                    last = dve.bn_aggr(mv[:, i], stats[:, i])
                link(last)
                link(dve.tensor_scalar(var[:], mv[:, :, 1], LN_EPS, None, ALU.add))
                rsqrt(dve, link, var[:], rstd[u][:], tmp[:])
                link(dve.tensor_tensor(tmp[:], mv[:, :, 0], rstd[u][:], ALU.mult))
                assert link.n == links
                dve.tensor_scalar(shift[u][:], tmp[:], -1.0, None, ALU.mult).then_inc(ln_done, 1)

            def finish(g, u):
                dve.wait_ge(rows_in, 32)
                for i in range(GT):
                    dve.wait_ge(xn_done, GT * g + i + 1)
                    dve.tensor_tensor(h1[u][:, i], h1[u][:, i], g_b[:], ALU.mult).then_inc(hg_done, 1)

            run_groups(dve, load, norm, finish)

        @block.scalar
        def _(act):
            def load(g, u):
                act.wait_ge(h_in[u], (16 * GT // NB) * (g - u) + 16 * GT)
                for i in range(GT):
                    act.activation(h1[u][:, i], h1[u][:, i], ACT.Copy, scale=ALPHA).then_inc(ah_done, 1)

            def norm(g, u):
                act.wait_ge(ln_done, g + NB + 1)
                for i in range(GT):
                    act.activation(h1[u][:, i], h1[u][:, i], ACT.Identity, bias=shift[u][:, i:i + 1],
                                   scale=rstd[u][:, i:i + 1]).then_inc(xn_done, 1)

            def finish(g, u):
                for i in range(GT):
                    act.wait_ge(o_done, GT * g + i + 1)
                    act.dma_start(out[bass.ds((g * GT + i) * P, P), :], h1[u][:, i]).then_inc(stored[u], 16)

            run_groups(act, load, norm, finish)


_NAMES = ["ln_in_g", "ln_in_b", "w_in", "conv_w", "conv_b", "lru_wa", "lru_ba", "lru_wx", "lru_bx", "lru_lambda",
          "q_norm_g", "k_norm_g", "attn_out_g", "lru_out_g", "w_out", "ln1_g", "ln1_b", "router_wg", "router_bg",
          "router_we", "router_be", "exp_w1", "exp_w3", "exp_w2", "ln2_g", "ln2_b"]


def rope_table():
    import numpy as np

    grid_w, theta, half = 64, 10000.0, HD // 4
    inv_freq = (theta ** (-np.arange(half, dtype=np.float32) / half)).astype(np.float32)
    pos = np.arange(SEQ)
    tab = np.zeros((P, TPS, 2, 2, 2, half), np.float32)
    for sec, where in enumerate((pos // grid_w, pos % grid_w)):
        ang = where.astype(np.float32)[:, None] * inv_freq
        cos = np.cos(ang).reshape(TPS, P, half).transpose(1, 0, 2)
        sin = np.sin(ang).reshape(TPS, P, half).transpose(1, 0, 2)
        for f in range(2):
            tab[:, :, 0, sec, f] = cos
            tab[:, :, 1, sec, f] = sin if f else -sin
    return tab.reshape(P, TPS * 2 * HD)


def kernel(**inputs):
    import numpy as np
    import concourse.bacc as bacc
    from concourse.bass_utils import run_bass_kernel_spmd

    nc = bacc.Bacc("TRN2", target_bir_lowering=False, num_devices=1)
    arrays = {"in_x": np.concatenate([inputs["x_prompt"][0], inputs["x_sample"][0]])}
    for name in _NAMES:
        arrays[f"in_{name}"] = np.ascontiguousarray(inputs[name])
    arrays["in_rope"] = rope_table()
    args = [nc.dram_tensor(n, a.shape, mybir.dt.from_np(a.dtype), kind="ExternalInput").ap() for n, a in arrays.items()]
    args.append(nc.dram_tensor("out", (T, D), F32, kind="ExternalOutput").ap())
    build(nc, *args)
    got = run_bass_kernel_spmd(nc, [arrays], core_ids=[0]).results[0]["out"]
    return got[None, 0:SEQ], got[None, SEQ:T]
```
